# Optimizing a Trainium2 kernel written in Bass

```python
import math, functools
import jax, jax.numpy as jnp
from jax import lax
import numpy as np

D_MODEL = 1024
BATCH = 1
SEQ = 256
DEPTH = 2

CONV_CH = 512
N_HEADS = 8
HEAD_DIM = 64
ATTN_CH = N_HEADS * HEAD_DIM
D_MIX = CONV_CH + ATTN_CH
D_IN = 2 * CONV_CH + 3 * ATTN_CH
CONV_K = 31
GRID_W = 64
WIN_R = 8
WIN_C = 16
Q_CB = 16
N_CB = GRID_W // Q_CB
BAND_C = Q_CB + WIN_C
D_FF = 2816
N_EXPERTS = 8
TOP_K = 2
D_FF_EXPERT = 3584
MOE_BLK = 128
N_DENSE = (DEPTH + 1) // 2
N_MOE = DEPTH // 2
D_PLE = 256
LN_EPS = 1e-5
DEEPNORM_ALPHA = (2.0 * DEPTH) ** 0.25
DEEPNORM_BETA = (8.0 * DEPTH) ** -0.25


def layer_norm(x, g, b):
    xf = x.astype(jnp.float32)
    mu = jnp.mean(xf, axis=-1, keepdims=True)
    xc = xf - mu
    var = jnp.mean(xc * xc, axis=-1, keepdims=True)
    y = xc * lax.rsqrt(var + LN_EPS)
    return (y * g.astype(jnp.float32) + b.astype(jnp.float32)).astype(x.dtype)

def conformer_conv(a, g, w, b, ln_g, ln_b):
    u = a * jax.nn.sigmoid(g)
    c = u.shape[-1]
    pad = CONV_K // 2
    y = lax.conv_general_dilated(
        u, w[:, None, :], window_strides=(1,), padding=[(pad, pad)],
        dimension_numbers=("NWC", "WIO", "NWC"), feature_group_count=c)
    y = layer_norm(y + b, ln_g, ln_b)
    return jax.nn.silu(y)

def neighbourhood_attention(q, k, v, rpb):
    B, T, H, Dh = q.shape
    rows = T // GRID_W
    kr = min(WIN_R, rows)
    scale = Dh ** -0.5
    band0 = np.clip(np.arange(N_CB) * Q_CB - WIN_C // 2, 0, GRID_W - BAND_C)
    key_col = band0[:, None] + np.arange(BAND_C)
    q_col = np.arange(GRID_W).reshape(N_CB, Q_CB)
    win0 = np.clip(q_col - WIN_C // 2, 0, GRID_W - WIN_C)
    col_mask = ((key_col[:, None, :] >= win0[:, :, None]) &
                (key_col[:, None, :] < win0[:, :, None] + WIN_C))
    dc_idx = np.clip(key_col[:, None, :] - q_col[:, :, None] + WIN_C - 1, 0, 2 * WIN_C - 2)
    rpb_c = rpb[:, :, dc_idx]
    kg = k.reshape(B, rows, GRID_W, H, Dh)
    vg = v.reshape(B, rows, GRID_W, H, Dh)
    qr = jnp.moveaxis(q.reshape(B, rows, N_CB, Q_CB, H, Dh), 1, 0)

    def row_fn(args):
        r, q_row = args
        r0 = jnp.clip(r - kr // 2, 0, rows - kr)
        k_band = lax.dynamic_slice_in_dim(kg, r0, kr, axis=1)[:, :, key_col]
        v_band = lax.dynamic_slice_in_dim(vg, r0, kr, axis=1)[:, :, key_col]
        s = jnp.einsum("bjqhd,bijkhd->bhjqik", q_row, k_band).astype(jnp.float32) * scale
        dr_idx = r0 + jnp.arange(kr) - r + WIN_R - 1
        bias = jnp.transpose(jnp.take(rpb_c, dr_idx, axis=1), (0, 2, 3, 1, 4))
        s = jnp.where(col_mask[:, :, None, :], s + bias.astype(jnp.float32), -jnp.inf)
        w = jax.nn.softmax(s.reshape(B, H, N_CB, Q_CB, kr * BAND_C), axis=-1)
        w = w.reshape(s.shape).astype(v.dtype)
        return jnp.einsum("bhjqik,bijkhd->bjqhd", w, v_band)

    out = lax.map(row_fn, (jnp.arange(rows), qr))
    return jnp.moveaxis(out, 0, 1).reshape(B, T, H * Dh)

def swiglu(x, w1, w3, w2):
    return (jax.nn.silu(x @ w1) * (x @ w3)) @ w2

def moe_swiglu(x, w_router, w1, w3, w2):
    B, T, D = x.shape
    xf = x.reshape(-1, D)
    n = xf.shape[0]
    logits = (xf @ w_router).astype(jnp.float32)
    top_vals, top_idx = lax.top_k(logits, TOP_K)
    gates = jax.nn.softmax(top_vals, axis=-1)
    n_assign = n * TOP_K
    e_flat = top_idx.reshape(-1)
    tok_flat = jnp.repeat(jnp.arange(n, dtype=jnp.int32), TOP_K)
    g_flat = gates.reshape(-1)
    order = jnp.argsort(e_flat)
    e_sorted = e_flat[order]
    tok_sorted = tok_flat[order]
    g_sorted = g_flat[order]
    counts = jnp.bincount(e_flat, length=N_EXPERTS)
    starts = jnp.cumsum(counts) - counts
    padded = (counts + MOE_BLK - 1) // MOE_BLK * MOE_BLK
    pends = jnp.cumsum(padded)
    pstarts = pends - padded
    dest = pstarts[e_sorted] + (jnp.arange(n_assign) - starts[e_sorted])
    n_blocks = -(-n_assign // MOE_BLK) + N_EXPERTS
    n_slots = n_blocks * MOE_BLK
    tok_buf = jnp.zeros((n_slots,), jnp.int32).at[dest].set(tok_sorted)
    gate_buf = jnp.zeros((n_slots,), jnp.float32).at[dest].set(g_sorted)
    block_e = jnp.minimum(
        jnp.searchsorted(pends, jnp.arange(n_blocks) * MOE_BLK, side="right"), N_EXPERTS - 1)

    def block_fn(args):
        tok, e = args
        xb = xf[tok]
        return (jax.nn.silu(xb @ w1[e]) * (xb @ w3[e])) @ w2[e]

    y = lax.map(block_fn, (tok_buf.reshape(n_blocks, MOE_BLK), block_e)).reshape(n_slots, D)
    y = y * gate_buf[:, None].astype(y.dtype)
    out = jax.ops.segment_sum(y, tok_buf, num_segments=n)
    return out.reshape(B, T, D)

def first_inputs(seed: int = 0) -> dict:
    key = jax.random.key(seed)
    ks = jax.random.split(key, 32)
    f32 = jnp.float32
    nrm = lambda k, shape, s: jax.random.normal(k, shape, f32) * s
    gain = lambda k, shape: 1.0 + 0.02 * jax.random.normal(k, shape, f32)
    return {
        "x": jax.random.normal(ks[0], (BATCH, SEQ, D_MODEL), f32),
        "p": jax.random.normal(ks[1], (DEPTH, BATCH, SEQ, D_PLE), f32),
        "ln_in_g": gain(ks[2], (D_MODEL,)),
        "ln_in_b": nrm(ks[3], (D_MODEL,), 0.02),
        "w_in": nrm(ks[4], (DEPTH, D_MODEL, D_IN), D_MODEL ** -0.5),
        "b_in": nrm(ks[5], (DEPTH, D_IN), 0.02),
        "conv_w": nrm(ks[6], (DEPTH, CONV_K, CONV_CH), CONV_K ** -0.5),
        "conv_b": nrm(ks[7], (DEPTH, CONV_CH), 0.02),
        "conv_ln_g": gain(ks[8], (DEPTH, CONV_CH)),
        "conv_ln_b": nrm(ks[9], (DEPTH, CONV_CH), 0.02),
        "rpb": nrm(ks[10], (DEPTH, N_HEADS, 2 * WIN_R - 1, 2 * WIN_C - 1), 0.02),
        "w_out": nrm(ks[11], (DEPTH, D_MIX, D_MODEL), D_MIX ** -0.5 * DEEPNORM_BETA),
        "b_out": nrm(ks[12], (DEPTH, D_MODEL), 0.02),
        "ln1_g": gain(ks[13], (DEPTH, D_MODEL)),
        "ln1_b": nrm(ks[14], (DEPTH, D_MODEL), 0.02),
        "ffn_w1": nrm(ks[15], (N_DENSE, D_MODEL, D_FF), D_MODEL ** -0.5),
        "ffn_w3": nrm(ks[16], (N_DENSE, D_MODEL, D_FF), D_MODEL ** -0.5),
        "ffn_w2": nrm(ks[17], (N_DENSE, D_FF, D_MODEL), D_FF ** -0.5 * DEEPNORM_BETA),
        "w_router": nrm(ks[18], (N_MOE, D_MODEL, N_EXPERTS), D_MODEL ** -0.5),
        "moe_w1": nrm(ks[19], (N_MOE, N_EXPERTS, D_MODEL, D_FF_EXPERT), D_MODEL ** -0.5),
        "moe_w3": nrm(ks[20], (N_MOE, N_EXPERTS, D_MODEL, D_FF_EXPERT), D_MODEL ** -0.5),
        "moe_w2": nrm(ks[21], (N_MOE, N_EXPERTS, D_FF_EXPERT, D_MODEL), D_FF_EXPERT ** -0.5 * DEEPNORM_BETA),
        "ple_w": nrm(ks[22], (DEPTH, D_PLE, D_MODEL), D_PLE ** -0.5 * DEEPNORM_BETA),
        "ple_gate_w": nrm(ks[23], (DEPTH, D_MODEL, D_MODEL), D_MODEL ** -0.5),
        "ple_gate_b": nrm(ks[24], (DEPTH, D_MODEL), 0.02),
        "ln2_g": gain(ks[25], (DEPTH, D_MODEL)),
        "ln2_b": nrm(ks[26], (DEPTH, D_MODEL), 0.02),
    }

def first_block(x, p, ln_in_g, ln_in_b, w_in, b_in, conv_w, conv_b, conv_ln_g, conv_ln_b,
              rpb, w_out, b_out, ln1_g, ln1_b, ffn_w1, ffn_w3, ffn_w2, w_router,
              moe_w1, moe_w3, moe_w2, ple_w, ple_gate_w, ple_gate_b, ln2_g, ln2_b):
    B, T, _ = x.shape
    h = layer_norm(x, ln_in_g, ln_in_b)
    for i in range(DEPTH):
        proj = h @ w_in[i] + b_in[i]
        a = proj[..., :CONV_CH]
        g = proj[..., CONV_CH:2 * CONV_CH]
        qkv = proj[..., 2 * CONV_CH:].reshape(B, T, 3, N_HEADS, HEAD_DIM)
        conv_out = conformer_conv(a, g, conv_w[i], conv_b[i], conv_ln_g[i], conv_ln_b[i])
        attn_out = neighbourhood_attention(qkv[:, :, 0], qkv[:, :, 1], qkv[:, :, 2], rpb[i])
        mix = jnp.concatenate([conv_out, attn_out], axis=-1) @ w_out[i] + b_out[i]
        h = layer_norm(DEEPNORM_ALPHA * h + mix, ln1_g[i], ln1_b[i])
        j = i // 2
        if i % 2 == 0:
            f = swiglu(h, ffn_w1[j], ffn_w3[j], ffn_w2[j])
        else:
            f = moe_swiglu(h, w_router[j], moe_w1[j], moe_w3[j], moe_w2[j])
        e = jax.nn.sigmoid(h @ ple_gate_w[i] + ple_gate_b[i]) * (p[i] @ ple_w[i])
        h = layer_norm(DEEPNORM_ALPHA * h + f + e, ln2_g[i], ln2_b[i])
    return h


CTX_LEN = 256
ATT_HEADS = 8
ATT_KV_HEADS = 2
ATT_HEAD_DIM = 64
ATT_WIDTH = ATT_HEADS * ATT_HEAD_DIM
KV_WIDTH = ATT_KV_HEADS * ATT_HEAD_DIM
WINDOW = 128
BLOCK = 128
ROPE_BASE = 10000.0
M_HEADS = 4
M_HEAD_DIM = 128
M_WIDTH = M_HEADS * M_HEAD_DIM
CONV_K_2 = 5
CHUNK = 128
N_DIR = 2
MIX_WIDTH = ATT_WIDTH + M_WIDTH
EPS = 1e-6
SPLIT_SIZES = (ATT_WIDTH, KV_WIDTH, KV_WIDTH, ATT_WIDTH, M_WIDTH, M_WIDTH, M_WIDTH, M_WIDTH, M_WIDTH, N_DIR * M_HEADS, N_DIR * M_HEADS)
IN_COLS = 2 * ATT_WIDTH + 2 * KV_WIDTH + 5 * M_WIDTH + 2 * N_DIR * M_HEADS


def rmsnorm(x, g):
    xf = x.astype(jnp.float32)
    y = xf * lax.rsqrt(jnp.mean(xf * xf, axis=-1, keepdims=True) + EPS)
    return (y * g.astype(jnp.float32)).astype(x.dtype)

def project(xn, w_in):
    idx = np.cumsum(SPLIT_SIZES)[:-1].tolist()
    return jnp.split(xn @ w_in, idx, axis=-1)

def axial_rope_tables(T):
    rows = T // GRID_W
    row = jnp.repeat(jnp.arange(rows), GRID_W).astype(jnp.float32)
    col = jnp.tile(jnp.arange(GRID_W), rows).astype(jnp.float32)
    half = ATT_HEAD_DIM // 2
    inv = ROPE_BASE ** (-jnp.arange(0, half, 2, dtype=jnp.float32) / half)
    ang_r = row[:, None] * inv
    ang_c = col[:, None] * inv
    return (jnp.cos(ang_r)[:, None, :], jnp.sin(ang_r)[:, None, :],
            jnp.cos(ang_c)[:, None, :], jnp.sin(ang_c)[:, None, :])

def rope_2d(u, tables):
    cos_r, sin_r, cos_c, sin_c = [t.astype(u.dtype) for t in tables]

    def rot(a, cos, sin):
        a1, a2 = jnp.split(a, 2, axis=-1)
        return jnp.concatenate([a1 * cos - a2 * sin, a2 * cos + a1 * sin], axis=-1)

    ur, uc = jnp.split(u, 2, axis=-1)
    return jnp.concatenate([rot(ur, cos_r, sin_r), rot(uc, cos_c, sin_c)], axis=-1)

def window_ctx_attention(q, k, v, kc, vc, sink):
    B, T, H, dh = q.shape
    G = H // ATT_KV_HEADS
    NB = T // BLOCK
    scale = dh ** -0.5
    qb = q.reshape(B, NB, BLOCK, ATT_KV_HEADS, G, dh)
    pad = ((0, 0), (BLOCK, BLOCK), (0, 0), (0, 0))
    kp = jnp.pad(k, pad).reshape(B, NB + 2, BLOCK, ATT_KV_HEADS, dh)
    vp = jnp.pad(v, pad).reshape(B, NB + 2, BLOCK, ATT_KV_HEADS, dh)
    kw = jnp.concatenate([kp[:, :-2], kp[:, 1:-1], kp[:, 2:]], axis=2)
    vw = jnp.concatenate([vp[:, :-2], vp[:, 1:-1], vp[:, 2:]], axis=2)
    s_win = jnp.einsum('bnqhgd,bnkhd->bhgnqk', qb, kw).astype(jnp.float32) * scale
    qpos = jnp.arange(NB)[:, None, None] * BLOCK + jnp.arange(BLOCK)[None, :, None]
    kpos = (jnp.arange(NB)[:, None, None] - 1) * BLOCK + jnp.arange(3 * BLOCK)[None, None, :]
    valid = (jnp.abs(qpos - kpos) <= WINDOW) & (kpos >= 0) & (kpos < T)
    s_win = jnp.where(valid, s_win, -jnp.inf)
    s_ctx = jnp.einsum('bnqhgd,bchd->bhgnqc', qb, kc).astype(jnp.float32) * scale
    s_sink = jnp.broadcast_to(sink.astype(jnp.float32).reshape(1, ATT_KV_HEADS, G, 1, 1, 1),
                              s_win.shape[:-1] + (1,))
    p = jax.nn.softmax(jnp.concatenate([s_win, s_ctx, s_sink], axis=-1), axis=-1)
    Lw = 3 * BLOCK
    Lc = kc.shape[1]
    p_win = p[..., :Lw].astype(v.dtype)
    p_ctx = p[..., Lw:Lw + Lc].astype(v.dtype)
    out = (jnp.einsum('bhgnqk,bnkhd->bnqhgd', p_win, vw)
           + jnp.einsum('bhgnqc,bchd->bnqhgd', p_ctx, vc))
    return out.reshape(B, T, H * dh)

def ctx_attention(qc, kc, vc, sink):
    B, Lc, H, dh = qc.shape
    G = H // ATT_KV_HEADS
    qg = qc.reshape(B, Lc, ATT_KV_HEADS, G, dh)
    s = jnp.einsum('bqhgd,bkhd->bhgqk', qg, kc).astype(jnp.float32) * dh ** -0.5
    s_sink = jnp.broadcast_to(sink.astype(jnp.float32).reshape(1, ATT_KV_HEADS, G, 1, 1),
                              s.shape[:-1] + (1,))
    p = jax.nn.softmax(jnp.concatenate([s, s_sink], axis=-1), axis=-1)
    out = jnp.einsum('bhgqk,bkhd->bqhgd', p[..., :Lc].astype(vc.dtype), vc)
    return out.reshape(B, Lc, H * dh)

def dwconv(u, w, b):
    C = u.shape[-1]
    y = lax.conv_general_dilated(u, w[:, None, :].astype(u.dtype), window_strides=(1,),
                                 padding=[(CONV_K_2 // 2, CONV_K_2 // 2)],
                                 dimension_numbers=('NWC', 'WIO', 'NWC'), feature_group_count=C)
    return y + b.astype(u.dtype)

def mlstm_init_state(B):
    N = N_DIR * B * M_HEADS
    return (jnp.zeros((N, M_HEAD_DIM, M_HEAD_DIM), jnp.float32),
            jnp.zeros((N, M_HEAD_DIM), jnp.float32),
            jnp.full((N,), -jnp.inf, jnp.float32))

def mlstm_chunkwise(q, k, v, i_pre, f_pre, state):
    N, T, dh = q.shape
    NC = T // CHUNK
    f32 = jnp.float32

    def chunks(u):
        return u.astype(f32).reshape((N, NC, CHUNK) + u.shape[2:]).swapaxes(0, 1)

    qc = chunks(q)
    kc = chunks(k) * dh ** -0.5
    vc = chunks(v)
    lf = chunks(jax.nn.log_sigmoid(f_pre.astype(f32)))
    ic = chunks(i_pre)
    lower = jnp.tril(jnp.ones((CHUNK, CHUNK), bool))

    def step(carry, inp):
        C, n, m = carry
        qq, kk, vv, lfc, ii = inp
        b = jnp.cumsum(lfc, axis=-1)
        dmat = jnp.where(lower, b[:, :, None] - b[:, None, :] + ii[:, None, :], -jnp.inf)
        inter = b + m[:, None]
        m_t = jnp.maximum(inter, jnp.max(dmat, axis=-1))
        w_inter = jnp.exp(inter - m_t)
        qk = jnp.einsum('ntd,nsd->nts', qq, kk) * jnp.exp(dmat - m_t[:, :, None])
        num = (w_inter[..., None] * jnp.einsum('nvd,ntd->ntv', C, qq)
               + jnp.einsum('nts,nsv->ntv', qk, vv))
        den = w_inter * jnp.einsum('nd,ntd->nt', n, qq) + qk.sum(-1)
        h = num / jnp.maximum(jnp.abs(den), jnp.exp(-m_t))[..., None]
        bL = b[:, -1]
        g = bL[:, None] - b + ii
        m_new = jnp.maximum(bL + m, jnp.max(g, axis=-1))
        a = jnp.exp(bL + m - m_new)
        w = jnp.exp(g - m_new[:, None])
        C_new = a[:, None, None] * C + jnp.einsum('ns,nsv,nsd->nvd', w, vv, kk)
        n_new = a[:, None] * n + jnp.einsum('ns,nsd->nd', w, kk)
        return (C_new, n_new, m_new), h

    state, h = lax.scan(step, state, (qc, kc, vc, lf, ic))
    h = h.swapaxes(0, 1).reshape(N, T, dh)
    return h.astype(q.dtype), state

def mlstm_bidir(q, k, v, i_pre, f_pre, state):
    B, T, _ = q.shape

    def heads(u):
        u = u.reshape(B, T, M_HEADS, M_HEAD_DIM).transpose(0, 2, 1, 3)
        return jnp.stack([u, jnp.flip(u, axis=2)]).reshape(N_DIR * B * M_HEADS, T, M_HEAD_DIM)

    def gates(gt):
        gt = gt.reshape(B, T, N_DIR, M_HEADS).transpose(2, 0, 3, 1)
        return jnp.stack([gt[0], jnp.flip(gt[1], axis=-1)]).reshape(N_DIR * B * M_HEADS, T)

    h, state = mlstm_chunkwise(heads(q), heads(k), heads(v), gates(i_pre), gates(f_pre), state)
    h = h.reshape(N_DIR, B, M_HEADS, T, M_HEAD_DIM)
    h = h[0] + jnp.flip(h[1], axis=2)
    return h.transpose(0, 2, 1, 3).reshape(B, T, M_WIDTH), state

def mlstm_post(h, o_pre, z, head_g):
    B, T, _ = h.shape
    h = jax.nn.sigmoid(o_pre) * h
    hh = rmsnorm(h.reshape(B, T, M_HEADS, M_HEAD_DIM), head_g.reshape(M_HEADS, M_HEAD_DIM))
    return hh.reshape(B, T, M_WIDTH) * jax.nn.silu(z)

def mlstm_qk(mq, mk, conv_w, conv_b):
    qk = jax.nn.silu(dwconv(jnp.concatenate([mq, mk], axis=-1), conv_w, conv_b))
    return jnp.split(qk, 2, axis=-1)

def hybrid_layer(x, ctx, mod_x, mod_c, tables, norm_g, w_in, conv_w, conv_b, gate_b, sink,
                 head_g, w_out, last):
    shift_x, scale_x, gate_x = mod_x
    shift_c, scale_c, gate_c = mod_c
    B, T, _ = x.shape
    Lc = ctx.shape[1]
    b_i, b_f = jnp.split(gate_b, 2)
    xn = rmsnorm(x, norm_g) * (1 + scale_x) + shift_x
    cn = rmsnorm(ctx, norm_g) * (1 + scale_c) + shift_c
    aq, ak, av, az, mq, mk, mv, mo, mz, mi, mf = project(xn, w_in)
    caq, cak, cav, caz, cmq, cmk, cmv, cmo, cmz, cmi, cmf = project(cn, w_in)

    q = rope_2d(aq.reshape(B, T, ATT_HEADS, ATT_HEAD_DIM), tables)
    k = rope_2d(ak.reshape(B, T, ATT_KV_HEADS, ATT_HEAD_DIM), tables)
    v = av.reshape(B, T, ATT_KV_HEADS, ATT_HEAD_DIM)
    kc = cak.reshape(B, Lc, ATT_KV_HEADS, ATT_HEAD_DIM)
    vc = cav.reshape(B, Lc, ATT_KV_HEADS, ATT_HEAD_DIM)
    att_x = window_ctx_attention(q, k, v, kc, vc, sink) * jax.nn.silu(az)

    cq, ck = mlstm_qk(cmq, cmk, conv_w, conv_b)
    xq, xk = mlstm_qk(mq, mk, conv_w, conv_b)
    h_ctx, ctx_state = mlstm_bidir(cq, ck, cmv, cmi + b_i, cmf + b_f, mlstm_init_state(B))
    h_lat, _ = mlstm_bidir(xq, xk, mv, mi + b_i, mf + b_f, ctx_state)
    m_x = mlstm_post(h_lat, mo, mz, head_g)

    out_x = jnp.concatenate([att_x, m_x], axis=-1) @ w_out
    x = x + gate_x * out_x
    if not last:
        qc = caq.reshape(B, Lc, ATT_HEADS, ATT_HEAD_DIM)
        att_c = ctx_attention(qc, kc, vc, sink) * jax.nn.silu(caz)
        m_c = mlstm_post(h_ctx, cmo, cmz, head_g)
        out_c = jnp.concatenate([att_c, m_c], axis=-1) @ w_out
        ctx = ctx + gate_c * out_c
    return x, ctx

def second_inputs(seed: int = 0) -> dict:
    key = jax.random.key(seed)
    ks = jax.random.split(key, 16)
    f32 = jnp.float32
    nrm = lambda k, s: jax.random.normal(k, s, f32)
    f_bias = jnp.tile(jnp.linspace(3.0, 6.0, M_HEADS), N_DIR)
    gate_b = jnp.concatenate([0.1 * nrm(ks[8], (DEPTH, N_DIR * M_HEADS)),
                              f_bias[None, :] + 0.1 * nrm(ks[9], (DEPTH, N_DIR * M_HEADS))], axis=-1)
    return {
        "x": nrm(ks[0], (BATCH, SEQ, D_MODEL)),
        "c": nrm(ks[1], (BATCH, D_MODEL)),
        "ctx": nrm(ks[2], (BATCH, CTX_LEN, D_MODEL)),
        "c_ctx": nrm(ks[3], (D_MODEL,)),
        "w_ada": 0.5 * D_MODEL ** -0.5 * nrm(ks[4], (DEPTH, D_MODEL, 3 * D_MODEL)),
        "b_ada": 0.01 * nrm(ks[5], (DEPTH, 3 * D_MODEL)),
        "norm_g": 1.0 + 0.02 * nrm(ks[6], (DEPTH, D_MODEL)),
        "w_in": D_MODEL ** -0.5 * nrm(ks[7], (DEPTH, D_MODEL, IN_COLS)),
        "conv_w": CONV_K_2 ** -0.5 * nrm(ks[10], (DEPTH, CONV_K_2, 2 * M_WIDTH)),
        "conv_b": 0.01 * nrm(ks[11], (DEPTH, 2 * M_WIDTH)),
        "gate_b": gate_b,
        "sink": 0.5 * nrm(ks[12], (DEPTH, ATT_HEADS)),
        "head_g": 1.0 + 0.02 * nrm(ks[13], (DEPTH, M_WIDTH)),
        "w_out": MIX_WIDTH ** -0.5 * nrm(ks[14], (DEPTH, MIX_WIDTH, D_MODEL)),
        "final_g": 1.0 + 0.02 * nrm(ks[15], (D_MODEL,)),
    }

def second_block(x, c, ctx, c_ctx, w_ada, b_ada, norm_g, w_in, conv_w, conv_b, gate_b, sink,
              head_g, w_out, final_g):
    T = x.shape[1]
    tables = axial_rope_tables(T)
    sc = jax.nn.silu(c)
    scc = jax.nn.silu(c_ctx)
    for l in range(DEPTH):
        mod_x = jnp.split((sc @ w_ada[l] + b_ada[l])[:, None, :], 3, axis=-1)
        mod_c = jnp.split(scc @ w_ada[l] + b_ada[l], 3, axis=-1)
        x, ctx = hybrid_layer(x, ctx, mod_x, mod_c, tables, norm_g[l], w_in[l], conv_w[l],
                              conv_b[l], gate_b[l], sink[l], head_g[l], w_out[l],
                              last=(l == DEPTH - 1))
    return rmsnorm(x, final_g)


def setup_inputs(seed=0):
    out = dict(first_inputs(seed))
    for name, value in second_inputs(seed + 1).items():
        if name != "x":
            out[name + "_2"] = value
    return out


def reference(
    x, p, ln_in_g, ln_in_b, w_in, b_in, conv_w, conv_b, conv_ln_g, conv_ln_b, rpb, w_out, b_out,
    ln1_g, ln1_b, ffn_w1, ffn_w3, ffn_w2, w_router, moe_w1, moe_w3, moe_w2, ple_w, ple_gate_w,
    ple_gate_b, ln2_g, ln2_b, c_2, ctx_2, c_ctx_2, w_ada_2, b_ada_2, norm_g_2, w_in_2, conv_w_2,
    conv_b_2, gate_b_2, sink_2, head_g_2, w_out_2, final_g_2,
):
    x = first_block(
        x, p, ln_in_g, ln_in_b, w_in, b_in, conv_w, conv_b, conv_ln_g, conv_ln_b, rpb, w_out,
        b_out, ln1_g, ln1_b, ffn_w1, ffn_w3, ffn_w2, w_router, moe_w1, moe_w3, moe_w2, ple_w,
        ple_gate_w, ple_gate_b, ln2_g, ln2_b,
    )
    return second_block(
        x, c_2, ctx_2, c_ctx_2, w_ada_2, b_ada_2, norm_g_2, w_in_2, conv_w_2, conv_b_2,
        gate_b_2, sink_2, head_g_2, w_out_2, final_g_2,
    )


_drawn_inputs = setup_inputs


def setup_inputs(seed=0):
    import zlib

    import numpy as np

    out = dict(_drawn_inputs(seed))
    spreads = {}
    factors = {'b_in': 4.811,
     'conv_b': 4.771,
     'conv_ln_g': 8.0,
     'conv_ln_b': 8.0,
     'rpb': 8.0,
     'ple_gate_b': 8.0,
     'b_ada_2': 5.401,
     'norm_g_2': 8.0,
     'conv_b_2': 176.654,
     'sink_2': 8.0,
     'head_g_2': 8.0,
     'final_g_2': 23.657}
    for name, (base, spread) in spreads.items():
        noise = np.random.default_rng([zlib.crc32(name.encode()), seed]).standard_normal(out[name].shape)
        drawn = base * np.exp(spread * noise) if base else spread * noise
        out[name] = __import__('jax').numpy.asarray(drawn.astype(out[name].dtype))
    for name, factor in factors.items():
        out[name] = (out[name] * factor).astype(out[name].dtype)
    return out
```

```python
from contextlib import ExitStack

import numpy as np

import concourse.bass as bass
from concourse import mybir

F32 = mybir.dt.float32
ALU = mybir.AluOpType
ACT = mybir.ActivationFunctionType
AX = mybir.AxisListType

P = 128
T = 256
TT = T // P
D = 1024
KC = D // P
DEPTH = 2
CONV_CH = 512
CC = CONV_CH // P
CONV_K = 31
PAD1 = CONV_K // 2
HEADS = 8
DH = 64
GRID_W = 64
ROWS = T // GRID_W
WIN_C = 16
D_FF = 2816
EXPERTS = 8
TOP_K = 2
D_FFE = 3584
D_PLE = 256
ALPHA = (2.0 * DEPTH) ** 0.25
M_HEADS = 4
M_DH = 128
CONV_K2 = 5
PAD2 = CONV_K2 // 2
SEG2 = T + 2 * PAD2
WINDOW = 128
NEG = -1e30

UC = 2048
GW = UC // KC
SLOTS = 6
GROUPS_DENSE = D_FF // GW
GROUPS_EXPERT = D_FFE // GW
UNITS_IN = 10
UNITS_ADA = 3 * D // GW
UNITS_OUT = D // GW
UNITS_IN2 = ["mq", "mq", "mk", "mk", "vg", "mv", "mv", "aq", "aq", "ak", "az", "az", "mz", "mz", "mo", "mo"]
UNITS_BEFORE_FFN = UNITS_IN + UNITS_ADA + UNITS_OUT + 1 + UNITS_OUT
MOE_START = 2 * UNITS_BEFORE_FFN + 3 * GROUPS_DENSE
MOE_UNITS = 3 * GROUPS_EXPERT
MOE_END = MOE_START + EXPERTS * MOE_UNITS
CAP = 96
UNITS = MOE_START + EXPERTS * MOE_UNITS + DEPTH * (len(UNITS_IN2) + UNITS_OUT)
assert MOE_UNITS % SLOTS == 0

NORMS = ["in", "conv0", "ln1_0", "ln2_0", "conv1", "ln1_1", "ln2_1", "rms0", "rms1", "final"]
OUTS = [n for n in NORMS if not n.startswith("conv")]


class Columns:

    def __init__(self):
        self.at, self.n = {}, 0

    def add(self, name, n):
        self.at[name] = (self.n, n)
        self.n += n

    def __call__(self, name, j=0, n=1):
        a = self.at[name][0] + j
        return slice(a, a + n)

    def all(self, name):
        a, n = self.at[name]
        return slice(a, a + n)


def param_columns():
    c = Columns()
    c.add("ln_in_g", KC), c.add("ln_in_b", KC)
    for l in range(DEPTH):
        for name, n in (("b_a", CC), ("b_g", CC), ("b_q", CC), ("b_k", CC), ("conv_w", CC * CONV_K),
                        ("conv_b", CC), ("conv_ln_g", CC), ("conv_ln_b", CC), ("b_out", KC), ("ln1_g", KC),
                        ("ln1_b", KC), ("ple_gate_b", KC), ("ln2_g", KC), ("ln2_b", KC), ("b_v", CONV_CH),
                        ("b_ada", 3 * KC), ("norm_g", KC), ("conv_w2", 2 * M_HEADS * CONV_K2),
                        ("conv_b2", 2 * M_HEADS), ("gate_b", 4 * M_HEADS), ("sink", HEADS), ("head_g", M_HEADS)):
            c.add(f"{name}{l}", n)
    c.add("w_router", KC * EXPERTS)
    c.add("final_g", KC)
    c.add("cond", KC * 2)
    return c


def const_columns():
    c = Columns()
    for name, n in (("ident", P), ("ones", P), ("zeros", P), ("tri_f", P), ("tri_b", P), ("mask_f", P),
                    ("mask_b", P), ("rot", P), ("cos", T), ("sin", T), ("win_mask", TT * 2 * T), ("slot", CAP),
                    ("nbr_mask", TT * T), ("before", EXPERTS * EXPERTS), ("eps5", 1), ("eps6", 1), ("one", 1)):
        c.add(name, n)
    return c


PC, CN = param_columns(), const_columns()


def build(nc, weights, params, consts, x_t, ctx_t, p_t, rel, out):
    with ExitStack() as ctx:
        def sb(name, shape):
            return ctx.enter_context(nc.sbuf_tensor(name, shape, F32))

        ring = sb("ring", [P, SLOTS, UC])
        par = sb("par", [P, PC.n])
        con = sb("con", [P, CN.n])
        xc = sb("xc", [P, KC, 2 * T])
        small = sb("small", [P, 640])
        crowded = ctx.enter_context(nc.sbuf_tensor("crowded", [P, EXPERTS], mybir.dt.int32))
        WORK = 31190
        work = sb("work", [P, WORK])
        ps = ctx.enter_context(nc.psum_tensor("ps", [P, 8, 512], F32))

        def carver(space, limit):
            at = [0]

            def carve(*shape):
                n = int(np.prod(shape))
                v = space[:, at[0]:at[0] + n]
                at[0] += n
                assert at[0] <= limit, at[0]
                names = "abcd"[:len(shape)]
                if len(shape) > 1:
                    v = v.rearrange(f"p ({' '.join(names)}) -> p {' '.join(names)}",
                                    **{k: s for k, s in zip(names[1:], shape[1:])})
                return v
            return carve

        cut = carver(small, 640)
        cond_s = cut(KC * 2)
        mod = cut(DEPTH, 3 * KC, 2)
        coef = cut(KC, 2)
        bq_s = cut(DEPTH, CC)
        nsink = cut(DEPTH, HEADS)
        rmax, rsum, rinv = cut(2, 2), cut(2, 2), cut(2, 2)
        esink = cut(2, 1)
        logits, gexp, gate = cut(TT, 8), cut(TT, 8), cut(TT, 8)
        gmax, gsum = cut(TT, 8), cut(TT, 1)
        rank_t = cut(TT, 8)
        gi, gf, lf, labs = cut(4, 8), cut(4, 8), cut(4, 8), cut(4, 8)

        cut = carver(work, WORK)
        cen, sq = cut(KC, T), cut(KC, T)
        res, mix1, ple = cut(KC, T), cut(KC, T), cut(KC, T)
        h_tok = cut(TT, D)
        glu, conv_acc = cut(CC, T + 2 * PAD1), cut(CC, T)
        q1, k1, v1 = cut(CC, T), cut(CC, T), cut(TT, CONV_CH)
        relb = cut(TT, HEADS, T)
        prob1, pt1 = cut(2, TT, T), cut(2, TT, T)
        p_sb = cut(DEPTH, 2, T)
        act_sb, silu_sb = cut(2, 2, T), cut(2, 2, T)
        std1, rstd1, sig_sb = cut(T), cut(T), cut(2, T)
        gcmp, geq = (act_sb[:, i, 0, 0:TT * 64].rearrange("p (a b) -> p a b", b=64) for i in range(2))

        cut = carver(relb.rearrange("p a b c -> p (a b c)"), TT * HEADS * T)
        sel, sel_g = cut(TT, CAP), cut(TT, CAP)
        sel_gt = cut(T)
        xg, y_sb = cut(KC, CAP), cut(D)
        moe_silu_sb, moe_act_sb = cut(2, 2, CAP), cut(2, 2, CAP)
        slot_of, gate_c = cut(TT, EXPERTS + 1), cut(TT, EXPERTS + 1)
        gate_diag, gate_row = cut(TT, P), cut(T)
        counts = cut(8)

        cut = carver(work, WORK)
        xn = cut(KC, 2 * T)
        mix2 = xn
        cqk = cut(2 * M_HEADS, 2 * T)
        sq2 = cqk
        aq, ak = cut(CC, 2 * T), cut(2 * T)
        azs, mzs = cut(CC, 2 * T), cut(M_HEADS, 2 * T)
        pre_at = 4096 * 2 + 2048 + 512 + 2048 * 2
        pre = cut(2 * M_HEADS, 2, SEG2)
        vtok = cut(4, P)
        mv = cut(4, M_HEADS, M_DH + 1)
        mos, hs = cut(4, M_HEADS * M_DH), cut(4, M_HEADS * M_DH)
        state = cut(2 * M_HEADS, M_DH + 1)
        wqk, wqk_t, kw = cut(M_HEADS, P), cut(M_HEADS, P), cut(M_HEADS, P)
        prob2, pt2 = cut(2, 2 * T), cut(2, 2 * T)
        std2, rstd2 = prob2[:, 0, :], prob2[:, 1, :]
        rope_t = pt2[:, 0, 0:T]
        cs_b, cs_t, cum_a = cut(4, 8), cut(4, 8), cut(4, 8)
        m_run, m_end, m_row, nm_row, c_max, a_max = (cut(8) for _ in range(6))
        ex, wt = cut(4, 8), cut(4, 8)
        den, rms_s, rms_i = cut(M_HEADS), cut(4 * M_HEADS), cut(4 * M_HEADS)
        cut = carver(work[:, pre_at:pre_at + 8 * 2 * SEG2], 8 * 2 * SEG2)
        adiag, amask, decay = cut(8, P), cut(8, P), cut(8, P)
        num, inter_s = cut(M_HEADS, M_DH + 1), cut(M_HEADS, M_DH + 1)

        names = """weights_used inputs_loaded rel_loaded rel_ready out_stored
            norm_src norm_centered norm_squared norm_std norm_scaled norm_out
            cond_ready prep_done glu_gate glu_out qk_out v_out mod_out conv_mixed
            nbr_scored nbr_max nbr_exp nbr_prob nbr_turned nbr_out
            mix_biased ple_copied ple_gate ple_out logits_out gate_exp chosen_out places_out
            crowded_out h_turned ffn_silu ffn_act res_added
            moe_sel moe_sel_g moe_gathered moe_xg_a moe_xg_d moe_h moe_silu moe_act moe_y moe_y_a moe_y_d
            moe_scattered moe_added moe_turned moe_gates_turned moe_order moe_weighted
            pre_copied vg_out mv_copied aqk_copied azs_out mzs_out mos_out conv2_acc cqk_out rope_out
            lf_abs lf_ln lf_out cum_out adiag_out decay_masked stats_out stats_exp decay_out
            qk_weighted qk_turned keys_weighted inter_scaled state_out mh_out
            mh_sumsq mh_std mh_normed mh_mixed
            att_scored att_max att_exp att_prob att_turned att_out x_added
            pad_zeroed dve_order""".split()
        s = {n: ctx.enter_context(nc.semaphore(n)) for n in names}
        weights_in = [ctx.enter_context(nc.semaphore(f"weights_in{i}")) for i in range(SLOTS)]
        bank_full = [ctx.enter_context(nc.semaphore(f"bank_full{i}")) for i in range(8)]
        block = ctx.enter_context(nc.Block())

        N_INPUTS = 5
        placed = {}
        in_loop = {}
        ident, ones, zeros = con[:, CN.all("ident")], con[:, CN.all("ones")], con[:, CN.all("zeros")]

        def normk(name):
            return NORMS.index(name) + 1

        def outk(name):
            return OUTS.index(name) + 1

        def att_items(l):
            return [(l, i, half, qt) for i in range(CC) for half in range(2) for qt in range(4 if l == 0 else 2)]

        ATT = {it: n + 1 for n, it in enumerate(att_items(0) + att_items(1))}

        ORDER = ([2, 3, 0, 1], [3, 2, 1, 0])

        def step_no(l, j):
            return 4 * l + j + 1

        @block.tensor
        def _(eng):
            count = [0] * 8
            readers = [None] * 8
            unit_no = [0]
            release = [False]

            def fill(key, bank, read_by):
                if readers[bank] is not None:
                    eng.wait_ge(*readers[bank])
                count[bank] += 1
                placed[key] = (bank, count[bank])
                readers[bank] = read_by
                return ps[:, bank, :]

            def next_unit(it=0):
                n = unit_no[0]
                unit_no[0] += 1
                slot = n % SLOTS
                eng.wait_ge(weights_in[slot], 16 * (n // SLOTS + 1) + 16 * (MOE_UNITS // SLOTS) * it)
                release[0] = n > 0
                return ring[:, slot, :]

            def mm(o, lhs, rhs, start, stop, **kw):
                ins = eng.matmul(o, lhs, rhs, start=start, stop=stop, **kw)
                if release[0]:
                    ins.then_inc(s["weights_used"], 1)
                    release[0] = False
                return ins

            def norm(name, src, chunks, n, centred=True):
                k = normk(name)
                if k > 1:
                    eng.wait_ge(s["norm_src"], k - 1)
                if centred:
                    o = fill(("mean", name), 0, (s["norm_centered"], k))
                    for c in range(chunks):
                        last = mm(o[:, 0:n], ones, src[:, c, 0:n], c == 0, c == chunks - 1)
                    last.then_inc(bank_full[0], 1)
                eng.wait_ge(s["norm_squared"], k)
                o = fill(("var", name), 1, (s["norm_std"], k))
                b = sq if centred else sq2
                for c in range(chunks):
                    last = mm(o[:, 0:n], ones, b[:, c, 0:n], c == 0, c == chunks - 1)
                last.then_inc(bank_full[1], 1)

            def features(w, col, o, src, n, kc=KC, wide=GW):
                for c in range(kc):
                    last = mm(o, w[:, c * wide + col:c * wide + col + P], src[:, c, 0:n], c == 0, c == kc - 1)
                return last

            def tokens(w, cols, o, src, tile):
                for c in range(KC):
                    last = mm(o, src[:, c, tile * P:tile * P + P], w[:, c * GW:c * GW + cols],
                              c == 0, c == KC - 1)
                return last

            def block1_projection(l):
                eng.wait_ge(s["norm_out"], outk("in" if l == 0 else "ln2_0"))
                for j in range(CC):
                    w = next_unit()
                    o = fill(("glu", l, j), j % 4, (s["glu_out"], CC * l + j + 1))
                    features(w, 0, o[:, 0:T], xc, T)
                    features(w, P, o[:, T:2 * T], xc, T).then_inc(bank_full[j % 4], 1)
                for j in range(CC):
                    w = next_unit()
                    o = fill(("qk", l, j), 4 + j % 4, (s["qk_out"], CC * l + j + 1))
                    features(w, 0, o[:, 0:T], xc, T)
                    features(w, P, o[:, T:2 * T], xc, T).then_inc(bank_full[4 + j % 4], 1)
                for j in range(2):
                    w = next_unit()
                    o = fill(("v", l, j), 4 + j, (s["v_out"], 2 * l + j + 1))
                    tokens(w, GW, o[:, 0:T], xc, 0)
                    tokens(w, GW, o[:, T:2 * T], xc, 1).then_inc(bank_full[4 + j], 1)

            def conditions(l):
                eng.wait_ge(s["cond_ready"], 1)
                o = fill(("mod", l), 6, (s["mod_out"], l + 1))
                cond = cond_s.rearrange("p (c e) -> p c e", e=2)
                for u in range(UNITS_ADA):
                    w = next_unit()
                    for half in range(2):
                        at = 2 * (2 * u + half)
                        last = features(w, half * P, o[:, at:at + 2], cond, 2)
                last.then_inc(bank_full[6], 1)

            def block1_attention(l):
                eng.wait_ge(s["qk_out"], CC * (l + 1))
                eng.wait_ge(s["v_out"], 2 * (l + 1))
                for i in range(HEADS + 2):
                    if i < HEADS:
                        b, p0 = 2 + i % 2, DH * (i % 2)
                        o = fill(("s", l, i), b, (s["nbr_scored"], HEADS * l + i + 1))
                        for t in range(TT):
                            last = mm(o[:, t * T:(t + 1) * T], q1[p0:p0 + DH, i // 2, t * P:t * P + P],
                                      k1[p0:p0 + DH, i // 2, :], True, True)
                        last.then_inc(bank_full[b], 1)
                    if 1 <= i <= HEADS:
                        h = i - 1
                        b = 4 + h % 2
                        eng.wait_ge(s["nbr_prob"], HEADS * l + h + 1)
                        o = fill(("pt", l, h), b, (s["nbr_turned"], HEADS * l + h + 1))
                        for t in range(TT):
                            for kt in range(TT):
                                last = eng.transpose(o[:, kt * T + t * P:kt * T + t * P + P],
                                                     prob1[:, h % 2, t, kt * P:kt * P + P], ident)
                        last.then_inc(bank_full[b], 1)
                    if i >= 2:
                        h = i - 2
                        eng.wait_ge(s["nbr_turned"], HEADS * l + h + 1)
                        if h % 2 == 0:
                            o2 = fill(("o", l, h // 2), 6 + (h // 2) % 2, (s["nbr_out"], CC * l + h // 2 + 1))
                        for kt in range(TT):
                            last = mm(o2[DH * (h % 2):DH * (h % 2) + DH, 0:T],
                                      v1[:, kt, h * DH:h * DH + DH], pt1[:, h % 2, kt, :], kt == 0, kt == TT - 1)
                        if h % 2 == 1:
                            last.then_inc(bank_full[6 + (h // 2) % 2], 1)

            def block1_out(l):
                eng.wait_ge(s["conv_mixed"], CC * (l + 1))
                eng.wait_ge(s["nbr_out"], CC * (l + 1))
                for c in range(KC):
                    if c % 2 == 0:
                        w = next_unit()
                    b = 2 + c % 4
                    o = fill(("mix", l, c), b, (s["mix_biased"], KC * l + c + 1))
                    features(w, (c % 2) * P, o[:, 0:T], mix1, T).then_inc(bank_full[b], 1)

            def ple_products(l):
                w = next_unit()
                for c in range(KC):
                    if c % 2 == 0:
                        o = fill(("ple", l, c // 2), 2 + c // 2, (s["ple_copied"], 4 * l + c // 2 + 1))
                    last = features(w, c * P, o[:, (c % 2) * T:(c % 2) * T + T], p_sb[:, l], T, kc=2, wide=D)
                    if c % 2:
                        last.then_inc(bank_full[2 + c // 2], 1)
                for c in range(KC):
                    if c % 2 == 0:
                        w = next_unit()
                    b = 4 + c % 4
                    o = fill(("pgate", l, c), b, (s["ple_gate"], KC * l + c + 1))
                    features(w, (c % 2) * P, o[:, 0:T], xc, T).then_inc(bank_full[b], 1)

            def router():
                o = fill(("logits",), 0, (s["logits_out"], 1))
                for t in range(TT):
                    for c in range(KC):
                        last = mm(o[:, t * 8:t * 8 + 8], xc[:, c, t * P:t * P + P],
                                  par[:, PC("w_router", c * EXPERTS, EXPERTS)], c == 0, c == KC - 1)
                last.then_inc(bank_full[0], 1)

            def places():
                eng.wait_ge(s["chosen_out"], 1)
                o = fill(("places",), 0, (s["places_out"], 1))
                mm(o[:, 0:8], con[:, CN.all("tri_f")], rank_t[:, 0, :], True, True)
                mm(o[:, 8:16], con[:, CN.all("tri_f")], rank_t[:, 1, :], True, False)
                mm(o[:, 8:16], ones, rank_t[:, 0, :], False, True)
                mm(o[:, 16:24], ones, rank_t[:, 0, :], True, False)
                mm(o[:, 16:24], ones, rank_t[:, 1, :], False, True).then_inc(bank_full[0], 1)

            def turn_tokens():
                for t in range(TT):
                    for half in range(2):
                        b = 2 * t + half
                        o = fill(("htok", t, half), b, (s["h_turned"], b + 1))
                        for c in range(4):
                            last = eng.transpose(o[:, c * P:c * P + P], xc[:, 4 * half + c, t * P:t * P + P], ident)
                        last.then_inc(bank_full[b], 1)

            def moe():
                G = GROUPS_EXPERT
                for r in readers:
                    if r is not None:
                        eng.wait_ge(*r)
                eng.wait_ge(s["h_turned"], 4)
                ubase = unit_no[0]

                def gather(nxt):
                    eng.wait_ge(s["moe_sel"], nxt + 1)
                    for half in range(2):
                        for c in range(4):
                            for t in range(TT):
                                f = 4 * half + c
                                last = mm(ps[:, half, c * CAP:(c + 1) * CAP], h_tok[:, t, f * P:f * P + P],
                                          sel[:, t, :], t == 0, t == TT - 1)
                        last.then_inc(s["moe_gathered"], 1)

                def turn(nxt):
                    eng.wait_ge(s["moe_sel_g"], nxt + 1)
                    for t in range(TT):
                        eng.transpose(ps[0:CAP, 7, t * P:t * P + P], sel_g[:, t, :], ident)
                    mm(ps[:, 7, T:2 * T], ones, gate_diag.rearrange("p a b -> p (a b)"), True, True)\
                        .then_inc(s["moe_turned"], 1)

                def groups(it, up, down):
                    for g in range(G + 1):
                        if g < G:
                            eng.wait_ge(s["moe_act"], G * it + (g + 1))
                            if g == 1:
                                eng.wait_ge(s["moe_gates_turned"], it + 1)
                            for k in range(2):
                                w = next_unit(it)
                                for c in range(2):
                                    last = up(w, g, c, k)
                            last.then_inc(s["moe_h"], 1)
                        if g >= 1:
                            eng.wait_ge(s["moe_act"], G * it + (g + 2))
                            last = down(next_unit(it), g - 1)
                    last.then_inc(s["moe_y"], 1)

                def few_up(w, g, c, k):
                    at = (2 * c + k) * CAP
                    return features(w, c * P, ps[:, 6 + g % 2, at:at + CAP], xg, CAP)

                def few_down(w, g):
                    for c in range(2):
                        for half in range(2):
                            last = mm(ps[0:CAP, 4 + half, :], moe_act_sb[:, g % 2, c, :],
                                      w[:, c * D + half * 512:c * D + half * 512 + 512],
                                      g == 0 and c == 0, g == G - 1 and c == 1)
                    return last

                def all_up(w, g, c, k):
                    return features(w, c * P, ps[:, 4 + 2 * (g % 2) + c, k * T:(k + 1) * T], xc, T)

                def all_down(w, g):
                    first, final = g == 0, g == G - 1
                    for c in range(2):
                        for o in range(KC):
                            last = mm(ps[:, o // 2, (o % 2) * T:(o % 2) * T + T],
                                      w[:, c * D + o * P:c * D + o * P + P], act_sb[:, g % 2, c, :],
                                      first and c == 0 and o % 2 == 0, final and c == 1,
                                      skip_group_check=True)
                    return last

                gather(0)
                turn(0)
                with eng.Fori(0, EXPERTS) as it:
                    is_crowded = eng.value_load(crowded[0:1, bass.ds(it, 1)], min_val=0, max_val=1)
                    eng.wait_ge(s["moe_xg_a"], it + 1)
                    eng.wait_ge(s["moe_xg_d"], it + 1)
                    eng.wait_ge(s["moe_added"], 4 * it + 4)
                    with eng.If(is_crowded != 0):
                        unit_no[0] = ubase
                        groups(it, all_up, all_down)
                        eng.sem_inc(s["moe_scattered"], 4)
                        eng.wait_ge(s["moe_added"], 4 * it + 8)
                        gather(it + 1)
                    with eng.Else():
                        unit_no[0] = ubase
                        groups(it, few_up, few_down)
                        gather(it + 1)
                        eng.wait_ge(s["moe_y_a"], it + 1)
                        eng.wait_ge(s["moe_y_d"], it + 1)
                        eng.wait_ge(s["moe_xg_a"], it + 2)
                        eng.wait_ge(s["moe_xg_d"], it + 2)
                        for c in range(KC):
                            ins = mm(ps[:, c // 2, (c % 2) * T:(c % 2) * T + T], y_sb[0:CAP, c * P:c * P + P],
                                     sel_gt[0:CAP, :], True, True)
                            if c % 2:
                                ins.then_inc(s["moe_scattered"], 1)
                    turn(it + 1)
                unit_no[0] = ubase + EXPERTS * MOE_UNITS
                for b in range(8):
                    readers[b] = (s["norm_src"], normk("ln2_1") - 1)

            def ffn(name, groups, act_base, loops):
                for b in range(4):
                    o = fill((name, "y", b), b, (s["res_added"], 4 * (name == "moe") + b + 1))
                    mm(o, zeros, con[:, 0:512], True, False)
                for b in range(4, 8):
                    if readers[b] is not None:
                        eng.wait_ge(*readers[b])
                base, ubase = list(count), unit_no[0]
                in_loop[name] = base

                def body(it):
                    count[:], unit_no[0] = base, ubase
                    for g in range(groups + 1):
                        if g < groups:
                            b = 4 + 2 * (g % 2)
                            if isinstance(it, int) and g < 2:
                                pass
                            else:
                                eng.wait_ge(s["ffn_act"], act_base + 2 * (g - 1) + 2 * groups * it)
                            w = next_unit(it)
                            for c in range(2):
                                features(w, c * P, ps[:, b + c, 0:T], xc, T)
                            w = next_unit(it)
                            for c in range(2):
                                features(w, c * P, ps[:, b + c, T:2 * T], xc, T).then_inc(bank_full[b + c], 1)
                                count[b + c] += 1
                        if g >= 1:
                            a = act_sb[:, (g - 1) % 2]
                            eng.wait_ge(s["ffn_act"], act_base + 2 * g + 2 * groups * it)
                            w = next_unit(it)
                            for c in range(2):
                                for o in range(KC):
                                    mm(ps[:, o // 2, (o % 2) * T:(o % 2) * T + T],
                                       w[:, c * D + o * P:c * D + o * P + P], a[:, c, :], False, False,
                                       skip_group_check=True)

                if loops == 1:
                    body(0)
                else:
                    with eng.Fori(0, loops) as it:
                        body(it)
                    for b in range(4, 8):
                        count[b] = base[b] + loops * (count[b] - base[b])
                    unit_no[0] = ubase + loops * (unit_no[0] - ubase)
                for b in range(4):
                    mm(ps[:, b, :], zeros, con[:, 0:512], False, True)\
                        .then_inc(bank_full[b], 1)
                for b in range(4, 8):
                    readers[b] = (s["ffn_act"], act_base + 2 * groups * loops)

            def block2_projection(l):
                n_q = 2 * T if l == 0 else T
                q_tiles = 4 if l == 0 else 2
                eng.wait_ge(s["norm_out"], outk(f"rms{l}"))
                for c in range(2 * M_HEADS):
                    if c % 2 == 0:
                        w = next_unit()
                    o = fill(("pre", l, c), c % 4, (s["pre_copied"], 8 * l + c + 1))
                    n = n_q if c < M_HEADS else 2 * T
                    features(w, (c % 2) * P, o[:, 0:n], xn, n).then_inc(bank_full[c % 4], 1)
                w = next_unit()
                for t in range(4):
                    o = fill(("vg", l, t), 4 + t, (s["vg_out"], 4 * l + t + 1))
                    tokens(w, P + 16, o[:, 0:P + 16], xn, t).then_inc(bank_full[4 + t], 1)
                for u in range(2):
                    w = next_unit()
                    for t in range(4):
                        o = fill(("mv", l, u, t), t, (s["mv_copied"], 8 * l + 4 * u + t + 1))
                        tokens(w, GW, o[:, 0:GW], xn, t).then_inc(bank_full[t], 1)
                for c in range(CC + 1):
                    if c % 2 == 0:
                        w = next_unit()
                    b = 4 + c % 4
                    n = n_q if c < CC else 2 * T
                    o = fill(("aqk", l, c), b, (s["aqk_copied"], 5 * l + c + 1))
                    features(w, (c % 2) * P, o[:, 0:n], xn, n).then_inc(bank_full[b], 1)
                for c in range(CC):
                    if c % 2 == 0:
                        w = next_unit()
                    o = fill(("az", l, c), c, (s["azs_out"], 4 * l + c + 1))
                    features(w, (c % 2) * P, o[:, 0:n_q], xn, n_q).then_inc(bank_full[c], 1)
                for c in range(M_HEADS):
                    if c % 2 == 0:
                        w = next_unit()
                    o = fill(("mz", l, c), 4 + c, (s["mzs_out"], 4 * l + c + 1))
                    features(w, (c % 2) * P, o[:, 0:n_q], xn, n_q).then_inc(bank_full[4 + c], 1)
                for u in range(2):
                    w = next_unit()
                    for t in range(q_tiles):
                        o = fill(("mo", l, u, t), t, (s["mos_out"], 8 * l + q_tiles * u + t + 1))
                        tokens(w, GW, o[:, 0:GW], xn, t).then_inc(bank_full[t], 1)
                for c in range(CC + 1):
                    b = 4 + c % 4
                    eng.wait_ge(s["aqk_copied"], 5 * l + c + 1)
                    src = aq[:, c, 0:T] if c < CC else ak[:, 0:T]
                    o = fill(("rope", l, c), b, (s["rope_out"], 5 * l + c + 1))
                    mm(o[:, 0:T], con[:, CN.all("rot")], src, True, True).then_inc(bank_full[b], 1)

            def mlstm(l):
                eng.wait_ge(s["lf_out"], l + 1)
                o = fill(("cum", l), 0, (s["cum_out"], l + 1))
                mm(o[:, 0:16], con[:, CN.all("tri_f")], lf[:, :, 0:4], True, True)
                mm(o[:, 16:32], con[:, CN.all("tri_b")], lf[:, :, 4:8], True, True)
                mm(o[:, 32:64], ones, lf[:, :, :].rearrange("p a b -> p (a b)"), True, True)\
                    .then_inc(bank_full[0], 1)
                eng.wait_ge(s["cqk_out"], 8 * (l + 1))
                eng.wait_ge(s["mv_copied"], 8 * (l + 1))
                for j in range(4):
                    k = step_no(l, j)
                    eng.wait_ge(s["adiag_out"], k)
                    for half in range(2):
                        o = fill(("arow", l, j, half), 6 + half, (s["decay_masked"], k))
                        mm(o, ones, adiag[:, 4 * half:4 * half + 4, :].rearrange("p a b -> p (a b)"), True, True)\
                            .then_inc(bank_full[6 + half], 1)
                    for d in range(2):
                        g = 2 * (k - 1) + d + 1
                        t = ORDER[d][j]
                        tok = slice(t * P, t * P + P)
                        rows = l == 0 or t < TT
                        if rows:
                            o = fill(("sc", l, j, d), 0, (s["qk_weighted"], g))
                            for h in range(M_HEADS):
                                last = mm(o[:, h * P:h * P + P], cqk[:, h, tok], cqk[:, M_HEADS + h, tok], True, True)
                            last.then_inc(bank_full[0], 1)
                        o = fill(("kt", l, j, d), 1, (s["keys_weighted"], g))
                        for h in range(M_HEADS):
                            last = eng.transpose(o[:, h * P:h * P + P], cqk[:, M_HEADS + h, tok], ident)
                        last.then_inc(bank_full[1], 1)
                        if rows:
                            eng.wait_ge(s["state_out"], max(g + l - 1, 9 * l + 1))
                            for half in range(2):
                                o = fill(("inter", l, j, d, half), 4 + half, (s["inter_scaled"], g))
                                for h in range(2):
                                    last = mm(o[:, h * 129:h * 129 + 129], cqk[:, 2 * half + h, tok],
                                              state[:, 4 * d + 2 * half + h, :], True, True)
                                last.then_inc(bank_full[4 + half], 1)
                        eng.wait_ge(s["keys_weighted"], g)
                        for half in range(2):
                            o = fill(("ds", l, j, d, half), 2 + half, (s["state_out"], g + l + 1))
                            for h in range(2):
                                last = mm(o[:, h * 129:h * 129 + 129], kw[:, 2 * half + h, :],
                                          mv[:, t, 2 * half + h, :], True, True)
                            last.then_inc(bank_full[2 + half], 1)
                        if rows:
                            eng.wait_ge(s["qk_weighted"], g)
                            o = fill(("wt", l, j, d), 0, (s["qk_turned"], g))
                            for h in range(M_HEADS):
                                last = eng.transpose(o[:, h * P:h * P + P], wqk[:, h, :], ident)
                            last.then_inc(bank_full[0], 1)
                            eng.wait_ge(s["qk_turned"], g)
                            for half in range(2):
                                o = fill(("intra", l, j, d, half), 6 + half, (s["mh_out"], g))
                                for h in range(2):
                                    last = mm(o[:, h * 129:h * 129 + 129], wqk_t[:, 2 * half + h, :],
                                              mv[:, t, 2 * half + h, :], True, True)
                                last.then_inc(bank_full[6 + half], 1)

            def mlstm_turn(l):
                eng.wait_ge(s["mh_normed"], l + 1)
                for t in range(4 if l == 0 else 2):
                    o = fill(("mt", l, t), t, (s["mh_mixed"], 4 * l + t + 1))
                    for h in range(M_HEADS):
                        last = eng.transpose(o[:, h * P:h * P + P], hs[:, t, h * P:h * P + P], ident)
                    last.then_inc(bank_full[t], 1)

            def block2_attention(l):
                items = att_items(l)
                eng.wait_ge(s["rope_out"], 5 * (l + 1))
                eng.wait_ge(s["vg_out"], 4 * (l + 1))
                for n in range(len(items) + 2):
                    if n < len(items):
                        _, i, half, qt = items[n]
                        k = ATT[items[n]]
                        b, p0 = 2 + k % 2, DH * half
                        o = fill(("as",) + items[n], b, (s["att_scored"], k))
                        keys = slice(0, 2 * T) if qt < TT else slice(T, 2 * T)
                        cols = slice(0, 2 * T) if qt < TT else slice(0, T)
                        mm(o[:, cols], aq[p0:p0 + DH, i, qt * P:qt * P + P], ak[p0:p0 + DH, keys], True, True)\
                            .then_inc(bank_full[b], 1)
                    if 1 <= n <= len(items):
                        k = ATT[items[n - 1]]
                        kts = 4 if items[n - 1][3] < TT else 2
                        b = 4 + k % 2
                        eng.wait_ge(s["att_prob"], k)
                        o = fill(("at",) + items[n - 1], b, (s["att_turned"], k))
                        for kt in range(kts):
                            last = eng.transpose(o[:, kt * P:kt * P + P], prob2[:, k % 2, kt * P:kt * P + P], ident)
                        last.then_inc(bank_full[b], 1)
                    if n >= 2:
                        _, i, half, qt = items[n - 2]
                        k = ATT[items[n - 2]]
                        eng.wait_ge(s["att_turned"], k)
                        if half == 0 and qt == 0:
                            o2 = fill(("ao", l, i), 6 + i % 2, (s["att_out"], CC * l + i + 1))
                        kts = 4 if qt < TT else 2
                        for kt in range(kts):
                            vt = kt if qt < TT else TT + kt
                            last = mm(o2[DH * half:DH * half + DH, qt * P:qt * P + P],
                                      vtok[:, vt, DH * half:DH * half + DH], pt2[:, k % 2, kt * P:kt * P + P],
                                      kt == 0, kt == kts - 1)
                        if half == 1 and qt == (3 if l == 0 else 1):
                            last.then_inc(bank_full[6 + i % 2], 1)

            def block2_out(l):
                n = 2 * T if l == 0 else T
                eng.wait_ge(s["mh_mixed"], 4 if l == 0 else 6)
                eng.wait_ge(s["att_out"], CC * (l + 1))
                for c in range(KC):
                    if c % 2 == 0:
                        w = next_unit()
                    o = fill(("xo", l, c), 2 + c % 4, (s["x_added"], KC * l + c + 1))
                    features(w, (c % 2) * P, o[:, 0:n], mix2, n).then_inc(bank_full[2 + c % 4], 1)

            eng.wait_ge(s["inputs_loaded"], 16 * N_INPUTS)
            norm("in", xc, KC, T)
            for l in range(DEPTH):
                block1_projection(l)
                conditions(l)
                norm(f"conv{l}", conv_acc, CC, T)
                block1_attention(l)
                block1_out(l)
                norm(f"ln1_{l}", res, KC, T)
                eng.wait_ge(s["norm_out"], outk(f"ln1_{l}"))
                if l == 1:
                    router()
                    turn_tokens()
                    places()
                ple_products(l)
                if l == 1:
                    moe()
                else:
                    ffn("dense", GROUPS_DENSE, 0, 1)
                norm(f"ln2_{l}", res, KC, T)
            for l in range(DEPTH):
                norm(f"rms{l}", xc, KC, 2 * T, centred=False)
                block2_projection(l)
                mlstm(l)
                mlstm_turn(l)
                block2_attention(l)
                block2_out(l)
            norm("final", xc, KC, T, centred=False)
            assert unit_no[0] == UNITS, (unit_no[0], UNITS)

        def tile(eng, *key):
            b, n = placed[key]
            eng.wait_ge(bank_full[b], n)
            return ps[:, b, :]

        @block.sync
        def _(eng):
            for n in range(SLOTS):
                eng.dma_start(ring[:, n, :], weights[n]).then_inc(weights_in[n], 16)
            rounds = (UNITS - SLOTS) // SLOTS
            with eng.Fori(0, rounds) as r:
                for i in range(SLOTS):
                    eng.wait_ge(s["weights_used"], SLOTS * r + (i + 1))
                    eng.dma_start(ring[:, i, :], weights[SLOTS * r + (SLOTS + i)]).then_inc(weights_in[i], 16)
            for n in range(SLOTS * (rounds + 1), UNITS):
                eng.wait_ge(s["weights_used"], n - SLOTS + 1)
                eng.dma_start(ring[:, n % SLOTS, :], weights[n]).then_inc(weights_in[n % SLOTS], 16)
            eng.wait_ge(s["norm_out"], outk("final"))
            eng.dma_start(out, cen).then_inc(s["out_stored"], 16)
            eng.wait_ge(s["out_stored"], 16)

        @block.gpsimd
        def _(eng):
            eng.wait_ge(s["inputs_loaded"], 16 * N_INPUTS)
            for l in range(DEPTH):
                if l:
                    eng.wait_ge(s["nbr_scored"], HEADS * l)
                for r in range(ROWS):
                    p0 = GRID_W * (r % 2)
                    src = rel[l, :, :, ROWS - 1 - r:2 * ROWS - 1 - r, :].rearrange("c h i j -> c h (i j)")
                    eng.dma_start(relb[p0:p0 + GRID_W, r // 2, :, :], src).then_inc(s["rel_loaded"], 16)
                eng.wait_ge(s["rel_loaded"], 16 * ROWS * (l + 1))
                for t in range(TT):
                    mask = con[:, CN("nbr_mask", t * T, T)].unsqueeze(1).broadcast_to([P, HEADS, T])
                    eng.tensor_tensor(relb[:, t], relb[:, t], mask, ALU.add).then_inc(s["rel_ready"], 1)

        @block.scalar
        def _(eng):
            eng.dma_start(par[:, :], params).then_inc(s["inputs_loaded"], 16)
            eng.dma_start(con[:, :], consts).then_inc(s["inputs_loaded"], 16)
            eng.dma_start(xc[:, :, 0:T], x_t).then_inc(s["inputs_loaded"], 16)
            eng.dma_start(xc[:, :, T:2 * T], ctx_t).then_inc(s["inputs_loaded"], 16)
            eng.dma_start(p_sb, p_t).then_inc(s["inputs_loaded"], 16)

            def norm(name, chunks, n, centred=True, src=None):
                k = normk(name)
                if centred:
                    eng.wait_ge(s["norm_centered"], k)
                    eng.activation(sq[:, 0:chunks, :], cen[:, 0:chunks, :], ACT.Square).then_inc(s["norm_squared"], 1)
                    o, eps = std1, "eps5"
                else:
                    eng.wait_ge(s["norm_src"], k - 1)
                    eng.activation(sq2[:, 0:chunks, 0:n], src[:, 0:chunks, 0:n], ACT.Square)\
                        .then_inc(s["norm_squared"], 1)
                    o, eps = std2, "eps6"
                v = tile(eng, "var", name)
                eng.activation(o[:, 0:n], v[:, 0:n], ACT.Sqrt, bias=con[:, CN(eps)], scale=1.0 / (chunks * P))\
                    .then_inc(s["norm_std"], 1)

            def block1_projection(l):
                for j in range(CC):
                    o = tile(eng, "glu", l, j)
                    if CC * l + j >= 2:
                        eng.wait_ge(s["glu_out"], CC * l + j - 1)
                    eng.activation(sig_sb[:, j % 2, :], o[:, T:2 * T], ACT.Sigmoid, bias=par[:, PC(f"b_g{l}", j)])\
                        .then_inc(s["glu_gate"], 1)
                for j in range(CC):
                    o = tile(eng, "qk", l, j)
                    eng.activation(q1[:, j, :], o[:, 0:T], ACT.Identity, bias=bq_s[:, l, j:j + 1], scale=DH ** -0.5)
                    eng.activation(k1[:, j, :], o[:, T:2 * T], ACT.Identity, bias=par[:, PC(f"b_k{l}", j)])\
                        .then_inc(s["qk_out"], 1)

            def conv_silu(l):
                eng.wait_ge(s["norm_scaled"], normk(f"conv{l}"))
                for j in range(CC):
                    eng.activation(mix1[:, j, :], cen[:, j, :], ACT.Silu, bias=par[:, PC(f"conv_ln_b{l}", j)],
                                   scale=par[:, PC(f"conv_ln_g{l}", j)]).then_inc(s["conv_mixed"], 1)

            def block1_attention(l):
                for i in range(HEADS + 2):
                    if i < HEADS:
                        k = HEADS * l + i + 1
                        eng.wait_ge(s["nbr_max"], k)
                        for t in range(TT):
                            eng.activation(prob1[:, i % 2, t, :], prob1[:, i % 2, t, :], ACT.Exp,
                                           bias=rmax[:, i % 2, t:t + 1], accum_out=rsum[:, i % 2, t:t + 1])\
                                .then_inc(s["nbr_exp"], 1)
                    if 1 <= i <= HEADS:
                        o = tile(eng, "pt", l, i - 1)
                        eng.activation(pt1[:, (i - 1) % 2].rearrange("p a b -> p (a b)"), o, ACT.Copy)\
                            .then_inc(s["nbr_turned"], 1)
                    if i >= 3 and i % 2 == 1:
                        h2 = (i - 3) // 2
                        o = tile(eng, "o", l, h2)
                        eng.activation(mix1[:, CC + h2, :], o[:, 0:T], ACT.Copy).then_inc(s["nbr_out"], 1)

            def block1_out(l):
                for c in range(KC):
                    o = tile(eng, "mix", l, c)
                    eng.activation(sq[:, c, :], o[:, 0:T], ACT.Identity, bias=par[:, PC(f"b_out{l}", c)])\
                        .then_inc(s["mix_biased"], 1)

            def ple_products(l):
                for c in range(4):
                    o = tile(eng, "ple", l, c)
                    eng.activation(ple[:, 2 * c:2 * c + 2, :].rearrange("p a b -> p (a b)"), o, ACT.Copy)\
                        .then_inc(s["ple_copied"], 1)
                for c in range(KC):
                    o = tile(eng, "pgate", l, c)
                    if KC * l + c >= 2:
                        eng.wait_ge(s["ple_out"], KC * l + c - 1)
                    eng.activation(sig_sb[:, c % 2, :], o[:, 0:T], ACT.Sigmoid,
                                   bias=par[:, PC(f"ple_gate_b{l}", c)]).then_inc(s["ple_gate"], 1)

            def gate_exp():
                eng.wait_ge(s["gate_exp"], 1)
                eng.activation(gexp, gexp, ACT.Exp).then_inc(s["gate_exp"], 1)

            def tokens_copy():
                for t in range(TT):
                    for half in range(2):
                        o = tile(eng, "htok", t, half)
                        eng.activation(h_tok[:, t, half * 512:half * 512 + 512], o, ACT.Copy).then_inc(s["h_turned"], 1)

            def moe():
                G = GROUPS_EXPERT

                def gathered(nxt):
                    eng.wait_ge(s["moe_gathered"], nxt * 2 + 1)
                    eng.activation(xg[:, 0:4, :].rearrange("p a b -> p (a b)"), ps[:, 0, 0:4 * CAP], ACT.Copy)\
                        .then_inc(s["moe_xg_a"], 1)

                def gates_turned(nxt):
                    eng.wait_ge(s["moe_turned"], nxt + 1)
                    eng.activation(sel_gt[0:CAP, :], ps[0:CAP, 7, 0:T], ACT.Copy)
                    eng.activation(gate_row, ps[:, 7, T:2 * T], ACT.Copy).then_inc(s["moe_gates_turned"], 1)

                gathered(0)
                gates_turned(0)
                eng.wait_ge(s["crowded_out"], 1)
                with eng.Fori(0, EXPERTS) as it:
                    is_crowded = eng.value_load(crowded[0:1, bass.ds(it, 1)], min_val=0, max_val=1)
                    with eng.If(is_crowded != 0):
                        for g in range(G):
                            b = 4 + 2 * (g % 2)
                            eng.wait_ge(s["moe_h"], it * G + (g + 1))
                            eng.activation(silu_sb[:, g % 2], ps[:, b:b + 2, 0:T], ACT.Silu).then_inc(s["moe_silu"], 1)
                        eng.sem_inc(s["moe_y_a"], 1)
                    with eng.Else():
                        for g in range(G):
                            h = ps[:, 6 + g % 2, 0:4 * CAP].rearrange("p (c k n) -> p c k n", c=2, k=2)
                            eng.wait_ge(s["moe_h"], it * G + (g + 1))
                            eng.activation(moe_silu_sb[:, g % 2], h[:, :, 0, :], ACT.Silu).then_inc(s["moe_silu"], 1)
                        eng.wait_ge(s["moe_y"], it + 1)
                        eng.activation(y_sb[0:CAP, 0:512], ps[0:CAP, 4, :], ACT.Copy).then_inc(s["moe_y_a"], 1)
                    gathered(it + 1)
                    gates_turned(it + 1)

            def ffn(name, groups, loops):
                base = in_loop[name]

                def body(it):
                    for g in range(groups):
                        for c in range(2):
                            b = 4 + 2 * (g % 2) + c
                            eng.wait_ge(bank_full[b], base[b] + g // 2 + 1 + (groups // 2) * it)
                            eng.activation(silu_sb[:, g % 2, c, :], ps[:, b, 0:T], ACT.Silu)\
                                .then_inc(s["ffn_silu"], 1)

                if loops == 1:
                    body(0)
                else:
                    with eng.Fori(0, loops) as it:
                        body(it)

            def block2_projection(l):
                n_q = 2 * T if l == 0 else T
                q_tiles = 4 if l == 0 else 2
                segs = 2 if l == 0 else 1
                eng.wait_ge(s["pad_zeroed"], l + 1)
                for c in range(2 * M_HEADS):
                    o = tile(eng, "pre", l, c)
                    sg = segs if c < M_HEADS else 2
                    eng.activation(pre[:, c, 0:sg, PAD2:PAD2 + T],
                                   o[:, 0:sg * T].rearrange("p (a b) -> p a b", b=T), ACT.Copy)\
                        .then_inc(s["pre_copied"], 1)
                for u in range(2):
                    for t in range(4):
                        o = tile(eng, "mv", l, u, t)
                        eng.activation(mv[:, t, 2 * u:2 * u + 2, 0:M_DH],
                                       o[:, 0:GW].rearrange("p (a b) -> p a b", b=M_DH), ACT.Copy)\
                            .then_inc(s["mv_copied"], 1)
                for c in range(CC + 1):
                    o = tile(eng, "aqk", l, c)
                    if c < CC:
                        eng.activation(aq[:, c, 0:n_q], o[:, 0:n_q], ACT.Copy, scale=DH ** -0.5)\
                            .then_inc(s["aqk_copied"], 1)
                    else:
                        eng.activation(ak, o, ACT.Copy).then_inc(s["aqk_copied"], 1)
                for c in range(CC):
                    o = tile(eng, "az", l, c)
                    eng.activation(azs[:, c, 0:n_q], o[:, 0:n_q], ACT.Silu).then_inc(s["azs_out"], 1)
                for c in range(M_HEADS):
                    o = tile(eng, "mz", l, c)
                    eng.activation(mzs[:, c, 0:n_q], o[:, 0:n_q], ACT.Silu).then_inc(s["mzs_out"], 1)
                for c in range(2 * M_HEADS):
                    eng.wait_ge(s["conv2_acc"], 8 * l + c + 1)
                    n = n_q if c < M_HEADS else 2 * T
                    eng.activation(cqk[:, c, 0:n], cqk[:, c, 0:n], ACT.Silu, bias=par[:, PC(f"conv_b2{l}", c)])\
                        .then_inc(s["cqk_out"], 1)
                for u in range(2):
                    for t in range(q_tiles):
                        o = tile(eng, "mo", l, u, t)
                        eng.activation(mos[:, t, u * GW:(u + 1) * GW], o[:, 0:GW], ACT.Sigmoid)\
                            .then_inc(s["mos_out"], 1)

            def mlstm(l):
                eng.wait_ge(s["lf_abs"], l + 1)
                eng.activation(labs, labs, ACT.Exp, scale=-1.0).then_inc(s["lf_ln"], 1)
                eng.wait_ge(s["lf_ln"], 2 * l + 1)
                eng.activation(labs, labs, ACT.Ln, bias=con[:, CN("one")]).then_inc(s["lf_ln"], 1)
                for j in range(4):
                    k = step_no(l, j)
                    eng.wait_ge(s["stats_out"], k)
                    eng.activation(wt, ex, ACT.Exp).then_inc(s["stats_exp"], 1)
                    for d in range(2):
                        t = ORDER[d][j]
                        for h in range(M_HEADS):
                            n = 4 * d + h
                            ins = eng.activation(decay[:, n, :], amask[:, n, :], ACT.Exp, bias=nm_row[:, n:n + 1])
                        ins.then_inc(s["decay_out"], 1)
                    eng.wait_ge(s["stats_exp"], k)
                    for d in range(2):
                        g = 2 * (k - 1) + d + 1
                        t = ORDER[d][j]
                        if l == 0 or t < TT:
                            if g > 1:
                                eng.wait_ge(s["mh_out"], g - 1)
                            for half in range(2):
                                o = tile(eng, "inter", l, j, d, half)
                                for h in range(2):
                                    n = 2 * half + h
                                    ins = eng.activation(inter_s[:, n, :], o[:, h * 129:h * 129 + 129], ACT.Copy,
                                                         scale=wt[:, 0, 4 * d + n:4 * d + n + 1])
                            ins.then_inc(s["inter_scaled"], 1)
                            o = tile(eng, "wt", l, j, d)
                            eng.activation(wqk_t.rearrange("p a b -> p (a b)"), o, ACT.Copy).then_inc(s["qk_turned"], 1)
                        else:
                            eng.wait_ge(s["mh_out"], g)
                            eng.sem_inc(s["inter_scaled"], 1)
                            eng.sem_inc(s["qk_turned"], 1)

            def mlstm_std(l):
                tiles = 4 if l == 0 else 2
                eng.wait_ge(s["mh_sumsq"], l + 1)
                n = tiles * M_HEADS
                eng.activation(rms_i[:, 0:n], rms_s[:, 0:n], ACT.Sqrt, bias=con[:, CN("eps6")], scale=1.0 / M_DH)\
                    .then_inc(s["mh_std"], 1)

            def block2_attention(l):
                items = att_items(l)
                for n in range(len(items) + 1):
                    if n < len(items):
                        _, i, half, qt = items[n]
                        k = ATT[items[n]]
                        h = i + CC * half
                        w = 2 * T if qt < TT else T
                        eng.wait_ge(s["att_max"], k)
                        eng.activation(esink[:, k % 2, :], par[:, PC(f"sink{l}", h)], ACT.Exp,
                                       bias=rmax[:, k % 2, 0:1])
                        eng.activation(prob2[:, k % 2, 0:w], prob2[:, k % 2, 0:w], ACT.Exp,
                                       bias=rmax[:, k % 2, 0:1], accum_out=rsum[:, k % 2, 0:1])\
                            .then_inc(s["att_exp"], 1)
                    if n >= 1:
                        k = ATT[items[n - 1]]
                        w = 2 * T if items[n - 1][3] < TT else T
                        o = tile(eng, "at", *items[n - 1])
                        eng.activation(pt2[:, k % 2, 0:w], o[:, 0:w], ACT.Copy).then_inc(s["att_turned"], 1)

            eng.wait_ge(s["inputs_loaded"], 16 * N_INPUTS)
            eng.activation(cond_s, par[:, PC.all("cond")], ACT.Silu).then_inc(s["cond_ready"], 1)
            norm("in", KC, T)
            eng.wait_ge(s["prep_done"], 1)
            for l in range(DEPTH):
                block1_projection(l)
                norm(f"conv{l}", CC, T)
                conv_silu(l)
                block1_attention(l)
                block1_out(l)
                norm(f"ln1_{l}", KC, T)
                if l == 1:
                    gate_exp()
                    tokens_copy()
                ple_products(l)
                if l == 1:
                    moe()
                else:
                    ffn("dense", GROUPS_DENSE, 1)
                norm(f"ln2_{l}", KC, T)
            for l in range(DEPTH):
                norm(f"rms{l}", KC, 2 * T, centred=False, src=xc)
                block2_projection(l)
                mlstm(l)
                mlstm_std(l)
                block2_attention(l)
            norm("final", KC, T, centred=False, src=xc)

        @block.vector
        def _(eng):
            order = [0]

            def link(ins):
                order[0] += 1
                ins.then_inc(s["dve_order"], 1)
                eng.wait_ge(s["dve_order"], order[0])

            def rows(v, a):
                return v.unsqueeze(1).broadcast_to([P, a, v.shape[1]])

            def norm(name, src, chunks, n, gain, centred=True, dst=None):
                k = normk(name)
                if centred:
                    o = tile(eng, "mean", name)
                    eng.scalar_tensor_tensor(out=cen[:, 0:chunks, :], in0=rows(o[:, 0:n], chunks),
                                             scalar=-1.0 / (chunks * P), in1=src[:, 0:chunks, 0:n],
                                             op0=ALU.mult, op1=ALU.add).then_inc(s["norm_centered"], 1)
                    a, std, rstd = cen, std1, rstd1
                else:
                    a, std, rstd = src, std2, rstd2
                eng.wait_ge(s["norm_std"], k)
                link(eng.reciprocal(rstd[:, 0:n], std[:, 0:n]))
                to = cen if centred else (xn if dst is None else dst)
                eng.tensor_tensor(to[:, 0:chunks, 0:n], a[:, 0:chunks, 0:n], rows(rstd[:, 0:n], chunks), ALU.mult)\
                    .then_inc(s["norm_scaled"], 1)
                eng.wait_ge(s["norm_scaled"], k)
                if gain is None:
                    return
                for c in range(chunks):
                    last = gain(c, to)
                last.then_inc(s["norm_out"], 1)

            def layer_gain(g, b, dst):
                def f(c, a):
                    return eng.tensor_scalar(dst[:, c, 0:T], a[:, c, 0:T], par[:, PC(g, c)], par[:, PC(b, c)],
                                             ALU.mult, ALU.add)
                return f

            def block1_projection(l):
                for j in range(CC):
                    o = tile(eng, "glu", l, j)
                    eng.wait_ge(s["glu_gate"], CC * l + j + 1)
                    eng.scalar_tensor_tensor(out=glu[:, j, PAD1:PAD1 + T], in0=o[:, 0:T],
                                             scalar=par[:, PC(f"b_a{l}", j)], in1=sig_sb[:, j % 2, :],
                                             op0=ALU.add, op1=ALU.mult).then_inc(s["glu_out"], 1)

            def conv(l):
                eng.wait_ge(s["glu_out"], CC * (l + 1))
                first = order[0]
                for tap in range(CONV_K):
                    for j in range(CC):
                        w = par[:, PC(f"conv_w{l}", j * CONV_K + tap)]
                        src = glu[:, j, tap:tap + T]
                        if tap:
                            eng.wait_ge(s["dve_order"], first + (tap - 1) * CC + j + 1)
                        if tap == 0:
                            ins = eng.tensor_scalar(conv_acc[:, j, :], src, w, par[:, PC(f"conv_b{l}", j)],
                                                    ALU.mult, ALU.add)
                        else:
                            ins = eng.scalar_tensor_tensor(out=conv_acc[:, j, :], in0=src, scalar=w,
                                                           in1=conv_acc[:, j, :], op0=ALU.mult, op1=ALU.add)
                        if tap == CONV_K - 1 and j == CC - 1:
                            ins.then_inc(s["norm_src"], 1)
                        else:
                            ins.then_inc(s["dve_order"], 1)
                            order[0] += 1
                eng.wait_ge(s["norm_src"], normk(f"conv{l}") - 1)
                eng.wait_ge(s["dve_order"], order[0])

            def values(l):
                for j in range(2):
                    o = tile(eng, "v", l, j)
                    bias = rows(par[:, PC(f"b_v{l}", j * GW, GW)], TT)
                    eng.tensor_tensor(v1[:, :, j * GW:(j + 1) * GW], o.rearrange("p (a b) -> p a b", b=GW), bias,
                                      ALU.add).then_inc(s["v_out"], 1)

            def conditions(l):
                o = tile(eng, "mod", l)
                m = mod[:, l]
                bias = par[:, PC.all(f"b_ada{l}")].unsqueeze(2).broadcast_to([P, 3 * KC, 2])
                eng.tensor_tensor(m, o[:, 0:6 * KC].rearrange("p (a b) -> p a b", b=2), bias, ALU.add)\
                    .then_inc(s["mod_out"], 1)

            def block1_attention(l):
                eng.wait_ge(s["rel_ready"], TT * (l + 1))
                for i in range(HEADS + 1):
                    if i < HEADS:
                        k = HEADS * l + i + 1
                        pr = prob1[:, i % 2]
                        o = tile(eng, "s", l, i)
                        eng.tensor_tensor(pr, o.rearrange("p (a b) -> p a b", b=T), relb[:, :, i, :], ALU.add)\
                            .then_inc(s["nbr_scored"], 1)
                        eng.wait_ge(s["nbr_scored"], k)
                        eng.tensor_reduce(rmax[:, i % 2, :], pr, AX.X, ALU.max, negate=True).then_inc(s["nbr_max"], 1)
                    if i >= 1:
                        h = i - 1
                        eng.wait_ge(s["nbr_exp"], 2 * (HEADS * l + h + 1))
                        link(eng.reciprocal(rinv[:, h % 2, :], rsum[:, h % 2, :]))
                        for t in range(TT):
                            ins = eng.tensor_scalar(prob1[:, h % 2, t, :], prob1[:, h % 2, t, :],
                                                    rinv[:, h % 2, t:t + 1], None, ALU.mult)
                        ins.then_inc(s["nbr_prob"], 1)

            def block1_out(l):
                for c in range(KC):
                    eng.wait_ge(s["mix_biased"], KC * l + c + 1)
                    ins = eng.scalar_tensor_tensor(out=res[:, c, :], in0=xc[:, c, 0:T], scalar=ALPHA,
                                                   in1=sq[:, c, :], op0=ALU.mult, op1=ALU.add)
                ins.then_inc(s["norm_src"], 1)
                eng.wait_ge(s["norm_src"], normk(f"ln1_{l}") - 1)

            def routing():
                o = tile(eng, "logits")
                eng.tensor_copy(logits, o[:, 0:TT * 8].rearrange("p (a b) -> p a b", b=8))\
                    .then_inc(s["logits_out"], 1)
                eng.wait_ge(s["logits_out"], 1)
                link(eng.tensor_reduce(gmax[:, :, 0], logits, AX.X, ALU.max))
                eng.tensor_tensor(gexp, logits, gmax[:, :, 0:1].broadcast_to([P, TT, 8]), ALU.subtract)\
                    .then_inc(s["gate_exp"], 1)
                before = con[:, CN.all("before")].rearrange("p (a b) -> p a b", b=8)
                for t in range(TT):
                    other = logits[:, t, :].unsqueeze(1).broadcast_to([P, 8, 8])
                    own = logits[:, t, :].unsqueeze(2).broadcast_to([P, 8, 8])
                    gc = gcmp[:, t, :].rearrange("p (a b) -> p a b", b=8)
                    ge = geq[:, t, :].rearrange("p (a b) -> p a b", b=8)
                    link(eng.tensor_tensor(gc, other, own, ALU.is_gt))
                    link(eng.tensor_tensor(ge, other, own, ALU.is_equal))
                    link(eng.tensor_tensor(ge, ge, before, ALU.mult))
                    link(eng.tensor_tensor(gc, gc, ge, ALU.add))
                    link(eng.tensor_reduce(rank_t[:, t, :], gc, AX.X, ALU.add))
                eng.tensor_scalar(rank_t, rank_t, float(TOP_K), None, ALU.is_lt).then_inc(s["chosen_out"], 1)
                eng.wait_ge(s["chosen_out"], 1)
                eng.wait_ge(s["gate_exp"], 2)
                link(eng.tensor_tensor(gate, gexp, rank_t, ALU.mult))
                link(eng.tensor_reduce(gsum[:, :, 0], gate, AX.X, ALU.add))
                link(eng.reciprocal(gsum, gsum))
                link(eng.tensor_tensor(gate, gate, gsum.broadcast_to([P, TT, 8]), ALU.mult))

            def places():
                o = tile(eng, "places")
                in_order = o[:, 0:16].rearrange("p (a b) -> p a b", b=8)
                eng.tensor_tensor(slot_of[:, :, 0:8], in_order, rank_t, ALU.mult).then_inc(s["dve_order"], 1)
                order[0] += 1
                eng.tensor_copy(counts, o[:, 16:24]).then_inc(s["places_out"], 1)
                eng.wait_ge(s["dve_order"], order[0])
                eng.wait_ge(s["places_out"], 1)
                link(eng.tensor_scalar(slot_of[:, :, 0:8], slot_of[:, :, 0:8], -1.0, None, ALU.add))
                link(eng.tensor_copy(slot_of[:, :, 8:9], slot_of[:, :, 0:1]))
                link(eng.tensor_copy(gate_c[:, :, 0:8], gate))
                link(eng.tensor_copy(gate_c[:, :, 8:9], gate[:, :, 0:1]))
                eng.tensor_scalar(crowded[:, :], counts, CAP + 0.5, None, ALU.is_gt).then_inc(s["crowded_out"], 1)

            def moe():
                G = GROUPS_EXPERT

                def gathered(nxt):
                    eng.wait_ge(s["moe_gathered"], nxt * 2 + 2)
                    eng.tensor_copy(xg[:, 4:8, :].rearrange("p a b -> p (a b)"), ps[:, 1, 0:4 * CAP])\
                        .then_inc(s["moe_xg_d"], 1)

                def select(e):
                    place = slot_of[:, :, bass.ds(e, 1)].broadcast_to([P, TT, CAP])
                    gates = gate_c[:, :, bass.ds(e, 1)]
                    eng.tensor_tensor(sel, rows(con[:, CN.all("slot")], TT), place, ALU.is_equal)\
                        .then_inc(s["moe_sel"], 1)
                    eng.tensor_tensor(gate_diag, rows(ident, TT), gates.broadcast_to([P, TT, P]), ALU.mult)
                    eng.wait_ge(s["moe_sel"], e + 1)
                    eng.tensor_tensor(sel_g, sel, gates.broadcast_to([P, TT, CAP]), ALU.mult)\
                        .then_inc(s["moe_sel_g"], 1)

                eng.sem_inc(s["moe_act"], 2)
                eng.sem_inc(s["moe_added"], 4)
                eng.wait_ge(s["crowded_out"], 1)
                select(0)
                gathered(0)
                with eng.Fori(0, EXPERTS) as it:
                    is_crowded = eng.value_load(crowded[0:1, bass.ds(it, 1)], min_val=0, max_val=1)
                    eng.wait_ge(s["moe_turned"], it + 1)
                    eng.wait_ge(s["moe_added"], it * 4 + 4)
                    select(it + 1)
                    with eng.If(is_crowded != 0):
                        eng.wait_ge(s["moe_gates_turned"], it + 1)
                        for g in range(G):
                            b = 4 + 2 * (g % 2)
                            v = silu_sb[:, g % 2]
                            eng.wait_ge(s["moe_silu"], it * G + (g + 1))
                            eng.tensor_tensor(v, v, rows(gate_row, 2), ALU.mult).then_inc(s["moe_weighted"], 1)
                            eng.wait_ge(s["moe_weighted"], it * G + (g + 1))
                            eng.tensor_tensor(act_sb[:, g % 2], v, ps[:, b:b + 2, T:2 * T], ALU.mult)\
                                .then_inc(s["moe_act"], 1)
                        eng.wait_ge(s["moe_y"], it + 1)
                        eng.sem_inc(s["moe_y_d"], 1)
                        for b in range(4):
                            r = res[:, 2 * b:2 * b + 2, :]
                            eng.tensor_tensor(r, ps[:, b, :].rearrange("p (a b) -> p a b", b=T), r, ALU.add)\
                                .then_inc(s["moe_added"], 1)
                        gathered(it + 1)
                    with eng.Else():
                        eng.sem_inc(s["moe_weighted"], G)
                        for g in range(G):
                            h = ps[:, 6 + g % 2, 0:4 * CAP].rearrange("p (c k n) -> p c k n", c=2, k=2)
                            eng.wait_ge(s["moe_silu"], it * G + (g + 1))
                            eng.tensor_tensor(moe_act_sb[:, g % 2], moe_silu_sb[:, g % 2], h[:, :, 1, :], ALU.mult)\
                                .then_inc(s["moe_act"], 1)
                        eng.wait_ge(s["moe_y"], it + 1)
                        eng.tensor_copy(y_sb[0:CAP, 512:1024], ps[0:CAP, 5, :]).then_inc(s["moe_y_d"], 1)
                        gathered(it + 1)
                        for b in range(4):
                            r = res[:, 2 * b:2 * b + 2, :]
                            eng.wait_ge(s["moe_scattered"], it * 4 + (b + 1))
                            eng.tensor_tensor(r, ps[:, b, :].rearrange("p (a b) -> p a b", b=T), r, ALU.add)\
                                .then_inc(s["moe_added"], 1)
                eng.wait_ge(s["moe_added"], 4 * EXPERTS + 4)
                eng.sem_inc(s["norm_src"], 1)

            def ple_products(l):
                eng.wait_ge(s["ple_copied"], 4 * (l + 1))
                for c in range(KC):
                    eng.wait_ge(s["ple_gate"], KC * l + c + 1)
                    eng.tensor_tensor(ple[:, c, :], ple[:, c, :], sig_sb[:, c % 2, :], ALU.mult)\
                        .then_inc(s["ple_out"], 1)
                eng.wait_ge(s["ple_out"], KC * (l + 1))
                link(eng.scalar_tensor_tensor(out=res, in0=xc[:, :, 0:T], scalar=ALPHA, in1=ple,
                                              op0=ALU.mult, op1=ALU.add))

            def ffn(name, groups, act_base, loops):
                base = in_loop[name]

                def body(it):
                    for g in range(groups):
                        for c in range(2):
                            b = 4 + 2 * (g % 2) + c
                            k = 2 * g + c + 1
                            eng.wait_ge(s["ffn_silu"], act_base + k + 2 * groups * it)
                            h1, h3 = silu_sb[:, g % 2, c, :], ps[:, b, T:2 * T]
                            if name == "moe":
                                link_at = order[0] + k + 2 * groups * it
                                eng.tensor_tensor(h1, h1, gates_bc[:, bass.ds(it, 1), :].squeeze(1)
                                                  if not isinstance(it, int) else gates_bc[:, it, :], ALU.mult)\
                                    .then_inc(s["dve_order"], 1)
                                eng.wait_ge(s["dve_order"], link_at)
                            eng.tensor_tensor(act_sb[:, g % 2, c, :], h1, h3, ALU.mult).then_inc(s["ffn_act"], 1)

                if loops == 1:
                    body(0)
                else:
                    with eng.Fori(0, loops) as it:
                        body(it)
                    order[0] += 2 * groups * loops
                for b in range(4):
                    o = tile(eng, name, "y", b)
                    r = res[:, 2 * b:2 * b + 2, :]
                    eng.tensor_tensor(r, o.rearrange("p (a b) -> p a b", b=T), r, ALU.add)\
                        .then_inc(s["res_added"], 1)
                eng.wait_ge(s["res_added"], 8 if name == "moe" else 4)
                eng.sem_inc(s["norm_src"], 1)

            def prepare_block2():
                link(eng.memset(mv[:, :, :, M_DH:M_DH + 1], 1.0))

            def zero_margins():
                eng.memset(pre[:, :, :, 0:PAD2], 0.0)
                eng.memset(pre[:, :, :, PAD2 + T:SEG2], 0.0).then_inc(s["pad_zeroed"], 1)

            def coefficients(l):
                g = par[:, PC.all(f"norm_g{l}")].unsqueeze(2).broadcast_to([P, KC, 2])
                eng.wait_ge(s["mod_out"], l + 1)
                link(eng.tensor_scalar(coef, mod[:, l, KC:2 * KC, :], 1.0, None, ALU.add))
                link(eng.tensor_tensor(coef, coef, g, ALU.mult))

            def modulate(l):
                def f(c, a):
                    for e in range(2):
                        v = a[:, c, e * T:(e + 1) * T]
                        ins = eng.tensor_scalar(v, v, coef[:, c, e:e + 1], mod[:, l, c, e:e + 1], ALU.mult, ALU.add)
                    return ins
                return f

            def gates2(l):
                for t in range(4):
                    o = tile(eng, "vg", l, t)
                    eng.tensor_copy(vtok[:, t, :], o[:, 0:P])
                    gb = PC(f"gate_b{l}", 0, 8), PC(f"gate_b{l}", 8, 8)
                    eng.tensor_tensor(gi[:, t, :], o[:, P:P + 8], par[:, gb[0]], ALU.add)
                    eng.tensor_tensor(gf[:, t, :], o[:, P + 8:P + 16], par[:, gb[1]], ALU.add).then_inc(s["vg_out"], 1)
                eng.wait_ge(s["vg_out"], 4 * (l + 1))
                eng.scalar_tensor_tensor(out=labs, in0=gf, scalar=-1.0, in1=gf, op0=ALU.mult, op1=ALU.max)\
                    .then_inc(s["lf_abs"], 1)

            def conv2(l):
                for c2 in range(0, 2 * M_HEADS, 2):
                    sg = 1 if l == 1 and c2 < M_HEADS else 2
                    eng.wait_ge(s["pre_copied"], 8 * l + c2 + 2)
                    for tap in range(CONV_K2):
                        for c in (c2, c2 + 1):
                            w = par[:, PC(f"conv_w2{l}", c * CONV_K2 + tap)]
                            src = pre[:, c, 0:sg, tap:tap + T]
                            acc = cqk[:, c, 0:sg * T].rearrange("p (a b) -> p a b", b=T)
                            if tap == 0:
                                ins = eng.tensor_scalar(acc, src, w, None, ALU.mult)
                            else:
                                eng.wait_ge(s["dve_order"], order[0] - 1)
                                ins = eng.scalar_tensor_tensor(out=acc, in0=src, scalar=w, in1=acc,
                                                               op0=ALU.mult, op1=ALU.add)
                            if tap == CONV_K2 - 1:
                                ins.then_inc(s["conv2_acc"], 1)
                                if c == c2:
                                    eng.wait_ge(s["dve_order"], order[0])
                            else:
                                ins.then_inc(s["dve_order"], 1)
                                order[0] += 1

            def rope(l):
                for c in range(CC + 1):
                    o = tile(eng, "rope", l, c)
                    v = aq[:, c, 0:T] if c < CC else ak[:, 0:T]
                    link(eng.tensor_tensor(rope_t, o[:, 0:T], con[:, CN.all("sin")], ALU.mult))
                    link(eng.tensor_tensor(v, v, con[:, CN.all("cos")], ALU.mult))
                    eng.tensor_tensor(v, v, rope_t, ALU.add).then_inc(s["rope_out"], 1)
                    eng.wait_ge(s["rope_out"], 5 * l + c + 1)

            def mlstm(l):
                SC = M_DH ** -0.5
                eng.wait_ge(s["lf_ln"], 2 * (l + 1))
                eng.scalar_tensor_tensor(out=lf, in0=gf, scalar=0.0, in1=labs, op0=ALU.min, op1=ALU.subtract)\
                    .then_inc(s["lf_out"], 1)
                eng.memset(m_run, NEG)
                eng.memset(state, 0.0).then_inc(s["state_out"], 1)
                o = tile(eng, "cum", l)
                for d in range(2):
                    b = o[:, 16 * d:16 * d + 16].rearrange("p (a b) -> p a b", b=4)
                    eng.tensor_copy(cs_b[:, :, 4 * d:4 * d + 4], b)
                eng.tensor_copy(cs_t, o[:, 32:64].rearrange("p (a b) -> p a b", b=8)).then_inc(s["cum_out"], 1)
                eng.wait_ge(s["cum_out"], l + 1)
                eng.wait_ge(s["state_out"], 9 * l + 1)
                link(eng.tensor_tensor(cum_a, gi, cs_b, ALU.subtract))
                for j in range(4):
                    k = step_no(l, j)
                    ts = [ORDER[d][j] for d in range(2)]
                    for d in range(2):
                        n = slice(4 * d, 4 * d + 4)
                        ins = eng.tensor_tensor(adiag[:, n, :], rows(ident, 4),
                                                cum_a[:, ts[d], n].unsqueeze(2).broadcast_to([P, 4, P]), ALU.mult)
                    ins.then_inc(s["adiag_out"], 1)
                    tile(eng, "arow", l, j, 0)
                    tile(eng, "arow", l, j, 1)
                    arow = ps[:, 6:8, :].rearrange("p a (b c) -> p (a b) c", c=P)
                    eng.tensor_reduce(a_max, arow, AX.X, ALU.max).then_inc(s["dve_order"], 1)
                    order[0] += 1
                    for d in range(2):
                        n = slice(4 * d, 4 * d + 4)
                        ins = eng.tensor_tensor(amask[:, n, :], arow[:, n, :],
                                                rows(con[:, CN.all("mask_b" if d else "mask_f")], 4), ALU.add)
                    ins.then_inc(s["decay_masked"], 1)
                    eng.wait_ge(s["decay_masked"], k)
                    eng.wait_ge(s["dve_order"], order[0])
                    link(eng.tensor_reduce(c_max, amask, AX.X, ALU.max))
                    link(eng.tensor_tensor(m_row, m_run, c_max, ALU.max))
                    link(eng.tensor_tensor(m_end, m_run, a_max, ALU.max))
                    eng.tensor_tensor(ex[:, 0, :], m_run, m_row, ALU.subtract)
                    link(eng.tensor_tensor(ex[:, 1, :], m_run, m_end, ALU.subtract))
                    for d in range(2):
                        n = slice(4 * d, 4 * d + 4)
                        eng.tensor_tensor(ex[:, 2, n], cum_a[:, ts[d], n], m_end[:, n], ALU.subtract)
                        eng.scalar_tensor_tensor(out=ex[:, 3, n], in0=cs_b[:, ts[d], n], scalar=-1.0,
                                                 in1=m_row[:, n], op0=ALU.mult, op1=ALU.subtract)
                        link(eng.tensor_tensor(m_run[:, n], cs_t[:, ts[d], n], m_end[:, n], ALU.add))
                    eng.tensor_scalar(nm_row, m_row, -1.0, None, ALU.mult).then_inc(s["stats_out"], 1)
                    eng.wait_ge(s["stats_exp"], k)
                    for d in range(2):
                        g = 2 * (k - 1) + d + 1
                        t = ts[d]
                        used = l == 0 or t < TT
                        if used:
                            o = tile(eng, "sc", l, j, d)
                            eng.wait_ge(s["decay_out"], g)
                            eng.scalar_tensor_tensor(out=wqk.rearrange("p a b -> p (a b)"), in0=o, scalar=SC,
                                                     in1=decay[:, 4 * d:4 * d + 4, :].rearrange("p a b -> p (a b)"),
                                                     op0=ALU.mult, op1=ALU.mult).then_inc(s["qk_weighted"], 1)
                        else:
                            eng.wait_ge(s["decay_out"], g)
                            eng.sem_inc(s["qk_weighted"], 1)
                        o = tile(eng, "kt", l, j, d)
                        for h in range(M_HEADS):
                            ins = eng.tensor_scalar(kw[:, h, :], o[:, h * P:h * P + P], wt[:, 2, 4 * d + h:4 * d + h + 1],
                                                    SC, ALU.mult, ALU.mult)
                        ins.then_inc(s["keys_weighted"], 1)
                        if used:
                            for half in range(2):
                                tile(eng, "inter", l, j, d, half)
                        for half in range(2):
                            o = tile(eng, "ds", l, j, d, half)
                            for h in range(2):
                                n = 4 * d + 2 * half + h
                                ins = eng.scalar_tensor_tensor(out=state[:, n, :], in0=state[:, n, :],
                                                               scalar=wt[:, 1, n:n + 1],
                                                               in1=o[:, h * 129:h * 129 + 129],
                                                               op0=ALU.mult, op1=ALU.add)
                        ins.then_inc(s["state_out"], 1)
                        if not used:
                            eng.sem_inc(s["mh_out"], 1)
                            continue
                        tile(eng, "intra", l, j, d, 0)
                        tile(eng, "intra", l, j, d, 1)
                        eng.wait_ge(s["inter_scaled"], g)
                        link(eng.tensor_tensor(num.rearrange("p (a b) c -> p a (b c)", b=2), ps[:, 6:8, 0:258],
                                               inter_s.rearrange("p (a b) c -> p a (b c)", b=2), ALU.add))
                        last_col = num[:, :, M_DH]
                        link(eng.scalar_tensor_tensor(out=den, in0=last_col, scalar=-1.0, in1=last_col,
                                                      op0=ALU.mult, op1=ALU.max))
                        link(eng.tensor_tensor(den, den, wt[:, 3, 4 * d:4 * d + 4], ALU.max))
                        link(eng.reciprocal(den, den))
                        inv = den.unsqueeze(2).broadcast_to([P, M_HEADS, M_DH])
                        to = hs[:, t, :].rearrange("p (a b) -> p a b", b=M_DH)
                        if j % 2 == 0:
                            eng.tensor_tensor(to, num[:, :, 0:M_DH], inv, ALU.mult).then_inc(s["mh_out"], 1)
                        else:
                            link(eng.tensor_tensor(num[:, :, 0:M_DH], num[:, :, 0:M_DH], inv, ALU.mult))
                            eng.tensor_tensor(to, to, num[:, :, 0:M_DH], ALU.add).then_inc(s["mh_out"], 1)
                        eng.wait_ge(s["mh_out"], g)

            def mlstm_post(l):
                tiles = 4 if l == 0 else 2
                n = tiles * M_HEADS
                h2 = hs[:, 0:tiles, :].rearrange("p a b -> p (a b)")
                o2 = mos[:, 0:tiles, :].rearrange("p a b -> p (a b)")
                h3 = hs[:, 0:tiles, :].rearrange("p a (b c) -> p (a b) c", c=M_DH)
                o3 = mos[:, 0:tiles, :].rearrange("p a (b c) -> p (a b) c", c=M_DH)
                eng.wait_ge(s["mos_out"], 8 if l == 0 else 12)
                link(eng.tensor_tensor(h2, h2, o2, ALU.mult))
                link(eng.tensor_tensor(o2, h2, h2, ALU.mult))
                eng.tensor_reduce(rms_s[:, 0:n], o3, AX.X, ALU.add).then_inc(s["mh_sumsq"], 1)
                eng.wait_ge(s["mh_std"], l + 1)
                link(eng.reciprocal(rms_i[:, 0:n], rms_i[:, 0:n]))
                eng.tensor_tensor(h3, h3, rms_i[:, 0:n].unsqueeze(2).broadcast_to([P, n, M_DH]), ALU.mult)\
                    .then_inc(s["mh_normed"], 1)
                eng.wait_ge(s["mzs_out"], 4 * (l + 1))
                for t in range(tiles):
                    o = tile(eng, "mt", l, t)
                    for h in range(M_HEADS):
                        ins = eng.scalar_tensor_tensor(out=mix2[:, CC + h, t * P:t * P + P], in0=o[:, h * P:h * P + P],
                                                       scalar=par[:, PC(f"head_g{l}", h)],
                                                       in1=mzs[:, h, t * P:t * P + P], op0=ALU.mult, op1=ALU.mult)
                    ins.then_inc(s["mh_mixed"], 1)

            def block2_attention(l):
                items = att_items(l)
                last_qt = 3 if l == 0 else 1
                w_out = 2 * T if l == 0 else T
                eng.wait_ge(s["azs_out"], 4 * (l + 1))
                for n in range(len(items) + 3):
                    if n < len(items):
                        _, i, half, qt = items[n]
                        k = ATT[items[n]]
                        h = i + CC * half
                        w = 2 * T if qt < TT else T
                        o = tile(eng, "as", *items[n])
                        pr = prob2[:, k % 2, 0:w]
                        if qt < TT:
                            eng.tensor_tensor(pr, o, con[:, CN("win_mask", qt * 2 * T, 2 * T)], ALU.add)\
                                .then_inc(s["att_scored"], 1)
                        else:
                            eng.tensor_copy(pr, o[:, 0:T]).then_inc(s["att_scored"], 1)
                        eng.wait_ge(s["att_scored"], k)
                        link(eng.tensor_reduce(rmax[:, k % 2, 0:1], pr, AX.X, ALU.max, negate=True))
                        eng.tensor_tensor(rmax[:, k % 2, 0:1], rmax[:, k % 2, 0:1], nsink[:, l, h:h + 1], ALU.min)\
                            .then_inc(s["att_max"], 1)
                    if 1 <= n <= len(items):
                        k = ATT[items[n - 1]]
                        w = 2 * T if items[n - 1][3] < TT else T
                        eng.wait_ge(s["att_exp"], k)
                        link(eng.tensor_tensor(rsum[:, k % 2, 0:1], rsum[:, k % 2, 0:1], esink[:, k % 2, :], ALU.add))
                        link(eng.reciprocal(rinv[:, k % 2, 0:1], rsum[:, k % 2, 0:1]))
                        pr = prob2[:, k % 2, 0:w]
                        eng.tensor_scalar(pr, pr, rinv[:, k % 2, 0:1], None, ALU.mult).then_inc(s["att_prob"], 1)
                    if n >= 3 and items[n - 3][2] == 1 and items[n - 3][3] == last_qt:
                        i = items[n - 3][1]
                        o = tile(eng, "ao", l, i)
                        eng.tensor_tensor(mix2[:, i, 0:w_out], o[:, 0:w_out], azs[:, i, 0:w_out], ALU.mult)\
                            .then_inc(s["att_out"], 1)

            def block2_out(l):
                for c in range(KC):
                    o = tile(eng, "xo", l, c)
                    for e in range(2 if l == 0 else 1):
                        v = xc[:, c, e * T:(e + 1) * T]
                        ins = eng.scalar_tensor_tensor(out=v, in0=o[:, e * T:(e + 1) * T],
                                                       scalar=mod[:, l, 2 * KC + c, e:e + 1], in1=v,
                                                       op0=ALU.mult, op1=ALU.add)
                    ins.then_inc(s["x_added"], 1)
                eng.wait_ge(s["x_added"], KC * (l + 1))
                eng.sem_inc(s["norm_src"], 1)

            eng.wait_ge(s["inputs_loaded"], 16 * N_INPUTS)
            for l in range(DEPTH):
                eng.tensor_scalar(bq_s[:, l, :], par[:, PC.all(f"b_q{l}")], DH ** -0.5, None, ALU.mult)
                eng.tensor_scalar(nsink[:, l, :], par[:, PC.all(f"sink{l}")], -1.0, None, ALU.mult)
            eng.memset(glu[:, :, 0:PAD1], 0.0)
            eng.memset(glu[:, :, PAD1 + T:], 0.0).then_inc(s["prep_done"], 1)
            eng.wait_ge(s["prep_done"], 1)
            norm("in", xc, KC, T, layer_gain("ln_in_g", "ln_in_b", xc))
            for l in range(DEPTH):
                block1_projection(l)
                conv(l)
                values(l)
                conditions(l)
                norm(f"conv{l}", conv_acc, CC, T, None)
                block1_attention(l)
                block1_out(l)
                norm(f"ln1_{l}", res, KC, T, layer_gain(f"ln1_g{l}", f"ln1_b{l}", xc))
                if l == 1:
                    routing()
                    places()
                ple_products(l)
                if l == 1:
                    moe()
                else:
                    ffn("dense", GROUPS_DENSE, 0, 1)
                norm(f"ln2_{l}", res, KC, T, layer_gain(f"ln2_g{l}", f"ln2_b{l}", xc))
            eng.wait_ge(s["norm_out"], outk("ln2_1"))
            eng.sem_inc(s["norm_src"], 1)
            prepare_block2()
            for l in range(DEPTH):
                coefficients(l)
                zero_margins()
                norm(f"rms{l}", xc, KC, 2 * T, modulate(l), centred=False)
                gates2(l)
                conv2(l)
                rope(l)
                mlstm(l)
                mlstm_post(l)
                block2_attention(l)
                block2_out(l)
            norm("final", xc, KC, T,
                 lambda c, a: eng.tensor_scalar(cen[:, c, :], cen[:, c, :], par[:, PC("final_g", c)], None, ALU.mult),
                 centred=False, dst=cen)


def weight_units(a):
    units = np.zeros((UNITS, P, UC), np.float32)
    n = [0]

    def put(block, slices):
        k, cols = block.shape
        units[n[0]].reshape(P, k // P, UC * P // k)[:, :, 0:cols] = block.reshape(k // P, P, cols).transpose(1, 0, 2)
        n[0] += 1

    def columns(w, ranges):
        put(np.concatenate([w[:, r[0]:r[1]] for r in ranges], axis=1), None)

    def whole(w):
        for c in range(0, w.shape[1], GW):
            columns(w, [(c, c + GW)])

    def ffn(w1, w3, w2):
        groups = w1.shape[1] // GW
        for g in range(groups + 1):
            if g < groups:
                columns(w1, [(g * GW, (g + 1) * GW)])
                columns(w3, [(g * GW, (g + 1) * GW)])
            if g:
                put(w2[(g - 1) * GW:g * GW], None)

    for l in range(DEPTH):
        w = a["w_in"][l]
        for j in range(CC):
            columns(w, [(j * P, j * P + P), (CONV_CH + j * P, CONV_CH + j * P + P)])
        q0 = 2 * CONV_CH
        for j in range(CC):
            columns(w, [(q0 + j * P, q0 + j * P + P), (q0 + 512 + j * P, q0 + 512 + j * P + P)])
        for j in range(2):
            columns(w, [(q0 + 1024 + j * GW, q0 + 1024 + (j + 1) * GW)])
        whole(a["w_ada_2"][l])
        whole(a["w_out"][l])
        put(a["ple_w"][l], None)
        whole(a["ple_gate_w"][l])
        if l == 0:
            ffn(a["ffn_w1"][0], a["ffn_w3"][0], a["ffn_w2"][0])
        else:
            for e in range(EXPERTS):
                ffn(a["moe_w1"][0, e], a["moe_w3"][0, e], a["moe_w2"][0, e])
    A = 512
    at = dict(aq=0, ak=A, av=A + 128, az=A + 256, mq=2 * A + 256, mk=3 * A + 256, mv=4 * A + 256, mo=5 * A + 256,
              mz=6 * A + 256, mi=7 * A + 256, mf=7 * A + 264)

    def pairs(base, i):
        return [(base + i * DH, base + i * DH + DH), (base + (i + 4) * DH, base + (i + 4) * DH + DH)]

    for l in range(DEPTH):
        w = a["w_in_2"][l]
        seen = {}
        for name in UNITS_IN2:
            u = seen.get(name, 0)
            seen[name] = u + 1
            if name == "vg":
                columns(w, [(at["av"], at["av"] + P), (at["mi"], at["mi"] + 16)])
            elif name == "ak":
                columns(w, [(at["ak"], at["ak"] + P)])
            elif name in ("aq", "az"):
                columns(w, pairs(at[name], 2 * u) + pairs(at[name], 2 * u + 1))
            else:
                columns(w, [(at[name] + u * GW, at[name] + (u + 1) * GW)])
        wo = a["w_out_2"][l]
        rows = [wo[r[0]:r[1]] for i in range(CC) for r in pairs(0, i)] + [wo[A:]]
        whole(np.concatenate(rows, axis=0))
    assert n[0] == UNITS
    return units


def param_tile(a):
    t = np.zeros((P, PC.n), np.float32)

    def col(name, v):
        t[:, PC.all(name)] = v.reshape(-1, P).T

    def row(name, v):
        t[:, PC.all(name)] = v.reshape(1, -1)

    col("ln_in_g", a["ln_in_g"]), col("ln_in_b", a["ln_in_b"])
    for l in range(DEPTH):
        b = a["b_in"][l]
        for i, name in enumerate(("b_a", "b_g", "b_q", "b_k")):
            col(f"{name}{l}", b[i * 512:(i + 1) * 512])
        row(f"b_v{l}", b[2048:])
        t[:, PC.all(f"conv_w{l}")] = a["conv_w"][l].reshape(CONV_K, CC, P).transpose(2, 1, 0).reshape(P, -1)
        t[:, PC.all(f"conv_w2{l}")] = a["conv_w_2"][l].reshape(CONV_K2, 8, P).transpose(2, 1, 0).reshape(P, -1)
        for name in ("conv_b", "conv_ln_g", "conv_ln_b", "b_out", "ln1_g", "ln1_b", "ple_gate_b", "ln2_g", "ln2_b"):
            col(f"{name}{l}", a[name][l])
        col(f"b_ada{l}", a["b_ada_2"][l]), col(f"norm_g{l}", a["norm_g_2"][l])
        col(f"conv_b2{l}", a["conv_b_2"][l]), col(f"head_g{l}", a["head_g_2"][l])
        row(f"gate_b{l}", a["gate_b_2"][l]), row(f"sink{l}", a["sink_2"][l])
    t[:, PC.all("w_router")] = a["w_router"][0].reshape(KC, P, EXPERTS).transpose(1, 0, 2).reshape(P, -1)
    col("final_g", a["final_g_2"])
    t[:, PC.all("cond")] = np.stack([a["c_2"].reshape(-1), a["c_ctx_2"].reshape(-1)]).reshape(2, KC, P)\
        .transpose(2, 1, 0).reshape(P, -1)
    return t


def const_tile():
    t = np.zeros((P, CN.n), np.float32)
    i = np.arange(P)
    t[:, CN.all("ident")] = np.eye(P)
    t[:, CN.all("ones")] = 1
    t[:, CN.all("tri_f")] = i[:, None] <= i[None, :]
    t[:, CN.all("tri_b")] = i[:, None] >= i[None, :]
    t[:, CN.all("mask_f")] = np.where(i[None, :] <= i[:, None], 0, NEG)
    t[:, CN.all("mask_b")] = np.where(i[None, :] >= i[:, None], 0, NEG)
    rot = np.zeros((P, P), np.float32)
    for m in i:
        if m % 32 < 16:
            rot[m + 16, m] = -1
        else:
            rot[m - 16, m] = 1
    t[:, CN.all("rot")] = rot
    inv = np.float32(10000.0) ** (-np.arange(0, DH // 2, 2, dtype=np.float32) / np.float32(DH // 2))
    tok = np.arange(T)
    row, col = (tok // GRID_W).astype(np.float32), (tok % GRID_W).astype(np.float32)
    for m in i:
        ang = (row if m % DH < 32 else col) * inv[m % 16]
        t[m, CN.all("cos")], t[m, CN.all("sin")] = np.cos(ang), np.sin(ang)
    win = np.zeros((P, TT, 2 * T), np.float32)
    nbr = np.zeros((P, TT, T), np.float32)
    kc = np.arange(T) % GRID_W
    for qt in range(TT):
        q = qt * P + i
        win[:, qt, 0:T] = np.where(np.abs(q[:, None] - tok[None, :]) <= WINDOW, 0, NEG)
        w0 = np.clip(q % GRID_W - WIN_C // 2, 0, GRID_W - WIN_C)
        nbr[:, qt] = np.where((kc[None, :] >= w0[:, None]) & (kc[None, :] < w0[:, None] + WIN_C), 0, NEG)
    t[:, CN.all("win_mask")] = win.reshape(P, -1)
    t[:, CN.all("nbr_mask")] = nbr.reshape(P, -1)
    t[:, CN.all("slot")] = np.arange(CAP)[None, :]
    e = np.arange(EXPERTS)
    t[:, CN.all("before")] = (e[None, :] < e[:, None]).reshape(1, -1)
    t[:, CN.all("eps5")], t[:, CN.all("eps6")], t[:, CN.all("one")] = 1e-5, 1e-6, 1
    return t


def relative_rows(rpb):
    out = np.zeros((DEPTH, GRID_W, HEADS, 2 * ROWS - 1, GRID_W), np.float32)
    for c in range(GRID_W):
        lo, hi = max(0, c - 15), min(GRID_W, c + 16)
        out[:, c, :, :, lo:hi] = rpb[:, :, 4:4 + 2 * ROWS - 1, lo - c + 15:hi - c + 15]
    return out


def kernel(**inputs):
    import concourse.bacc as _bacc
    from concourse.bass_utils import run_bass_kernel_spmd as _run

    a = {k: np.asarray(v) for k, v in inputs.items()}

    def feature_major(v):
        return np.ascontiguousarray(v.T.reshape(-1, P, v.shape[0]).transpose(1, 0, 2))

    arrays = {
        "weights": weight_units(a),
        "params": param_tile(a),
        "consts": const_tile(),
        "x_t": feature_major(a["x"][0]),
        "ctx_t": feature_major(a["ctx_2"][0]),
        "p_t": np.ascontiguousarray(np.stack([feature_major(a["p"][l, 0]) for l in range(DEPTH)], axis=1)),
        "rel": relative_rows(a["rpb"]),
    }
    nc = _bacc.Bacc("TRN2", target_bir_lowering=False, num_devices=1)
    args = [nc.dram_tensor(n, v.shape, F32, kind="ExternalInput").ap() for n, v in arrays.items()]
    out = nc.dram_tensor("out", (P, KC, T), F32, kind="ExternalOutput").ap()
    build(nc, *args, out)
    r = _run(nc, [arrays], core_ids=[0])
    y = r.results[0]["out"]
    return np.ascontiguousarray(y.transpose(2, 1, 0).reshape(1, T, D))
```

```python
from contextlib import ExitStack

import numpy as np

import concourse.bass as bass
from concourse import mybir

F32 = mybir.dt.float32
ALU = mybir.AluOpType
ACT = mybir.ActivationFunctionType
AX = mybir.AxisListType

P = 128
T = 256
TT = T // P
D = 1024
KC = D // P
DEPTH = 2
CONV_CH = 512
CC = CONV_CH // P
CONV_K = 31
PAD1 = CONV_K // 2
HEADS = 8
DH = 64
GRID_W = 64
ROWS = T // GRID_W
WIN_C = 16
D_FF = 2816
EXPERTS = 8
TOP_K = 2
D_FFE = 3584
D_PLE = 256
ALPHA = (2.0 * DEPTH) ** 0.25
M_HEADS = 4
M_DH = 128
CONV_K2 = 5
PAD2 = CONV_K2 // 2
SEG2 = T + 2 * PAD2
WINDOW = 128
NEG = -1e30

UC = 2048
GW = UC // KC
SLOTS = 6
GROUPS_DENSE = D_FF // GW
GROUPS_EXPERT = D_FFE // GW
UNITS_IN = 10
UNITS_ADA = 3 * D // GW
UNITS_OUT = D // GW
UNITS_IN2 = ["mq", "mq", "mk", "mk", "vg", "mv", "mv", "aq", "aq", "ak", "az", "az", "mz", "mz", "mo", "mo"]
UNITS_BEFORE_FFN = UNITS_IN + UNITS_ADA + UNITS_OUT + 1 + UNITS_OUT
MOE_START = 2 * UNITS_BEFORE_FFN + 3 * GROUPS_DENSE
MOE_UNITS = 3 * GROUPS_EXPERT
CAP = 96
UNITS = MOE_START + EXPERTS * MOE_UNITS + DEPTH * (len(UNITS_IN2) + UNITS_OUT)
assert MOE_UNITS % SLOTS == 0

NORMS = ["in", "conv0", "ln1_0", "ln2_0", "conv1", "ln1_1", "ln2_1", "rms0", "rms1", "final"]
OUTS = [n for n in NORMS if not n.startswith("conv")]


class Columns:

    def __init__(self):
        self.at, self.n = {}, 0

    def add(self, name, n):
        self.at[name] = (self.n, n)
        self.n += n

    def __call__(self, name, j=0, n=1):
        a = self.at[name][0] + j
        return slice(a, a + n)

    def all(self, name):
        a, n = self.at[name]
        return slice(a, a + n)


def param_columns():
    c = Columns()
    c.add("ln_in_g", KC), c.add("ln_in_b", KC)
    for l in range(DEPTH):
        for name, n in (("b_a", CC), ("b_g", CC), ("b_q", CC), ("b_k", CC), ("conv_w", CC * CONV_K),
                        ("conv_b", CC), ("conv_ln_g", CC), ("conv_ln_b", CC), ("b_out", KC), ("ln1_g", KC),
                        ("ln1_b", KC), ("ple_gate_b", KC), ("ln2_g", KC), ("ln2_b", KC), ("b_v", CONV_CH),
                        ("b_ada", 3 * KC), ("norm_g", KC), ("conv_w2", 2 * M_HEADS * CONV_K2),
                        ("conv_b2", 2 * M_HEADS), ("gate_b", 4 * M_HEADS), ("sink", HEADS), ("head_g", M_HEADS)):
            c.add(f"{name}{l}", n)
    c.add("w_router", KC * EXPERTS)
    c.add("final_g", KC)
    c.add("cond", KC * 2)
    return c


def const_columns():
    c = Columns()
    for name, n in (("ones", P), ("ident", P), ("zeros", P), ("tri_f", P), ("eps5", 1), ("eps6", 1), ("one", 1),
                    ("tri_b", P), ("mask_f", P), ("mask_b", P), ("rot", P), ("cos", T), ("sin", T), ("win_mask", TT * 2 * T), ("slot", CAP),
                    ("nbr_mask", TT * T), ("before", EXPERTS * EXPERTS)):
        c.add(name, n)
    c.early = c.at["eps5"][0] + 3
    return c


PC, CN = param_columns(), const_columns()


def build(nc, weights, params, consts, x_t, ctx_t, p_t, rel, out):
    with ExitStack() as ctx:
        def sb(name, shape):
            return ctx.enter_context(nc.sbuf_tensor(name, shape, F32))

        ring = sb("ring", [P, SLOTS, UC])
        par = sb("par", [P, PC.n])
        con = sb("con", [P, CN.n])
        xc = sb("xc", [P, KC, 2 * T])
        small = sb("small", [P, 640])
        crowded = ctx.enter_context(nc.sbuf_tensor("crowded", [P, EXPERTS], mybir.dt.int32))
        WORK = 31190
        work = sb("work", [P, WORK])
        ps = ctx.enter_context(nc.psum_tensor("ps", [P, 8, 512], F32))

        def carver(space, limit):
            at = [0]

            def carve(*shape):
                n = int(np.prod(shape))
                v = space[:, at[0]:at[0] + n]
                at[0] += n
                assert at[0] <= limit, at[0]
                names = "abcd"[:len(shape)]
                if len(shape) > 1:
                    v = v.rearrange(f"p ({' '.join(names)}) -> p {' '.join(names)}",
                                    **{k: s for k, s in zip(names[1:], shape[1:])})
                return v
            return carve

        cut = carver(small, 640)
        cond_s = cut(KC * 2)
        mod = cut(DEPTH, 3 * KC, 2)
        coef = cut(KC, 2)
        bq_s = cut(DEPTH, CC)
        nsink = cut(DEPTH, HEADS)
        rmax, rsum, rinv = cut(4, 2), cut(4, 2), cut(4, 2)
        esink = cut(4, 1)
        logits, gexp, gate = cut(TT, 8), cut(TT, 8), cut(TT, 8)
        gmax, gsum = cut(TT, 8), cut(TT, 1)
        rank_t = cut(TT, 8)
        gi, gf, lf, labs = cut(4, 8), cut(4, 8), cut(4, 8), cut(4, 8)

        cut = carver(work, WORK)
        cen, sq = cut(KC, T), cut(KC, T)
        res, mix1, ple = cut(KC, T), cut(KC, T), cut(KC, T)
        h_tok = cut(TT, D)
        glu, conv_acc = cut(CC, T + 2 * PAD1), cut(CC, T)
        q1, k1, v1 = cut(CC, T), cut(CC, T), cut(TT, CONV_CH)
        relb = cut(TT, HEADS, T)
        prob1, pt1 = cut(3, TT, T), cut(2, TT, T)
        p_sb = cut(DEPTH, 2, T)
        act_sb, silu_sb = cut(2, 2, T), cut(2, 2, T)
        cond_row = cut(2, T)
        std1, rstd1, sig_sb = cut(T), cut(T), cut(2, T)
        gcmp, geq = (act_sb[:, i, 0, 0:TT * 64].rearrange("p (a b) -> p a b", b=64) for i in range(2))

        cut = carver(relb.rearrange("p a b c -> p (a b c)"), TT * HEADS * T)
        sel, sel_g = cut(TT, CAP), cut(TT, CAP)
        sel_gt = cut(T)
        xg, y_sb = cut(KC, CAP), cut(D)
        moe_silu_sb, moe_act_sb = cut(2, 2, CAP), cut(2, 2, CAP)
        slot_of, gate_c = cut(TT, EXPERTS + 1), cut(TT, EXPERTS + 1)
        gate_diag, gate_row = cut(TT, P), cut(T)
        counts = cut(8)

        cut = carver(work, WORK)
        xn = cut(KC, 2 * T)
        mix2 = xn
        cqk = cut(2 * M_HEADS, 2 * T)
        sq2 = cqk
        aq, ak = cut(CC, 2 * T), cut(2 * T)
        azs, mzs = cut(CC, 2 * T), cut(M_HEADS, 2 * T)
        pre_at = 4096 * 2 + 2048 + 512 + 2048 * 2
        pre = cut(2 * M_HEADS, 2, SEG2)
        vtok = cut(4, P)
        mv = cut(4, M_HEADS, M_DH + 1)
        mos, hs = cut(4, M_HEADS * M_DH), cut(4, M_HEADS * M_DH)
        state = cut(2 * M_HEADS, M_DH + 1)
        wqk, wqk_t, kw = cut(M_HEADS, P), cut(M_HEADS, P), cut(M_HEADS, P)
        pt2 = cut(2, 2 * T)
        prob2 = mix2[:, CC:CC + 4, :]
        std2, rstd2 = pt2[:, 0, :], pt2[:, 1, :]
        rope_t = pt2[:, 0, 0:T]
        cs_b, cs_t, cum_a = cut(4, 8), cut(4, 8), cut(4, 8)
        m_run, m_end, m_row, nm_row, c_max, a_max = (cut(8) for _ in range(6))
        ex, wt = cut(4, 8), cut(4, 8)
        den, rms_s, rms_i = cut(M_HEADS), cut(4 * M_HEADS), cut(4 * M_HEADS)
        cut = carver(work[:, pre_at:pre_at + 8 * 2 * SEG2], 8 * 2 * SEG2)
        adiag, amask, decay = cut(8, P), cut(8, P), cut(8, P)
        num, inter_s = cut(M_HEADS, M_DH + 1), cut(M_HEADS, M_DH + 1)

        names = """weights_used inputs_loaded late_loaded rel_loaded rel_ready out_stored
            norm_src norm_centered norm_squared norm_std norm_scaled norm_out norm_out_a coef_out
            cond_ready cond_row prep_done glu_gate glu_out qk_out v_out mod_out conv_mixed
            nbr_scored nbr_max nbr_exp nbr_prob nbr_turned nbr_out
            mix_biased mix_added ple_copied ple_gate ple_out logits_out gate_exp chosen_out places_out
            crowded_out h_turned ffn_silu ffn_act res_added
            moe_sel moe_sel_g moe_gathered moe_xg_a moe_xg_d moe_h moe_silu moe_act moe_y moe_y_a moe_y_d
            moe_scattered moe_added moe_turned moe_gates_turned moe_weighted
            pre_copied vg_out mv_copied aqk_copied azs_out mzs_out mos_out conv2_acc cqk_out rope_out
            lf_abs lf_ln lf_out cum_out adiag_out decay_masked stats_out stats_exp decay_out
            qk_weighted qk_turned keys_weighted inter_scaled state_out mh_out
            mh_sumsq mh_std mh_normed mh_mixed
            att_scored att_max att_exp att_prob att_turned att_out x_added
            pad_zeroed dve_order""".split()
        s = {n: ctx.enter_context(nc.semaphore(n)) for n in names}
        weights_in = [ctx.enter_context(nc.semaphore(f"weights_in{i}")) for i in range(SLOTS)]
        bank_full = [ctx.enter_context(nc.semaphore(f"bank_full{i}")) for i in range(8)]
        block = ctx.enter_context(nc.Block())

        N_INPUTS, N_LATE = 3, 3
        placed = {}
        before_ffn = []
        ident, ones, zeros = con[:, CN.all("ident")], con[:, CN.all("ones")], con[:, CN.all("zeros")]

        def normk(name):
            return NORMS.index(name) + 1

        def chunks_of(name):
            return CC if name.startswith("conv") else KC

        def before(name):
            return sum(chunks_of(n) for n in NORMS[:NORMS.index(name)])

        def outk(name, chunk=KC - 1):
            return OUTS.index(name) * KC + chunk + 1

        def source(name, c):
            if name.startswith("ln1"):
                return s["mix_added"], KC * int(name[-1]) + c + 1
            if name == "rms0":
                return s["norm_out"], outk("ln2_1", c)
            if name in ("rms1", "final"):
                return s["x_added"], KC * (name == "final") + c + 1
            return s["norm_src"], 1 + ["conv0", "ln2_0", "conv1", "ln2_1"].index(name)

        def att_items(l):
            return [(l, i, half, qt) for i in range(CC) for half in range(2) for qt in range(4 if l == 0 else 2)]

        ATT_LAG = 5
        ATT = {it: n + 1 for n, it in enumerate(att_items(0) + att_items(1))}

        YIELDS = 4 * (3 + 2 * 6)

        def interleave(l, mlstm, attention):
            rounds = len(att_items(l)) + ATT_LAG
            for i, _ in enumerate(mlstm):
                for _ in range((i + 1) * rounds // YIELDS - i * rounds // YIELDS):
                    next(attention)
            assert i + 1 == YIELDS
            assert next(attention, "ended") == "ended"

        ORDER = ([2, 3, 0, 1], [3, 2, 1, 0])

        def step_no(l, j):
            return 4 * l + j + 1

        @block.tensor
        def _(eng):
            count = [0] * 8
            readers = [None] * 8
            unit_no = [0]
            release = [False]

            def fill(key, bank, read_by):
                if readers[bank] is not None:
                    eng.wait_ge(*readers[bank])
                count[bank] += 1
                placed[key] = (bank, count[bank])
                readers[bank] = read_by
                return ps[:, bank, :]

            def next_unit(it=0):
                n = unit_no[0]
                unit_no[0] += 1
                slot = n % SLOTS
                eng.wait_ge(weights_in[slot], 16 * (n // SLOTS + 1) + 16 * (MOE_UNITS // SLOTS) * it)
                release[0] = n > 0
                return ring[:, slot, :]

            def mm(o, lhs, rhs, start, stop, **kw):
                ins = eng.matmul(o, lhs, rhs, start=start, stop=stop, **kw)
                if release[0]:
                    ins.then_inc(s["weights_used"], 1)
                    release[0] = False
                return ins

            def norm(name, src, chunks, n, centred=True, bank=0):
                k, base = normk(name), before(name)
                if centred:
                    o = fill(("mean", name), bank, (s["norm_centered"], base + chunks))
                    for c in range(chunks):
                        if k > 1:
                            eng.wait_ge(*source(name, c))
                        last = mm(o[:, 0:n], ones, src[:, c, 0:n], c == 0, c == chunks - 1)
                    last.then_inc(bank_full[bank], 1)
                o = fill(("var", name), bank + 1, (s["norm_std"], k))
                b = sq if centred else sq2
                for c in range(chunks):
                    eng.wait_ge(s["norm_squared"], base + c + 1)
                    last = mm(o[:, 0:n], ones, b[:, c, 0:n], c == 0, c == chunks - 1)
                last.then_inc(bank_full[bank + 1], 1)

            fresh = [None]

            def chunk_ready(c):
                if fresh[0] is not None:
                    eng.wait_ge(s["norm_out"], outk(fresh[0], c))
                    if fresh[0].startswith("rms"):
                        eng.wait_ge(s["norm_out_a"], KC * int(fresh[0][-1]) + c + 1)
                    if c == KC - 1:
                        fresh[0] = None

            def features(w, col, o, src, n, kc=KC, wide=GW):
                for c in range(kc):
                    if kc == KC:
                        chunk_ready(c)
                    last = mm(o, w[:, c * wide + col:c * wide + col + P], src[:, c, 0:n], c == 0, c == kc - 1)
                return last

            def tokens(w, cols, o, src, tile):
                for c in range(KC):
                    last = mm(o, src[:, c, tile * P:tile * P + P], w[:, c * GW:c * GW + cols],
                              c == 0, c == KC - 1)
                return last

            def block1_projection(l):
                fresh[0] = "in" if l == 0 else "ln2_0"
                for j in range(CC):
                    w = next_unit()
                    o = fill(("glu", l, j), j % 4, (s["glu_out"], CC * l + j + 1))
                    features(w, 0, o[:, 0:T], xc, T)
                    features(w, P, o[:, T:2 * T], xc, T).then_inc(bank_full[j % 4], 1)
                for j in range(CC):
                    w = next_unit()
                    o = fill(("qk", l, j), 4 + j % 4, (s["qk_out"], CC * l + j + 1))
                    features(w, 0, o[:, 0:T], xc, T)
                    features(w, P, o[:, T:2 * T], xc, T).then_inc(bank_full[4 + j % 4], 1)
                for j in range(2):
                    w = next_unit()
                    o = fill(("v", l, j), 4 + j, (s["v_out"], 2 * l + j + 1))
                    tokens(w, GW, o[:, 0:T], xc, 0)
                    tokens(w, GW, o[:, T:2 * T], xc, 1).then_inc(bank_full[4 + j], 1)

            def conditions(l):
                eng.wait_ge(s["cond_ready"], 1)
                mod_t = fill(("mod", l), 0, (s["mod_out"], l + 1))
                cond = cond_s.rearrange("p (c e) -> p c e", e=2)
                for u in range(UNITS_ADA + 1):
                    if u < UNITS_ADA:
                        w = next_unit()
                        o = fill(("row", l, u), 1, (s["cond_row"], UNITS_ADA * l + u + 1))
                        for c in range(KC):
                            last = mm(o[0:2, 0:GW], cond[:, c, :], w[:, c * GW:(c + 1) * GW], c == 0, c == KC - 1)
                        last.then_inc(bank_full[1], 1)
                    if u >= 1:
                        eng.wait_ge(s["cond_row"], UNITS_ADA * l + u)
                        for half in range(2):
                            at = 2 * (2 * (u - 1) + half)
                            last = eng.transpose(mod_t[:, at:at + 2], cond_row[0:2, (u - 1) % 2, half * P:half * P + P],
                                                 ident[0:2, 0:2])
                    if u == UNITS_ADA:
                        last.then_inc(bank_full[0], 1)
                    yield

            def block1_attention(l, filler):
                eng.wait_ge(s["qk_out"], CC * (l + 1))
                eng.wait_ge(s["v_out"], 2 * (l + 1))
                for i in range(HEADS + 3):
                    next(filler, None)
                    if i < HEADS:
                        b, p0 = 2 + i % 2, DH * (i % 2)
                        o = fill(("s", l, i), b, (s["nbr_scored"], HEADS * l + i + 1))
                        for t in range(TT):
                            last = mm(o[:, t * T:(t + 1) * T], q1[p0:p0 + DH, i // 2, t * P:t * P + P],
                                      k1[p0:p0 + DH, i // 2, :], True, True)
                        last.then_inc(bank_full[b], 1)
                    if 2 <= i < HEADS + 2:
                        h = i - 2
                        b = 4 + h % 2
                        eng.wait_ge(s["nbr_prob"], HEADS * l + h + 1)
                        o = fill(("pt", l, h), b, (s["nbr_turned"], HEADS * l + h + 1))
                        for t in range(TT):
                            for kt in range(TT):
                                last = eng.transpose(o[:, kt * T + t * P:kt * T + t * P + P],
                                                     prob1[:, h % 3, t, kt * P:kt * P + P], ident)
                        last.then_inc(bank_full[b], 1)
                    if i >= 3:
                        h = i - 3
                        eng.wait_ge(s["nbr_turned"], HEADS * l + h + 1)
                        if h % 2 == 0:
                            o2 = fill(("o", l, h // 2), 6 + (h // 2) % 2, (s["nbr_out"], CC * l + h // 2 + 1))
                        for kt in range(TT):
                            last = mm(o2[DH * (h % 2):DH * (h % 2) + DH, 0:T],
                                      v1[:, kt, h * DH:h * DH + DH], pt1[:, h % 2, kt, :], kt == 0, kt == TT - 1)
                        if h % 2 == 1:
                            last.then_inc(bank_full[6 + (h // 2) % 2], 1)

            def block1_out(l):
                eng.wait_ge(s["conv_mixed"], CC * (l + 1))
                eng.wait_ge(s["nbr_out"], CC * (l + 1))
                for c in range(KC):
                    if c % 2 == 0:
                        w = next_unit()
                    b = 2 + c % 4
                    o = fill(("mix", l, c), b, (s["mix_biased"], KC * l + c + 1))
                    features(w, (c % 2) * P, o[:, 0:T], mix1, T).then_inc(bank_full[b], 1)

            def ple_products(l):
                eng.wait_ge(s["late_loaded"], 16 * N_LATE)
                w = next_unit()
                for c in range(KC):
                    if c % 2 == 0:
                        o = fill(("ple", l, c // 2), 2 + c // 2, (s["ple_copied"], 4 * l + c // 2 + 1))
                    last = features(w, c * P, o[:, (c % 2) * T:(c % 2) * T + T], p_sb[:, l], T, kc=2, wide=D)
                    if c % 2:
                        last.then_inc(bank_full[2 + c // 2], 1)
                if l == 0:
                    fresh[0] = "ln1_0"
                for c in range(KC):
                    if c % 2 == 0:
                        w = next_unit()
                    b = 4 + c % 4
                    o = fill(("pgate", l, c), b, (s["ple_gate"], KC * l + c + 1))
                    features(w, (c % 2) * P, o[:, 0:T], xc, T).then_inc(bank_full[b], 1)

            def router():
                o = fill(("logits",), 0, (s["logits_out"], 1))
                for t in range(TT):
                    for c in range(KC):
                        last = mm(o[:, t * 8:t * 8 + 8], xc[:, c, t * P:t * P + P],
                                  par[:, PC("w_router", c * EXPERTS, EXPERTS)], c == 0, c == KC - 1)
                last.then_inc(bank_full[0], 1)

            def places():
                eng.wait_ge(s["chosen_out"], 1)
                o = fill(("places",), 0, (s["places_out"], 1))
                mm(o[:, 0:8], con[:, CN.all("tri_f")], rank_t[:, 0, :], True, True)
                mm(o[:, 8:16], con[:, CN.all("tri_f")], rank_t[:, 1, :], True, False)
                mm(o[:, 8:16], ones, rank_t[:, 0, :], False, True)
                mm(o[:, 16:24], ones, rank_t[:, 0, :], True, False)
                mm(o[:, 16:24], ones, rank_t[:, 1, :], False, True).then_inc(bank_full[0], 1)

            def turn_tokens():
                for t in range(TT):
                    for half in range(2):
                        b = 2 * t + half
                        o = fill(("htok", t, half), b, (s["h_turned"], b + 1))
                        for c in range(4):
                            last = eng.transpose(o[:, c * P:c * P + P], xc[:, 4 * half + c, t * P:t * P + P], ident)
                        last.then_inc(bank_full[b], 1)

            def moe():
                G = GROUPS_EXPERT
                for r in readers:
                    if r is not None:
                        eng.wait_ge(*r)
                eng.wait_ge(s["h_turned"], 4)
                ubase = unit_no[0]

                def gather(nxt):
                    eng.wait_ge(s["moe_sel"], nxt + 1)
                    for half in range(2):
                        for c in range(4):
                            for t in range(TT):
                                f = 4 * half + c
                                last = mm(ps[:, half, c * CAP:(c + 1) * CAP], h_tok[:, t, f * P:f * P + P],
                                          sel[:, t, :], t == 0, t == TT - 1)
                        last.then_inc(s["moe_gathered"], 1)

                def turn(nxt):
                    eng.wait_ge(s["moe_sel_g"], nxt + 1)
                    for t in range(TT):
                        eng.transpose(ps[0:CAP, 7, t * P:t * P + P], sel_g[:, t, :], ident)
                    mm(ps[:, 7, T:2 * T], ones, gate_diag.rearrange("p a b -> p (a b)"), True, True)\
                        .then_inc(s["moe_turned"], 1)

                def groups(it, up, down):
                    for g in range(G + 1):
                        if g < G:
                            eng.wait_ge(s["moe_act"], G * it + (g + 1))
                            if g == 1:
                                eng.wait_ge(s["moe_gates_turned"], it + 1)
                            for k in range(2):
                                w = next_unit(it)
                                for c in range(2):
                                    last = up(w, g, c, k)
                            last.then_inc(s["moe_h"], 1)
                        if g >= 1:
                            eng.wait_ge(s["moe_act"], G * it + (g + 2))
                            last = down(next_unit(it), g - 1)
                    last.then_inc(s["moe_y"], 1)

                def few_up(w, g, c, k):
                    at = (2 * c + k) * CAP
                    return features(w, c * P, ps[:, 6 + g % 2, at:at + CAP], xg, CAP)

                def few_down(w, g):
                    for c in range(2):
                        for half in range(2):
                            last = mm(ps[0:CAP, 4 + half, :], moe_act_sb[:, g % 2, c, :],
                                      w[:, c * D + half * 512:c * D + half * 512 + 512],
                                      g == 0 and c == 0, g == G - 1 and c == 1)
                    return last

                def all_up(w, g, c, k):
                    return features(w, c * P, ps[:, 4 + 2 * (g % 2) + c, k * T:(k + 1) * T], xc, T)

                def all_down(w, g):
                    first, final = g == 0, g == G - 1
                    for c in range(2):
                        for o in range(KC):
                            last = mm(ps[:, o // 2, (o % 2) * T:(o % 2) * T + T],
                                      w[:, c * D + o * P:c * D + o * P + P], act_sb[:, g % 2, c, :],
                                      first and c == 0 and o % 2 == 0, final and c == 1,
                                      skip_group_check=True)
                    return last

                gather(0)
                turn(0)
                with eng.Fori(0, EXPERTS) as it:
                    is_crowded = eng.value_load(crowded[0:1, bass.ds(it, 1)], min_val=0, max_val=1)
                    eng.wait_ge(s["moe_xg_a"], it + 1)
                    eng.wait_ge(s["moe_xg_d"], it + 1)
                    eng.wait_ge(s["moe_added"], 4 * it + 4)
                    with eng.If(is_crowded != 0):
                        unit_no[0] = ubase
                        groups(it, all_up, all_down)
                        eng.sem_inc(s["moe_scattered"], 4)
                        eng.wait_ge(s["moe_added"], 4 * it + 8)
                        gather(it + 1)
                    with eng.Else():
                        unit_no[0] = ubase
                        groups(it, few_up, few_down)
                        gather(it + 1)
                        eng.wait_ge(s["moe_y_a"], it + 1)
                        eng.wait_ge(s["moe_y_d"], it + 1)
                        eng.wait_ge(s["moe_xg_a"], it + 2)
                        eng.wait_ge(s["moe_xg_d"], it + 2)
                        for c in range(KC):
                            ins = mm(ps[:, c // 2, (c % 2) * T:(c % 2) * T + T], y_sb[0:CAP, c * P:c * P + P],
                                     sel_gt[0:CAP, :], True, True)
                            if c % 2:
                                ins.then_inc(s["moe_scattered"], 1)
                    turn(it + 1)
                unit_no[0] = ubase + EXPERTS * MOE_UNITS
                for b in range(8):
                    readers[b] = source("ln2_1", 0)

            def ffn():
                for b in range(4):
                    o = fill(("dense", "y", b), b, (s["res_added"], b + 1))
                    mm(o, zeros, con[:, 0:512], True, False)
                for b in range(4, 8):
                    if readers[b] is not None:
                        eng.wait_ge(*readers[b])
                before_ffn.extend(count)
                for g in range(GROUPS_DENSE + 1):
                    if g < GROUPS_DENSE:
                        b = 4 + 2 * (g % 2)
                        if g >= 2:
                            eng.wait_ge(s["ffn_act"], 2 * (g - 1))
                        w = next_unit()
                        for c in range(2):
                            features(w, c * P, ps[:, b + c, 0:T], xc, T)
                        w = next_unit()
                        for c in range(2):
                            features(w, c * P, ps[:, b + c, T:2 * T], xc, T).then_inc(bank_full[b + c], 1)
                            count[b + c] += 1
                    if g >= 1:
                        a = act_sb[:, (g - 1) % 2]
                        eng.wait_ge(s["ffn_act"], 2 * g)
                        w = next_unit()
                        for c in range(2):
                            for o in range(KC):
                                mm(ps[:, o // 2, (o % 2) * T:(o % 2) * T + T],
                                   w[:, c * D + o * P:c * D + o * P + P], a[:, c, :], False, False,
                                   skip_group_check=True)
                for b in range(4):
                    mm(ps[:, b, :], zeros, con[:, 0:512], False, True)\
                        .then_inc(bank_full[b], 1)
                for b in range(4, 8):
                    readers[b] = (s["ffn_act"], 2 * GROUPS_DENSE)

            def block2_projection(l):
                n_q = 2 * T if l == 0 else T
                q_tiles = 4 if l == 0 else 2
                fresh[0] = f"rms{l}"
                for c in range(2 * M_HEADS):
                    if c % 2 == 0:
                        w = next_unit()
                    o = fill(("pre", l, c), c % 4, (s["pre_copied"], 8 * l + c + 1))
                    n = n_q if c < M_HEADS else 2 * T
                    features(w, (c % 2) * P, o[:, 0:n], xn, n).then_inc(bank_full[c % 4], 1)
                w = next_unit()
                for t in range(4):
                    o = fill(("vg", l, t), 4 + t, (s["vg_out"], 4 * l + t + 1))
                    tokens(w, P + 16, o[:, 0:P + 16], xn, t).then_inc(bank_full[4 + t], 1)
                for u in range(2):
                    w = next_unit()
                    for t in range(4):
                        o = fill(("mv", l, u, t), t, (s["mv_copied"], 8 * l + 4 * u + t + 1))
                        tokens(w, GW, o[:, 0:GW], xn, t).then_inc(bank_full[t], 1)
                for c in range(CC + 1):
                    if c % 2 == 0:
                        w = next_unit()
                    b = 4 + c % 4
                    n = n_q if c < CC else 2 * T
                    o = fill(("aqk", l, c), b, (s["aqk_copied"], 5 * l + c + 1))
                    features(w, (c % 2) * P, o[:, 0:n], xn, n).then_inc(bank_full[b], 1)
                for c in range(CC):
                    if c % 2 == 0:
                        w = next_unit()
                    o = fill(("az", l, c), c, (s["azs_out"], 4 * l + c + 1))
                    features(w, (c % 2) * P, o[:, 0:n_q], xn, n_q).then_inc(bank_full[c], 1)
                for c in range(M_HEADS):
                    if c % 2 == 0:
                        w = next_unit()
                    o = fill(("mz", l, c), 4 + c, (s["mzs_out"], 4 * l + c + 1))
                    features(w, (c % 2) * P, o[:, 0:n_q], xn, n_q).then_inc(bank_full[4 + c], 1)
                for u in range(2):
                    w = next_unit()
                    for t in range(q_tiles):
                        o = fill(("mo", l, u, t), t, (s["mos_out"], 8 * l + q_tiles * u + t + 1))
                        tokens(w, GW, o[:, 0:GW], xn, t).then_inc(bank_full[t], 1)
                for c in range(CC + 1):
                    b = 4 + c % 4
                    eng.wait_ge(s["aqk_copied"], 5 * l + c + 1)
                    src = aq[:, c, 0:T] if c < CC else ak[:, 0:T]
                    o = fill(("rope", l, c), b, (s["rope_out"], 5 * l + c + 1))
                    mm(o[:, 0:T], con[:, CN.all("rot")], src, True, True).then_inc(bank_full[b], 1)

            def mlstm(l):
                eng.wait_ge(s["lf_out"], l + 1)
                o = fill(("cum", l), 0, (s["cum_out"], l + 1))
                mm(o[:, 0:16], con[:, CN.all("tri_f")], lf[:, :, 0:4], True, True)
                mm(o[:, 16:32], con[:, CN.all("tri_b")], lf[:, :, 4:8], True, True)
                mm(o[:, 32:64], ones, lf[:, :, :].rearrange("p a b -> p (a b)"), True, True)\
                    .then_inc(bank_full[0], 1)
                eng.wait_ge(s["cqk_out"], 8 * (l + 1))
                eng.wait_ge(s["mv_copied"], 8 * (l + 1))
                for j in range(4):
                    k = step_no(l, j)
                    eng.wait_ge(s["adiag_out"], k)
                    for half in range(2):
                        o = fill(("arow", l, j, half), 2 + half, (s["decay_masked"], k))
                        mm(o, ones, adiag[:, 4 * half:4 * half + 4, :].rearrange("p a b -> p (a b)"), True, True)\
                            .then_inc(bank_full[2 + half], 1)
                    yield
                    yield
                    yield
                    for d in range(2):
                        g = 2 * (k - 1) + d + 1
                        t = ORDER[d][j]
                        tok = slice(t * P, t * P + P)
                        rows = l == 0 or t < TT
                        if rows:
                            o = fill(("sc", l, j, d), 0, (s["qk_weighted"], g))
                            for h in range(M_HEADS):
                                last = mm(o[:, h * P:h * P + P], cqk[:, h, tok], cqk[:, M_HEADS + h, tok], True, True)
                            last.then_inc(bank_full[0], 1)
                        o = fill(("kt", l, j, d), 1, (s["keys_weighted"], g))
                        for h in range(M_HEADS):
                            last = eng.transpose(o[:, h * P:h * P + P], cqk[:, M_HEADS + h, tok], ident)
                        last.then_inc(bank_full[1], 1)
                        if rows:
                            eng.wait_ge(s["state_out"], max(g + l - 1, 9 * l + 1))
                            for half in range(2):
                                o = fill(("inter", l, j, d, half), 2 + half, (s["inter_scaled"], g))
                                for h in range(2):
                                    last = mm(o[:, h * 129:h * 129 + 129], cqk[:, 2 * half + h, tok],
                                              state[:, 4 * d + 2 * half + h, :], True, True)
                                last.then_inc(bank_full[2 + half], 1)
                        yield
                        yield
                        if rows:
                            eng.wait_ge(s["qk_weighted"], g)
                            o = fill(("wt", l, j, d), 0, (s["qk_turned"], g))
                            for h in range(M_HEADS):
                                last = eng.transpose(o[:, h * P:h * P + P], wqk[:, h, :], ident)
                            last.then_inc(bank_full[0], 1)
                        yield
                        yield
                        if rows:
                            eng.wait_ge(s["qk_turned"], g)
                            for half in range(2):
                                o = fill(("intra", l, j, d, half), 2 + half, (s["mh_out"], g))
                                for h in range(2):
                                    last = mm(o[:, h * 129:h * 129 + 129], wqk_t[:, 2 * half + h, :],
                                              mv[:, t, 2 * half + h, :], True, True)
                                last.then_inc(bank_full[2 + half], 1)
                        eng.wait_ge(s["keys_weighted"], g)
                        for half in range(2):
                            o = fill(("ds", l, j, d, half), half, (s["state_out"], g + l + 1))
                            for h in range(2):
                                last = mm(o[:, h * 129:h * 129 + 129], kw[:, 2 * half + h, :],
                                          mv[:, t, 2 * half + h, :], True, True)
                            last.then_inc(bank_full[half], 1)
                        yield
                        yield

            def mlstm_turn(l):
                eng.wait_ge(s["mh_normed"], l + 1)
                for t in range(4 if l == 0 else 2):
                    o = fill(("mt", l, t), t, (s["mh_mixed"], 4 * l + t + 1))
                    for h in range(M_HEADS):
                        last = eng.transpose(o[:, h * P:h * P + P], hs[:, t, h * P:h * P + P], ident)
                    last.then_inc(bank_full[t], 1)

            def block2_attention(l):
                items = att_items(l)
                eng.wait_ge(s["rope_out"], 5 * (l + 1))
                eng.wait_ge(s["vg_out"], 4 * (l + 1))
                for n in range(len(items) + ATT_LAG):
                    if n < len(items):
                        _, i, half, qt = items[n]
                        k = ATT[items[n]]
                        b, p0 = 4 + k % 2, DH * half
                        o = fill(("as",) + items[n], b, (s["att_scored"], k))
                        keys = slice(0, 2 * T) if qt < TT else slice(T, 2 * T)
                        cols = slice(0, 2 * T) if qt < TT else slice(0, T)
                        mm(o[:, cols], aq[p0:p0 + DH, i, qt * P:qt * P + P], ak[p0:p0 + DH, keys], True, True)\
                            .then_inc(bank_full[b], 1)
                    if 3 <= n < len(items) + 3:
                        item = items[n - 3]
                        k = ATT[item]
                        kts = 4 if item[3] < TT else 2
                        b = 6
                        eng.wait_ge(s["att_prob"], k)
                        o = fill(("at",) + item, b, (s["att_turned"], k))
                        for kt in range(kts):
                            last = eng.transpose(o[:, kt * P:kt * P + P], prob2[:, k % 4, kt * P:kt * P + P], ident)
                        last.then_inc(bank_full[b], 1)
                    if 4 <= n < len(items) + 4:
                        _, i, half, qt = items[n - 4]
                        k = ATT[items[n - 4]]
                        eng.wait_ge(s["att_turned"], k)
                        if half == 0 and qt == 0:
                            o2 = fill(("ao", l, i), 7, (s["att_out"], CC * l + i + 1))
                        kts = 4 if qt < TT else 2
                        for kt in range(kts):
                            vt = kt if qt < TT else TT + kt
                            last = mm(o2[DH * half:DH * half + DH, qt * P:qt * P + P],
                                      vtok[:, vt, DH * half:DH * half + DH], pt2[:, k % 2, kt * P:kt * P + P],
                                      kt == 0, kt == kts - 1)
                        if half == 1 and qt == (3 if l == 0 else 1):
                            last.then_inc(bank_full[7], 1)
                    yield

            def out_half(l, w, c, o, half):
                n = 2 * T if l == 0 else T
                for k in range(CC * half, CC * half + CC):
                    last = mm(o[:, 0:n], w[:, k * GW + (c % 2) * P:k * GW + (c % 2) * P + P], mix2[:, k, 0:n],
                              k == 0, k == KC - 1)
                return last

            def block2_out_start(l):
                eng.wait_ge(s["att_out"], CC * (l + 1))
                started = []
                for c in range(4):
                    if c % 2 == 0:
                        w = next_unit()
                        if c == 2:
                            release[0] = False
                    o = fill(("xo", l, c), 4 + c, (s["x_added"], KC * l + c + 1))
                    out_half(l, w, c, o, 0)
                    started.append((w, o))
                return started

            def block2_out(l, started):
                eng.wait_ge(s["mh_mixed"], 4 if l == 0 else 6)
                for c, (w, o) in enumerate(started):
                    if c == 2:
                        release[0] = True
                    out_half(l, w, c, o, 1).then_inc(bank_full[4 + c], 1)
                for c in range(4, KC):
                    if c % 2 == 0:
                        w = next_unit()
                    o = fill(("xo", l, c), c, (s["x_added"], KC * l + c + 1))
                    out_half(l, w, c, o, 0)
                    out_half(l, w, c, o, 1).then_inc(bank_full[c], 1)

            eng.wait_ge(s["inputs_loaded"], 16 * N_INPUTS)
            norm("in", xc, KC, T)
            for l in range(DEPTH):
                block1_projection(l)
                filler = conditions(l)
                for _ in range(3):
                    next(filler)
                norm(f"conv{l}", conv_acc, CC, T, bank=2)
                block1_attention(l, filler)
                for _ in filler:
                    pass
                block1_out(l)
                norm(f"ln1_{l}", res, KC, T)
                if l == 1:
                    eng.wait_ge(s["norm_out"], outk(f"ln1_{l}"))
                    router()
                    turn_tokens()
                    places()
                ple_products(l)
                if l == 1:
                    moe()
                else:
                    ffn()
                norm(f"ln2_{l}", res, KC, T)
            for l in range(DEPTH):
                norm(f"rms{l}", xc, KC, 2 * T, centred=False)
                block2_projection(l)
                interleave(l, mlstm(l), block2_attention(l))
                started = block2_out_start(l)
                mlstm_turn(l)
                block2_out(l, started)
            norm("final", xc, KC, T, centred=False)
            assert unit_no[0] == UNITS, (unit_no[0], UNITS)

        def tile(eng, *key):
            b, n = placed[key]
            eng.wait_ge(bank_full[b], n)
            return ps[:, b, :]

        @block.sync
        def _(eng):
            eng.dma_start(con[:, 0:CN.early], consts[:, 0:CN.early]).then_inc(s["inputs_loaded"], 16)
            eng.dma_start(xc[:, :, 0:T], x_t).then_inc(s["inputs_loaded"], 16)
            eng.dma_start(par[:, :], params).then_inc(s["inputs_loaded"], 16)
            for n in range(SLOTS):
                eng.dma_start(ring[:, n, :], weights[n]).then_inc(weights_in[n], 16)
            rounds = (UNITS - SLOTS) // SLOTS
            with eng.Fori(0, rounds) as r:
                for i in range(SLOTS):
                    eng.wait_ge(s["weights_used"], SLOTS * r + (i + 1))
                    eng.dma_start(ring[:, i, :], weights[SLOTS * r + (SLOTS + i)]).then_inc(weights_in[i], 16)
            for n in range(SLOTS * (rounds + 1), UNITS):
                eng.wait_ge(s["weights_used"], n - SLOTS + 1)
                eng.dma_start(ring[:, n % SLOTS, :], weights[n]).then_inc(weights_in[n % SLOTS], 16)
            eng.wait_ge(s["norm_out"], outk("final"))
            eng.dma_start(out, cen).then_inc(s["out_stored"], 16)
            eng.wait_ge(s["out_stored"], 16)

        @block.gpsimd
        def _(eng):
            eng.wait_ge(s["late_loaded"], 16 * N_LATE)
            for l in range(DEPTH):
                if l:
                    eng.wait_ge(s["nbr_scored"], HEADS * l)
                for r in range(ROWS):
                    p0 = GRID_W * (r % 2)
                    src = rel[l, :, :, ROWS - 1 - r:2 * ROWS - 1 - r, :].rearrange("c h i j -> c h (i j)")
                    eng.dma_start(relb[p0:p0 + GRID_W, r // 2, :, :], src).then_inc(s["rel_loaded"], 16)
                eng.wait_ge(s["rel_loaded"], 16 * ROWS * (l + 1))
                for t in range(TT):
                    mask = con[:, CN("nbr_mask", t * T, T)].unsqueeze(1).broadcast_to([P, HEADS, T])
                    eng.tensor_tensor(relb[:, t], relb[:, t], mask, ALU.add).then_inc(s["rel_ready"], 1)

        @block.scalar
        def _(eng):
            def norm(name, chunks, n, centred=True, src=None):
                k, base = normk(name), before(name)
                for c in range(chunks):
                    if centred:
                        eng.wait_ge(s["norm_centered"], base + c + 1)
                        to, a = sq, cen
                    else:
                        eng.wait_ge(*source(name, c))
                        to, a = sq2, src
                    eng.activation(to[:, c, 0:n], a[:, c, 0:n], ACT.Square).then_inc(s["norm_squared"], 1)
                o, eps = (std1, "eps5") if centred else (std2, "eps6")
                v = tile(eng, "var", name)
                eng.activation(o[:, 0:n], v[:, 0:n], ACT.Sqrt, bias=con[:, CN(eps)], scale=1.0 / (chunks * P))\
                    .then_inc(s["norm_std"], 1)

            def conditions(l):
                for u in range(UNITS_ADA):
                    o = tile(eng, "row", l, u)
                    eng.activation(cond_row[0:2, u % 2, :], o[0:2, 0:GW], ACT.Copy).then_inc(s["cond_row"], 1)
                    yield

            def modulate(l):
                eng.wait_ge(s["coef_out"], l + 1)
                for c in range(KC):
                    eng.wait_ge(s["norm_scaled"], before(f"rms{l}") + c + 1)
                    v = xn[:, c, T:2 * T]
                    eng.activation(v, v, ACT.Identity, bias=mod[:, l, c, 1:2], scale=coef[:, c, 1:2])\
                        .then_inc(s["norm_out_a"], 1)

            def block1_projection(l):
                for j in range(CC):
                    o = tile(eng, "glu", l, j)
                    if CC * l + j >= 2:
                        eng.wait_ge(s["glu_out"], CC * l + j - 1)
                    eng.activation(sig_sb[:, j % 2, :], o[:, T:2 * T], ACT.Sigmoid, bias=par[:, PC(f"b_g{l}", j)])\
                        .then_inc(s["glu_gate"], 1)
                for j in range(CC):
                    o = tile(eng, "qk", l, j)
                    eng.activation(q1[:, j, :], o[:, 0:T], ACT.Identity, bias=bq_s[:, l, j:j + 1], scale=DH ** -0.5)
                    eng.activation(k1[:, j, :], o[:, T:2 * T], ACT.Identity, bias=par[:, PC(f"b_k{l}", j)])\
                        .then_inc(s["qk_out"], 1)

            def conv_silu(l):
                for j in range(CC):
                    eng.wait_ge(s["norm_scaled"], before(f"conv{l}") + j + 1)
                    eng.activation(mix1[:, j, :], cen[:, j, :], ACT.Silu, bias=par[:, PC(f"conv_ln_b{l}", j)],
                                   scale=par[:, PC(f"conv_ln_g{l}", j)]).then_inc(s["conv_mixed"], 1)

            def block1_attention(l, filler):
                for i in range(HEADS + 4):
                    next(filler, None)
                    if 3 <= i < HEADS + 3:
                        o = tile(eng, "pt", l, i - 3)
                        eng.activation(pt1[:, (i - 3) % 2].rearrange("p a b -> p (a b)"), o, ACT.Copy)\
                            .then_inc(s["nbr_turned"], 1)
                    if i < HEADS:
                        k = HEADS * l + i + 1
                        eng.wait_ge(s["nbr_max"], k)
                        for t in range(TT):
                            eng.activation(prob1[:, i % 3, t, :], prob1[:, i % 3, t, :], ACT.Exp,
                                           bias=rmax[:, i % 3, t:t + 1], accum_out=rsum[:, i % 3, t:t + 1])\
                                .then_inc(s["nbr_exp"], 1)
                    if i >= 5 and i % 2 == 1:
                        h2 = (i - 5) // 2
                        o = tile(eng, "o", l, h2)
                        eng.activation(mix1[:, CC + h2, :], o[:, 0:T], ACT.Copy).then_inc(s["nbr_out"], 1)

            def block1_out(l):
                for c in range(KC):
                    o = tile(eng, "mix", l, c)
                    eng.activation(sq[:, c, :], o[:, 0:T], ACT.Identity, bias=par[:, PC(f"b_out{l}", c)])\
                        .then_inc(s["mix_biased"], 1)

            def ple_products(l):
                for c in range(4):
                    o = tile(eng, "ple", l, c)
                    eng.activation(ple[:, 2 * c:2 * c + 2, :].rearrange("p a b -> p (a b)"), o, ACT.Copy)\
                        .then_inc(s["ple_copied"], 1)
                for c in range(KC):
                    o = tile(eng, "pgate", l, c)
                    if KC * l + c >= 2:
                        eng.wait_ge(s["ple_out"], KC * l + c - 1)
                    eng.activation(sig_sb[:, c % 2, :], o[:, 0:T], ACT.Sigmoid,
                                   bias=par[:, PC(f"ple_gate_b{l}", c)]).then_inc(s["ple_gate"], 1)

            def gate_exp():
                eng.wait_ge(s["gate_exp"], 1)
                eng.activation(gexp, gexp, ACT.Exp).then_inc(s["gate_exp"], 1)

            def tokens_copy():
                for t in range(TT):
                    for half in range(2):
                        o = tile(eng, "htok", t, half)
                        eng.activation(h_tok[:, t, half * 512:half * 512 + 512], o, ACT.Copy).then_inc(s["h_turned"], 1)

            def moe():
                G = GROUPS_EXPERT

                def gathered(nxt):
                    eng.wait_ge(s["moe_gathered"], nxt * 2 + 1)
                    eng.activation(xg[:, 0:4, :].rearrange("p a b -> p (a b)"), ps[:, 0, 0:4 * CAP], ACT.Copy)\
                        .then_inc(s["moe_xg_a"], 1)

                def gates_turned(nxt):
                    eng.wait_ge(s["moe_turned"], nxt + 1)
                    eng.activation(sel_gt[0:CAP, :], ps[0:CAP, 7, 0:T], ACT.Copy)
                    eng.activation(gate_row, ps[:, 7, T:2 * T], ACT.Copy).then_inc(s["moe_gates_turned"], 1)

                gathered(0)
                gates_turned(0)
                eng.wait_ge(s["crowded_out"], 1)
                with eng.Fori(0, EXPERTS) as it:
                    is_crowded = eng.value_load(crowded[0:1, bass.ds(it, 1)], min_val=0, max_val=1)
                    with eng.If(is_crowded != 0):
                        for g in range(G):
                            b = 4 + 2 * (g % 2)
                            eng.wait_ge(s["moe_h"], it * G + (g + 1))
                            eng.activation(silu_sb[:, g % 2], ps[:, b:b + 2, 0:T], ACT.Silu).then_inc(s["moe_silu"], 1)
                        eng.sem_inc(s["moe_y_a"], 1)
                    with eng.Else():
                        for g in range(G):
                            h = ps[:, 6 + g % 2, 0:4 * CAP].rearrange("p (c k n) -> p c k n", c=2, k=2)
                            eng.wait_ge(s["moe_h"], it * G + (g + 1))
                            eng.activation(moe_silu_sb[:, g % 2], h[:, :, 0, :], ACT.Silu).then_inc(s["moe_silu"], 1)
                        eng.wait_ge(s["moe_y"], it + 1)
                        eng.activation(y_sb[0:CAP, 0:512], ps[0:CAP, 4, :], ACT.Copy).then_inc(s["moe_y_a"], 1)
                    gathered(it + 1)
                    gates_turned(it + 1)

            def ffn():
                for g in range(GROUPS_DENSE):
                    for c in range(2):
                        b = 4 + 2 * (g % 2) + c
                        eng.wait_ge(bank_full[b], before_ffn[b] + g // 2 + 1)
                        eng.activation(silu_sb[:, g % 2, c, :], ps[:, b, 0:T], ACT.Silu).then_inc(s["ffn_silu"], 1)

            def block2_projection(l):
                n_q = 2 * T if l == 0 else T
                q_tiles = 4 if l == 0 else 2
                segs = 2 if l == 0 else 1
                eng.wait_ge(s["pad_zeroed"], l + 1)
                for c in range(2 * M_HEADS):
                    o = tile(eng, "pre", l, c)
                    sg = segs if c < M_HEADS else 2
                    eng.activation(pre[:, c, 0:sg, PAD2:PAD2 + T],
                                   o[:, 0:sg * T].rearrange("p (a b) -> p a b", b=T), ACT.Copy)\
                        .then_inc(s["pre_copied"], 1)
                for u in range(2):
                    for t in range(4):
                        o = tile(eng, "mv", l, u, t)
                        eng.activation(mv[:, t, 2 * u:2 * u + 2, 0:M_DH],
                                       o[:, 0:GW].rearrange("p (a b) -> p a b", b=M_DH), ACT.Copy)\
                            .then_inc(s["mv_copied"], 1)
                for c in range(CC + 1):
                    o = tile(eng, "aqk", l, c)
                    if c < CC:
                        eng.activation(aq[:, c, 0:n_q], o[:, 0:n_q], ACT.Copy, scale=DH ** -0.5)\
                            .then_inc(s["aqk_copied"], 1)
                    else:
                        eng.activation(ak, o, ACT.Copy).then_inc(s["aqk_copied"], 1)
                for c in range(CC):
                    o = tile(eng, "az", l, c)
                    eng.activation(azs[:, c, 0:n_q], o[:, 0:n_q], ACT.Silu).then_inc(s["azs_out"], 1)
                for c in range(M_HEADS):
                    o = tile(eng, "mz", l, c)
                    eng.activation(mzs[:, c, 0:n_q], o[:, 0:n_q], ACT.Silu).then_inc(s["mzs_out"], 1)
                for c in range(2 * M_HEADS):
                    eng.wait_ge(s["conv2_acc"], 8 * l + c + 1)
                    n = n_q if c < M_HEADS else 2 * T
                    eng.activation(cqk[:, c, 0:n], cqk[:, c, 0:n], ACT.Silu, bias=par[:, PC(f"conv_b2{l}", c)])\
                        .then_inc(s["cqk_out"], 1)
                for u in range(2):
                    for t in range(q_tiles):
                        o = tile(eng, "mo", l, u, t)
                        eng.activation(mos[:, t, u * GW:(u + 1) * GW], o[:, 0:GW], ACT.Sigmoid)\
                            .then_inc(s["mos_out"], 1)

            def mlstm(l):
                eng.wait_ge(s["lf_abs"], l + 1)
                eng.activation(labs, labs, ACT.Exp, scale=-1.0).then_inc(s["lf_ln"], 1)
                eng.wait_ge(s["lf_ln"], 2 * l + 1)
                eng.activation(labs, labs, ACT.Ln, bias=con[:, CN("one")]).then_inc(s["lf_ln"], 1)
                for j in range(4):
                    k = step_no(l, j)
                    yield
                    yield
                    eng.wait_ge(s["stats_out"], k)
                    eng.activation(wt, ex, ACT.Exp).then_inc(s["stats_exp"], 1)
                    for d in range(2):
                        for h in range(M_HEADS):
                            n = 4 * d + h
                            ins = eng.activation(decay[:, n, :], amask[:, n, :], ACT.Exp, bias=nm_row[:, n:n + 1])
                        ins.then_inc(s["decay_out"], 1)
                    eng.wait_ge(s["stats_exp"], k)
                    yield
                    for d in range(2):
                        g = 2 * (k - 1) + d + 1
                        t = ORDER[d][j]
                        rows = l == 0 or t < TT
                        yield
                        if rows:
                            if g > 1:
                                eng.wait_ge(s["mh_out"], g - 1)
                            for half in range(2):
                                o = tile(eng, "inter", l, j, d, half)
                                for h in range(2):
                                    n = 2 * half + h
                                    ins = eng.activation(inter_s[:, n, :], o[:, h * 129:h * 129 + 129], ACT.Copy,
                                                         scale=wt[:, 0, 4 * d + n:4 * d + n + 1])
                            ins.then_inc(s["inter_scaled"], 1)
                        else:
                            eng.sem_inc(s["inter_scaled"], 1)
                        yield
                        yield
                        if rows:
                            o = tile(eng, "wt", l, j, d)
                            eng.activation(wqk_t.rearrange("p a b -> p (a b)"), o, ACT.Copy).then_inc(s["qk_turned"], 1)
                        else:
                            eng.sem_inc(s["qk_turned"], 1)
                        yield
                        yield
                        if not rows:
                            eng.wait_ge(s["mh_out"], g)
                        yield

            def mlstm_std(l):
                tiles = 4 if l == 0 else 2
                eng.wait_ge(s["mh_sumsq"], l + 1)
                n = tiles * M_HEADS
                eng.activation(rms_i[:, 0:n], rms_s[:, 0:n], ACT.Sqrt, bias=con[:, CN("eps6")], scale=1.0 / M_DH)\
                    .then_inc(s["mh_std"], 1)

            def block2_attention(l):
                items = att_items(l)
                for n in range(len(items) + ATT_LAG):
                    if 4 <= n < len(items) + 4:
                        item = items[n - 4]
                        k = ATT[item]
                        w = 2 * T if item[3] < TT else T
                        o = tile(eng, "at", *item)
                        eng.activation(pt2[:, k % 2, 0:w], o[:, 0:w], ACT.Copy).then_inc(s["att_turned"], 1)
                    if n < len(items):
                        _, i, half, qt = items[n]
                        k = ATT[items[n]]
                        h = i + CC * half
                        w = 2 * T if qt < TT else T
                        eng.wait_ge(s["att_max"], k)
                        eng.activation(esink[:, k % 4, :], par[:, PC(f"sink{l}", h)], ACT.Exp,
                                       bias=rmax[:, k % 4, 0:1])
                        eng.activation(prob2[:, k % 4, 0:w], prob2[:, k % 4, 0:w], ACT.Exp,
                                       bias=rmax[:, k % 4, 0:1], accum_out=rsum[:, k % 4, 0:1])\
                            .then_inc(s["att_exp"], 1)
                    yield

            eng.wait_ge(s["inputs_loaded"], 16 * N_INPUTS)
            eng.dma_start(con[:, CN.early:], consts[:, CN.early:]).then_inc(s["late_loaded"], 16)
            eng.dma_start(p_sb, p_t).then_inc(s["late_loaded"], 16)
            eng.dma_start(xc[:, :, T:2 * T], ctx_t).then_inc(s["late_loaded"], 16)
            eng.activation(cond_s, par[:, PC.all("cond")], ACT.Silu).then_inc(s["cond_ready"], 1)
            norm("in", KC, T)
            eng.wait_ge(s["prep_done"], 1)
            for l in range(DEPTH):
                block1_projection(l)
                filler = conditions(l)
                for _ in range(3):
                    next(filler)
                norm(f"conv{l}", CC, T)
                conv_silu(l)
                block1_attention(l, filler)
                for _ in filler:
                    pass
                block1_out(l)
                norm(f"ln1_{l}", KC, T)
                if l == 1:
                    gate_exp()
                    tokens_copy()
                ple_products(l)
                if l == 1:
                    moe()
                else:
                    ffn()
                norm(f"ln2_{l}", KC, T)
            for l in range(DEPTH):
                norm(f"rms{l}", KC, 2 * T, centred=False, src=xc)
                modulate(l)
                block2_projection(l)
                interleave(l, mlstm(l), block2_attention(l))
                mlstm_std(l)
            norm("final", KC, T, centred=False, src=xc)

        @block.vector
        def _(eng):
            order = [0]

            def link(ins):
                order[0] += 1
                ins.then_inc(s["dve_order"], 1)
                eng.wait_ge(s["dve_order"], order[0])

            def rows(v, a):
                return v.unsqueeze(1).broadcast_to([P, a, v.shape[1]])

            def norm(name, src, chunks, n, gain, centred=True, dst=None):
                k, base = normk(name), before(name)
                if centred:
                    o = tile(eng, "mean", name)
                    for c in range(chunks):
                        eng.scalar_tensor_tensor(out=cen[:, c, :], in0=o[:, 0:n], scalar=-1.0 / (chunks * P),
                                                 in1=src[:, c, 0:n], op0=ALU.mult, op1=ALU.add)\
                            .then_inc(s["norm_centered"], 1)
                    a, std, rstd = cen, std1, rstd1
                else:
                    a, std, rstd = src, std2, rstd2
                eng.wait_ge(s["norm_std"], k)
                link(eng.reciprocal(rstd[:, 0:n], std[:, 0:n]))
                to = cen if centred else (xn if dst is None else dst)
                for c in range(chunks + 1):
                    if c < chunks:
                        eng.tensor_tensor(to[:, c, 0:n], a[:, c, 0:n], rstd[:, 0:n], ALU.mult)\
                            .then_inc(s["norm_scaled"], 1)
                    if c >= 1 and gain is not None:
                        eng.wait_ge(s["norm_scaled"], base + c)
                        gain(c - 1, to).then_inc(s["norm_out"], 1)

            def layer_gain(g, b, dst):
                def f(c, a):
                    return eng.tensor_scalar(dst[:, c, 0:T], a[:, c, 0:T], par[:, PC(g, c)], par[:, PC(b, c)],
                                             ALU.mult, ALU.add)
                return f

            def block1_projection(l):
                for j in range(CC):
                    o = tile(eng, "glu", l, j)
                    eng.wait_ge(s["glu_gate"], CC * l + j + 1)
                    eng.scalar_tensor_tensor(out=glu[:, j, PAD1:PAD1 + T], in0=o[:, 0:T],
                                             scalar=par[:, PC(f"b_a{l}", j)], in1=sig_sb[:, j % 2, :],
                                             op0=ALU.add, op1=ALU.mult).then_inc(s["glu_out"], 1)

            def conv(l):
                eng.wait_ge(s["glu_out"], CC * (l + 1))
                first = order[0]
                for tap in range(CONV_K):
                    for j in range(CC):
                        w = par[:, PC(f"conv_w{l}", j * CONV_K + tap)]
                        src = glu[:, j, tap:tap + T]
                        if tap:
                            eng.wait_ge(s["dve_order"], first + (tap - 1) * CC + j + 1)
                        if tap == 0:
                            ins = eng.tensor_scalar(conv_acc[:, j, :], src, w, par[:, PC(f"conv_b{l}", j)],
                                                    ALU.mult, ALU.add)
                        else:
                            ins = eng.scalar_tensor_tensor(out=conv_acc[:, j, :], in0=src, scalar=w,
                                                           in1=conv_acc[:, j, :], op0=ALU.mult, op1=ALU.add)
                        if tap == CONV_K - 1 and j == CC - 1:
                            ins.then_inc(s["norm_src"], 1)
                        else:
                            ins.then_inc(s["dve_order"], 1)
                            order[0] += 1
                eng.wait_ge(*source(f"conv{l}", 0))
                eng.wait_ge(s["dve_order"], order[0])

            def values(l):
                for j in range(2):
                    o = tile(eng, "v", l, j)
                    bias = rows(par[:, PC(f"b_v{l}", j * GW, GW)], TT)
                    eng.tensor_tensor(v1[:, :, j * GW:(j + 1) * GW], o.rearrange("p (a b) -> p a b", b=GW), bias,
                                      ALU.add).then_inc(s["v_out"], 1)

            def conditions(l):
                o = tile(eng, "mod", l)
                m = mod[:, l]
                bias = par[:, PC.all(f"b_ada{l}")].unsqueeze(2).broadcast_to([P, 3 * KC, 2])
                eng.tensor_tensor(m, o[:, 0:6 * KC].rearrange("p (a b) -> p a b", b=2), bias, ALU.add)\
                    .then_inc(s["mod_out"], 1)

            def block1_attention(l):
                eng.wait_ge(s["rel_ready"], TT * (l + 1))
                for i in range(HEADS + 2):
                    if i >= 2:
                        h = i - 2
                        eng.wait_ge(s["nbr_exp"], 2 * (HEADS * l + h + 1))
                        link(eng.reciprocal(rinv[:, h % 3, :], rsum[:, h % 3, :]))
                        for t in range(TT):
                            ins = eng.tensor_scalar(prob1[:, h % 3, t, :], prob1[:, h % 3, t, :],
                                                    rinv[:, h % 3, t:t + 1], None, ALU.mult)
                        ins.then_inc(s["nbr_prob"], 1)
                    if i < HEADS:
                        k = HEADS * l + i + 1
                        pr = prob1[:, i % 3]
                        o = tile(eng, "s", l, i)
                        if i >= 3:
                            tile(eng, "pt", l, i - 3)
                        eng.tensor_tensor(pr, o.rearrange("p (a b) -> p a b", b=T), relb[:, :, i, :], ALU.add)\
                            .then_inc(s["nbr_scored"], 1)
                        eng.wait_ge(s["nbr_scored"], k)
                        eng.tensor_reduce(rmax[:, i % 3, :], pr, AX.X, ALU.max, negate=True).then_inc(s["nbr_max"], 1)

            def block1_out(l):
                for c in range(KC):
                    eng.wait_ge(s["mix_biased"], KC * l + c + 1)
                    eng.scalar_tensor_tensor(out=res[:, c, :], in0=xc[:, c, 0:T], scalar=ALPHA,
                                             in1=sq[:, c, :], op0=ALU.mult, op1=ALU.add).then_inc(s["mix_added"], 1)
                eng.wait_ge(s["mix_added"], KC * (l + 1))

            def routing():
                o = tile(eng, "logits")
                eng.tensor_copy(logits, o[:, 0:TT * 8].rearrange("p (a b) -> p a b", b=8))\
                    .then_inc(s["logits_out"], 1)
                eng.wait_ge(s["logits_out"], 1)
                link(eng.tensor_reduce(gmax[:, :, 0], logits, AX.X, ALU.max))
                eng.tensor_tensor(gexp, logits, gmax[:, :, 0:1].broadcast_to([P, TT, 8]), ALU.subtract)\
                    .then_inc(s["gate_exp"], 1)
                before = con[:, CN.all("before")].rearrange("p (a b) -> p a b", b=8)
                for t in range(TT):
                    other = logits[:, t, :].unsqueeze(1).broadcast_to([P, 8, 8])
                    own = logits[:, t, :].unsqueeze(2).broadcast_to([P, 8, 8])
                    gc = gcmp[:, t, :].rearrange("p (a b) -> p a b", b=8)
                    ge = geq[:, t, :].rearrange("p (a b) -> p a b", b=8)
                    link(eng.tensor_tensor(gc, other, own, ALU.is_gt))
                    link(eng.tensor_tensor(ge, other, own, ALU.is_equal))
                    link(eng.tensor_tensor(ge, ge, before, ALU.mult))
                    link(eng.tensor_tensor(gc, gc, ge, ALU.add))
                    link(eng.tensor_reduce(rank_t[:, t, :], gc, AX.X, ALU.add))
                eng.tensor_scalar(rank_t, rank_t, float(TOP_K), None, ALU.is_lt).then_inc(s["chosen_out"], 1)
                eng.wait_ge(s["chosen_out"], 1)
                eng.wait_ge(s["gate_exp"], 2)
                link(eng.tensor_tensor(gate, gexp, rank_t, ALU.mult))
                link(eng.tensor_reduce(gsum[:, :, 0], gate, AX.X, ALU.add))
                link(eng.reciprocal(gsum, gsum))
                link(eng.tensor_tensor(gate, gate, gsum.broadcast_to([P, TT, 8]), ALU.mult))

            def places():
                o = tile(eng, "places")
                in_order = o[:, 0:16].rearrange("p (a b) -> p a b", b=8)
                eng.tensor_tensor(slot_of[:, :, 0:8], in_order, rank_t, ALU.mult).then_inc(s["dve_order"], 1)
                order[0] += 1
                eng.tensor_copy(counts, o[:, 16:24]).then_inc(s["places_out"], 1)
                eng.wait_ge(s["dve_order"], order[0])
                eng.wait_ge(s["places_out"], 1)
                link(eng.tensor_scalar(slot_of[:, :, 0:8], slot_of[:, :, 0:8], -1.0, None, ALU.add))
                link(eng.tensor_copy(slot_of[:, :, 8:9], slot_of[:, :, 0:1]))
                link(eng.tensor_copy(gate_c[:, :, 0:8], gate))
                link(eng.tensor_copy(gate_c[:, :, 8:9], gate[:, :, 0:1]))
                eng.tensor_scalar(crowded[:, :], counts, CAP + 0.5, None, ALU.is_gt).then_inc(s["crowded_out"], 1)

            def moe():
                G = GROUPS_EXPERT

                def gathered(nxt):
                    eng.wait_ge(s["moe_gathered"], nxt * 2 + 2)
                    eng.tensor_copy(xg[:, 4:8, :].rearrange("p a b -> p (a b)"), ps[:, 1, 0:4 * CAP])\
                        .then_inc(s["moe_xg_d"], 1)

                def select(e):
                    place = slot_of[:, :, bass.ds(e, 1)].broadcast_to([P, TT, CAP])
                    gates = gate_c[:, :, bass.ds(e, 1)]
                    eng.tensor_tensor(sel, rows(con[:, CN.all("slot")], TT), place, ALU.is_equal)\
                        .then_inc(s["moe_sel"], 1)
                    eng.tensor_tensor(gate_diag, rows(ident, TT), gates.broadcast_to([P, TT, P]), ALU.mult)
                    eng.wait_ge(s["moe_sel"], e + 1)
                    eng.tensor_tensor(sel_g, sel, gates.broadcast_to([P, TT, CAP]), ALU.mult)\
                        .then_inc(s["moe_sel_g"], 1)

                eng.sem_inc(s["moe_act"], 2)
                eng.sem_inc(s["moe_added"], 4)
                eng.wait_ge(s["crowded_out"], 1)
                select(0)
                gathered(0)
                with eng.Fori(0, EXPERTS) as it:
                    is_crowded = eng.value_load(crowded[0:1, bass.ds(it, 1)], min_val=0, max_val=1)
                    eng.wait_ge(s["moe_turned"], it + 1)
                    eng.wait_ge(s["moe_added"], it * 4 + 4)
                    select(it + 1)
                    with eng.If(is_crowded != 0):
                        eng.wait_ge(s["moe_gates_turned"], it + 1)
                        for g in range(G):
                            b = 4 + 2 * (g % 2)
                            v = silu_sb[:, g % 2]
                            eng.wait_ge(s["moe_silu"], it * G + (g + 1))
                            eng.tensor_tensor(v, v, rows(gate_row, 2), ALU.mult).then_inc(s["moe_weighted"], 1)
                            eng.wait_ge(s["moe_weighted"], it * G + (g + 1))
                            eng.tensor_tensor(act_sb[:, g % 2], v, ps[:, b:b + 2, T:2 * T], ALU.mult)\
                                .then_inc(s["moe_act"], 1)
                        eng.wait_ge(s["moe_y"], it + 1)
                        eng.sem_inc(s["moe_y_d"], 1)
                        for b in range(4):
                            r = res[:, 2 * b:2 * b + 2, :]
                            eng.tensor_tensor(r, ps[:, b, :].rearrange("p (a b) -> p a b", b=T), r, ALU.add)\
                                .then_inc(s["moe_added"], 1)
                        gathered(it + 1)
                    with eng.Else():
                        eng.sem_inc(s["moe_weighted"], G)
                        for g in range(G):
                            h = ps[:, 6 + g % 2, 0:4 * CAP].rearrange("p (c k n) -> p c k n", c=2, k=2)
                            eng.wait_ge(s["moe_silu"], it * G + (g + 1))
                            eng.tensor_tensor(moe_act_sb[:, g % 2], moe_silu_sb[:, g % 2], h[:, :, 1, :], ALU.mult)\
                                .then_inc(s["moe_act"], 1)
                        eng.wait_ge(s["moe_y"], it + 1)
                        eng.tensor_copy(y_sb[0:CAP, 512:1024], ps[0:CAP, 5, :]).then_inc(s["moe_y_d"], 1)
                        gathered(it + 1)
                        for b in range(4):
                            r = res[:, 2 * b:2 * b + 2, :]
                            eng.wait_ge(s["moe_scattered"], it * 4 + (b + 1))
                            eng.tensor_tensor(r, ps[:, b, :].rearrange("p (a b) -> p a b", b=T), r, ALU.add)\
                                .then_inc(s["moe_added"], 1)
                eng.wait_ge(s["moe_added"], 4 * EXPERTS + 4)
                eng.sem_inc(s["norm_src"], 1)

            def ple_products(l):
                eng.wait_ge(s["ple_copied"], 4 * (l + 1))
                for c in range(KC):
                    eng.wait_ge(s["ple_gate"], KC * l + c + 1)
                    eng.tensor_tensor(ple[:, c, :], ple[:, c, :], sig_sb[:, c % 2, :], ALU.mult)\
                        .then_inc(s["ple_out"], 1)
                eng.wait_ge(s["ple_out"], KC * (l + 1))
                link(eng.scalar_tensor_tensor(out=res, in0=xc[:, :, 0:T], scalar=ALPHA, in1=ple,
                                              op0=ALU.mult, op1=ALU.add))

            def ffn():
                for g in range(GROUPS_DENSE):
                    for c in range(2):
                        eng.wait_ge(s["ffn_silu"], 2 * g + c + 1)
                        eng.tensor_tensor(act_sb[:, g % 2, c, :], silu_sb[:, g % 2, c, :],
                                          ps[:, 4 + 2 * (g % 2) + c, T:2 * T], ALU.mult).then_inc(s["ffn_act"], 1)
                for b in range(4):
                    o = tile(eng, "dense", "y", b)
                    r = res[:, 2 * b:2 * b + 2, :]
                    eng.tensor_tensor(r, o.rearrange("p (a b) -> p a b", b=T), r, ALU.add)\
                        .then_inc(s["res_added"], 1)
                eng.wait_ge(s["res_added"], 4)
                eng.sem_inc(s["norm_src"], 1)

            def prepare_block2():
                link(eng.memset(mv[:, :, :, M_DH:M_DH + 1], 1.0))

            def zero_margins():
                eng.memset(pre[:, :, :, 0:PAD2], 0.0)
                eng.memset(pre[:, :, :, PAD2 + T:SEG2], 0.0).then_inc(s["pad_zeroed"], 1)

            def coefficients(l):
                g = par[:, PC.all(f"norm_g{l}")].unsqueeze(2).broadcast_to([P, KC, 2])
                eng.wait_ge(s["mod_out"], l + 1)
                link(eng.tensor_scalar(coef, mod[:, l, KC:2 * KC, :], 1.0, None, ALU.add))
                eng.tensor_tensor(coef, coef, g, ALU.mult).then_inc(s["coef_out"], 1)
                eng.wait_ge(s["coef_out"], l + 1)

            def modulate(l):
                def f(c, a):
                    v = a[:, c, 0:T]
                    return eng.tensor_scalar(v, v, coef[:, c, 0:1], mod[:, l, c, 0:1], ALU.mult, ALU.add)
                return f

            def gates2(l):
                for t in range(4):
                    o = tile(eng, "vg", l, t)
                    eng.tensor_copy(vtok[:, t, :], o[:, 0:P])
                    gb = PC(f"gate_b{l}", 0, 8), PC(f"gate_b{l}", 8, 8)
                    eng.tensor_tensor(gi[:, t, :], o[:, P:P + 8], par[:, gb[0]], ALU.add)
                    eng.tensor_tensor(gf[:, t, :], o[:, P + 8:P + 16], par[:, gb[1]], ALU.add).then_inc(s["vg_out"], 1)
                eng.wait_ge(s["vg_out"], 4 * (l + 1))
                eng.scalar_tensor_tensor(out=labs, in0=gf, scalar=-1.0, in1=gf, op0=ALU.mult, op1=ALU.max)\
                    .then_inc(s["lf_abs"], 1)

            def conv2(l):
                for c2 in range(0, 2 * M_HEADS, 2):
                    sg = 1 if l == 1 and c2 < M_HEADS else 2
                    eng.wait_ge(s["pre_copied"], 8 * l + c2 + 2)
                    for tap in range(CONV_K2):
                        for c in (c2, c2 + 1):
                            w = par[:, PC(f"conv_w2{l}", c * CONV_K2 + tap)]
                            src = pre[:, c, 0:sg, tap:tap + T]
                            acc = cqk[:, c, 0:sg * T].rearrange("p (a b) -> p a b", b=T)
                            if tap == 0:
                                ins = eng.tensor_scalar(acc, src, w, None, ALU.mult)
                            else:
                                eng.wait_ge(s["dve_order"], order[0] - 1)
                                ins = eng.scalar_tensor_tensor(out=acc, in0=src, scalar=w, in1=acc,
                                                               op0=ALU.mult, op1=ALU.add)
                            if tap == CONV_K2 - 1:
                                ins.then_inc(s["conv2_acc"], 1)
                                if c == c2:
                                    eng.wait_ge(s["dve_order"], order[0])
                            else:
                                ins.then_inc(s["dve_order"], 1)
                                order[0] += 1

            def rope(l):
                for c in range(CC + 1):
                    o = tile(eng, "rope", l, c)
                    v = aq[:, c, 0:T] if c < CC else ak[:, 0:T]
                    link(eng.tensor_tensor(rope_t, o[:, 0:T], con[:, CN.all("sin")], ALU.mult))
                    link(eng.tensor_tensor(v, v, con[:, CN.all("cos")], ALU.mult))
                    eng.tensor_tensor(v, v, rope_t, ALU.add).then_inc(s["rope_out"], 1)
                    eng.wait_ge(s["rope_out"], 5 * l + c + 1)

            def mlstm(l):
                SC = M_DH ** -0.5
                eng.wait_ge(s["lf_ln"], 2 * (l + 1))
                eng.scalar_tensor_tensor(out=lf, in0=gf, scalar=0.0, in1=labs, op0=ALU.min, op1=ALU.subtract)\
                    .then_inc(s["lf_out"], 1)
                eng.memset(m_run, NEG)
                eng.memset(state, 0.0).then_inc(s["state_out"], 1)
                o = tile(eng, "cum", l)
                for d in range(2):
                    b = o[:, 16 * d:16 * d + 16].rearrange("p (a b) -> p a b", b=4)
                    eng.tensor_copy(cs_b[:, :, 4 * d:4 * d + 4], b)
                eng.tensor_copy(cs_t, o[:, 32:64].rearrange("p (a b) -> p a b", b=8)).then_inc(s["cum_out"], 1)
                eng.wait_ge(s["cum_out"], l + 1)
                eng.wait_ge(s["state_out"], 9 * l + 1)
                link(eng.tensor_tensor(cum_a, gi, cs_b, ALU.subtract))

                def diagonals(j):
                    for d in range(2):
                        n = slice(4 * d, 4 * d + 4)
                        ins = eng.tensor_tensor(adiag[:, n, :], rows(ident, 4),
                                                cum_a[:, ORDER[d][j], n].unsqueeze(2).broadcast_to([P, 4, P]),
                                                ALU.mult)
                    ins.then_inc(s["adiag_out"], 1)

                diagonals(0)
                for j in range(4):
                    k = step_no(l, j)
                    ts = [ORDER[d][j] for d in range(2)]
                    yield
                    tile(eng, "arow", l, j, 0)
                    tile(eng, "arow", l, j, 1)
                    arow = ps[:, 2:4, :].rearrange("p a (b c) -> p (a b) c", c=P)
                    eng.tensor_reduce(a_max, arow, AX.X, ALU.max).then_inc(s["dve_order"], 1)
                    order[0] += 1
                    for d in range(2):
                        n = slice(4 * d, 4 * d + 4)
                        ins = eng.tensor_tensor(amask[:, n, :], arow[:, n, :],
                                                rows(con[:, CN.all("mask_b" if d else "mask_f")], 4), ALU.add)
                    ins.then_inc(s["decay_masked"], 1)
                    eng.wait_ge(s["decay_masked"], k)
                    eng.wait_ge(s["dve_order"], order[0])
                    link(eng.tensor_reduce(c_max, amask, AX.X, ALU.max))
                    link(eng.tensor_tensor(m_row, m_run, c_max, ALU.max))
                    link(eng.tensor_tensor(m_end, m_run, a_max, ALU.max))
                    eng.tensor_tensor(ex[:, 0, :], m_run, m_row, ALU.subtract)
                    link(eng.tensor_tensor(ex[:, 1, :], m_run, m_end, ALU.subtract))
                    for d in range(2):
                        n = slice(4 * d, 4 * d + 4)
                        eng.tensor_tensor(ex[:, 2, n], cum_a[:, ts[d], n], m_end[:, n], ALU.subtract)
                        eng.scalar_tensor_tensor(out=ex[:, 3, n], in0=cs_b[:, ts[d], n], scalar=-1.0,
                                                 in1=m_row[:, n], op0=ALU.mult, op1=ALU.subtract)
                        link(eng.tensor_tensor(m_run[:, n], cs_t[:, ts[d], n], m_end[:, n], ALU.add))
                    eng.tensor_scalar(nm_row, m_row, -1.0, None, ALU.mult).then_inc(s["stats_out"], 1)
                    yield
                    if j < 3:
                        diagonals(j + 1)
                    yield
                    eng.wait_ge(s["stats_exp"], k)
                    for d in range(2):
                        g = 2 * (k - 1) + d + 1
                        t = ts[d]
                        used = l == 0 or t < TT
                        yield
                        if used:
                            o = tile(eng, "sc", l, j, d)
                            eng.wait_ge(s["decay_out"], g)
                            eng.scalar_tensor_tensor(out=wqk.rearrange("p a b -> p (a b)"), in0=o, scalar=SC,
                                                     in1=decay[:, 4 * d:4 * d + 4, :].rearrange("p a b -> p (a b)"),
                                                     op0=ALU.mult, op1=ALU.mult).then_inc(s["qk_weighted"], 1)
                        else:
                            eng.wait_ge(s["decay_out"], g)
                            eng.sem_inc(s["qk_weighted"], 1)
                        o = tile(eng, "kt", l, j, d)
                        for h in range(M_HEADS):
                            ins = eng.tensor_scalar(kw[:, h, :], o[:, h * P:h * P + P], wt[:, 2, 4 * d + h:4 * d + h + 1],
                                                    SC, ALU.mult, ALU.mult)
                        ins.then_inc(s["keys_weighted"], 1)
                        yield
                        yield
                        yield
                        yield
                        if used:
                            for half in range(2):
                                tile(eng, "inter", l, j, d, half)
                        for half in range(2):
                            o = tile(eng, "ds", l, j, d, half)
                            for h in range(2):
                                n = 4 * d + 2 * half + h
                                ins = eng.scalar_tensor_tensor(out=state[:, n, :], in0=state[:, n, :],
                                                               scalar=wt[:, 1, n:n + 1],
                                                               in1=o[:, h * 129:h * 129 + 129],
                                                               op0=ALU.mult, op1=ALU.add)
                        ins.then_inc(s["state_out"], 1)
                        if not used:
                            eng.sem_inc(s["mh_out"], 1)
                            yield
                            continue
                        tile(eng, "intra", l, j, d, 0)
                        tile(eng, "intra", l, j, d, 1)
                        eng.wait_ge(s["inter_scaled"], g)
                        link(eng.tensor_tensor(num.rearrange("p (a b) c -> p a (b c)", b=2), ps[:, 2:4, 0:258],
                                               inter_s.rearrange("p (a b) c -> p a (b c)", b=2), ALU.add))
                        last_col = num[:, :, M_DH]
                        link(eng.scalar_tensor_tensor(out=den, in0=last_col, scalar=-1.0, in1=last_col,
                                                      op0=ALU.mult, op1=ALU.max))
                        link(eng.tensor_tensor(den, den, wt[:, 3, 4 * d:4 * d + 4], ALU.max))
                        link(eng.reciprocal(den, den))
                        inv = den.unsqueeze(2).broadcast_to([P, M_HEADS, M_DH])
                        to = hs[:, t, :].rearrange("p (a b) -> p a b", b=M_DH)
                        if j % 2 == 0:
                            eng.tensor_tensor(to, num[:, :, 0:M_DH], inv, ALU.mult).then_inc(s["mh_out"], 1)
                        else:
                            link(eng.tensor_tensor(num[:, :, 0:M_DH], num[:, :, 0:M_DH], inv, ALU.mult))
                            eng.tensor_tensor(to, to, num[:, :, 0:M_DH], ALU.add).then_inc(s["mh_out"], 1)
                        eng.wait_ge(s["mh_out"], g)
                        yield

            def mlstm_post(l):
                tiles = 4 if l == 0 else 2
                n = tiles * M_HEADS
                h2 = hs[:, 0:tiles, :].rearrange("p a b -> p (a b)")
                o2 = mos[:, 0:tiles, :].rearrange("p a b -> p (a b)")
                h3 = hs[:, 0:tiles, :].rearrange("p a (b c) -> p (a b) c", c=M_DH)
                o3 = mos[:, 0:tiles, :].rearrange("p a (b c) -> p (a b) c", c=M_DH)
                eng.wait_ge(s["mos_out"], 8 if l == 0 else 12)
                link(eng.tensor_tensor(h2, h2, o2, ALU.mult))
                link(eng.tensor_tensor(o2, h2, h2, ALU.mult))
                eng.tensor_reduce(rms_s[:, 0:n], o3, AX.X, ALU.add).then_inc(s["mh_sumsq"], 1)
                eng.wait_ge(s["mh_std"], l + 1)
                link(eng.reciprocal(rms_i[:, 0:n], rms_i[:, 0:n]))
                eng.tensor_tensor(h3, h3, rms_i[:, 0:n].unsqueeze(2).broadcast_to([P, n, M_DH]), ALU.mult)\
                    .then_inc(s["mh_normed"], 1)
                eng.wait_ge(s["mzs_out"], 4 * (l + 1))
                for t in range(tiles):
                    o = tile(eng, "mt", l, t)
                    for h in range(M_HEADS):
                        ins = eng.scalar_tensor_tensor(out=mix2[:, CC + h, t * P:t * P + P], in0=o[:, h * P:h * P + P],
                                                       scalar=par[:, PC(f"head_g{l}", h)],
                                                       in1=mzs[:, h, t * P:t * P + P], op0=ALU.mult, op1=ALU.mult)
                    ins.then_inc(s["mh_mixed"], 1)

            def block2_attention(l):
                items = att_items(l)
                last_qt = 3 if l == 0 else 1
                w_out = 2 * T if l == 0 else T
                eng.wait_ge(s["azs_out"], 4 * (l + 1))
                for n in range(len(items) + ATT_LAG):
                    if 2 <= n < len(items) + 2:
                        item = items[n - 2]
                        k = ATT[item]
                        w = 2 * T if item[3] < TT else T
                        eng.wait_ge(s["att_exp"], k)
                        link(eng.tensor_tensor(rsum[:, k % 4, 0:1], rsum[:, k % 4, 0:1], esink[:, k % 4, :], ALU.add))
                        link(eng.reciprocal(rinv[:, k % 4, 0:1], rsum[:, k % 4, 0:1]))
                        pr = prob2[:, k % 4, 0:w]
                        eng.tensor_scalar(pr, pr, rinv[:, k % 4, 0:1], None, ALU.mult).then_inc(s["att_prob"], 1)
                    if n < len(items):
                        _, i, half, qt = items[n]
                        k = ATT[items[n]]
                        h = i + CC * half
                        w = 2 * T if qt < TT else T
                        o = tile(eng, "as", *items[n])
                        if n >= 4:
                            tile(eng, "at", *items[n - 4])
                        pr = prob2[:, k % 4, 0:w]
                        if qt < TT:
                            eng.tensor_tensor(pr, o, con[:, CN("win_mask", qt * 2 * T, 2 * T)], ALU.add)\
                                .then_inc(s["att_scored"], 1)
                        else:
                            eng.tensor_copy(pr, o[:, 0:T]).then_inc(s["att_scored"], 1)
                        eng.wait_ge(s["att_scored"], k)
                        link(eng.tensor_reduce(rmax[:, k % 4, 0:1], pr, AX.X, ALU.max, negate=True))
                        eng.tensor_tensor(rmax[:, k % 4, 0:1], rmax[:, k % 4, 0:1], nsink[:, l, h:h + 1], ALU.min)\
                            .then_inc(s["att_max"], 1)
                    if n >= 5 and items[n - 5][2] == 1 and items[n - 5][3] == last_qt:
                        i = items[n - 5][1]
                        o = tile(eng, "ao", l, i)
                        eng.tensor_tensor(mix2[:, i, 0:w_out], o[:, 0:w_out], azs[:, i, 0:w_out], ALU.mult)\
                            .then_inc(s["att_out"], 1)
                    yield

            def block2_out(l):
                for c in range(KC):
                    o = tile(eng, "xo", l, c)
                    for e in range(2 if l == 0 else 1):
                        v = xc[:, c, e * T:(e + 1) * T]
                        ins = eng.scalar_tensor_tensor(out=v, in0=o[:, e * T:(e + 1) * T],
                                                       scalar=mod[:, l, 2 * KC + c, e:e + 1], in1=v,
                                                       op0=ALU.mult, op1=ALU.add)
                    ins.then_inc(s["x_added"], 1)
                eng.wait_ge(s["x_added"], KC * (l + 1))

            eng.wait_ge(s["inputs_loaded"], 16 * N_INPUTS)
            for l in range(DEPTH):
                eng.tensor_scalar(bq_s[:, l, :], par[:, PC.all(f"b_q{l}")], DH ** -0.5, None, ALU.mult)
                eng.tensor_scalar(nsink[:, l, :], par[:, PC.all(f"sink{l}")], -1.0, None, ALU.mult)
            eng.memset(glu[:, :, 0:PAD1], 0.0)
            eng.memset(glu[:, :, PAD1 + T:], 0.0).then_inc(s["prep_done"], 1)
            eng.wait_ge(s["prep_done"], 1)
            norm("in", xc, KC, T, layer_gain("ln_in_g", "ln_in_b", xc))
            for l in range(DEPTH):
                block1_projection(l)
                conv(l)
                values(l)
                norm(f"conv{l}", conv_acc, CC, T, None)
                block1_attention(l)
                conditions(l)
                block1_out(l)
                norm(f"ln1_{l}", res, KC, T, layer_gain(f"ln1_g{l}", f"ln1_b{l}", xc))
                if l == 1:
                    routing()
                    places()
                ple_products(l)
                if l == 1:
                    moe()
                else:
                    ffn()
                norm(f"ln2_{l}", res, KC, T, layer_gain(f"ln2_g{l}", f"ln2_b{l}", xc))
            eng.wait_ge(s["norm_out"], outk("ln2_1"))
            prepare_block2()
            for l in range(DEPTH):
                coefficients(l)
                zero_margins()
                norm(f"rms{l}", xc, KC, 2 * T, modulate(l), centred=False)
                gates2(l)
                conv2(l)
                rope(l)
                interleave(l, mlstm(l), block2_attention(l))
                mlstm_post(l)
                block2_out(l)
            norm("final", xc, KC, T,
                 lambda c, a: eng.tensor_scalar(cen[:, c, :], cen[:, c, :], par[:, PC("final_g", c)], None, ALU.mult),
                 centred=False, dst=cen)


def weight_units(a):
    units = np.zeros((UNITS, P, UC), np.float32)
    n = [0]

    def put(block, slices):
        k, cols = block.shape
        units[n[0]].reshape(P, k // P, UC * P // k)[:, :, 0:cols] = block.reshape(k // P, P, cols).transpose(1, 0, 2)
        n[0] += 1

    def columns(w, ranges):
        put(np.concatenate([w[:, r[0]:r[1]] for r in ranges], axis=1), None)

    def whole(w):
        for c in range(0, w.shape[1], GW):
            columns(w, [(c, c + GW)])

    def ffn(w1, w3, w2):
        groups = w1.shape[1] // GW
        for g in range(groups + 1):
            if g < groups:
                columns(w1, [(g * GW, (g + 1) * GW)])
                columns(w3, [(g * GW, (g + 1) * GW)])
            if g:
                put(w2[(g - 1) * GW:g * GW], None)

    for l in range(DEPTH):
        w = a["w_in"][l]
        for j in range(CC):
            columns(w, [(j * P, j * P + P), (CONV_CH + j * P, CONV_CH + j * P + P)])
        q0 = 2 * CONV_CH
        for j in range(CC):
            columns(w, [(q0 + j * P, q0 + j * P + P), (q0 + 512 + j * P, q0 + 512 + j * P + P)])
        for j in range(2):
            columns(w, [(q0 + 1024 + j * GW, q0 + 1024 + (j + 1) * GW)])
        whole(a["w_ada_2"][l])
        whole(a["w_out"][l])
        put(a["ple_w"][l], None)
        whole(a["ple_gate_w"][l])
        if l == 0:
            ffn(a["ffn_w1"][0], a["ffn_w3"][0], a["ffn_w2"][0])
        else:
            for e in range(EXPERTS):
                ffn(a["moe_w1"][0, e], a["moe_w3"][0, e], a["moe_w2"][0, e])
    A = 512
    at = dict(aq=0, ak=A, av=A + 128, az=A + 256, mq=2 * A + 256, mk=3 * A + 256, mv=4 * A + 256, mo=5 * A + 256,
              mz=6 * A + 256, mi=7 * A + 256, mf=7 * A + 264)

    def pairs(base, i):
        return [(base + i * DH, base + i * DH + DH), (base + (i + 4) * DH, base + (i + 4) * DH + DH)]

    for l in range(DEPTH):
        w = a["w_in_2"][l]
        seen = {}
        for name in UNITS_IN2:
            u = seen.get(name, 0)
            seen[name] = u + 1
            if name == "vg":
                columns(w, [(at["av"], at["av"] + P), (at["mi"], at["mi"] + 16)])
            elif name == "ak":
                columns(w, [(at["ak"], at["ak"] + P)])
            elif name in ("aq", "az"):
                columns(w, pairs(at[name], 2 * u) + pairs(at[name], 2 * u + 1))
            else:
                columns(w, [(at[name] + u * GW, at[name] + (u + 1) * GW)])
        wo = a["w_out_2"][l]
        rows = [wo[r[0]:r[1]] for i in range(CC) for r in pairs(0, i)] + [wo[A:]]
        whole(np.concatenate(rows, axis=0))
    assert n[0] == UNITS
    return units


def param_tile(a):
    t = np.zeros((P, PC.n), np.float32)

    def col(name, v):
        t[:, PC.all(name)] = v.reshape(-1, P).T

    def row(name, v):
        t[:, PC.all(name)] = v.reshape(1, -1)

    col("ln_in_g", a["ln_in_g"]), col("ln_in_b", a["ln_in_b"])
    for l in range(DEPTH):
        b = a["b_in"][l]
        for i, name in enumerate(("b_a", "b_g", "b_q", "b_k")):
            col(f"{name}{l}", b[i * 512:(i + 1) * 512])
        row(f"b_v{l}", b[2048:])
        t[:, PC.all(f"conv_w{l}")] = a["conv_w"][l].reshape(CONV_K, CC, P).transpose(2, 1, 0).reshape(P, -1)
        t[:, PC.all(f"conv_w2{l}")] = a["conv_w_2"][l].reshape(CONV_K2, 8, P).transpose(2, 1, 0).reshape(P, -1)
        for name in ("conv_b", "conv_ln_g", "conv_ln_b", "b_out", "ln1_g", "ln1_b", "ple_gate_b", "ln2_g", "ln2_b"):
            col(f"{name}{l}", a[name][l])
        col(f"b_ada{l}", a["b_ada_2"][l]), col(f"norm_g{l}", a["norm_g_2"][l])
        col(f"conv_b2{l}", a["conv_b_2"][l]), col(f"head_g{l}", a["head_g_2"][l])
        row(f"gate_b{l}", a["gate_b_2"][l]), row(f"sink{l}", a["sink_2"][l])
    t[:, PC.all("w_router")] = a["w_router"][0].reshape(KC, P, EXPERTS).transpose(1, 0, 2).reshape(P, -1)
    col("final_g", a["final_g_2"])
    t[:, PC.all("cond")] = np.stack([a["c_2"].reshape(-1), a["c_ctx_2"].reshape(-1)]).reshape(2, KC, P)\
        .transpose(2, 1, 0).reshape(P, -1)
    return t


def const_tile():
    t = np.zeros((P, CN.n), np.float32)
    i = np.arange(P)
    t[:, CN.all("ident")] = np.eye(P)
    t[:, CN.all("ones")] = 1
    t[:, CN.all("tri_f")] = i[:, None] <= i[None, :]
    t[:, CN.all("tri_b")] = i[:, None] >= i[None, :]
    t[:, CN.all("mask_f")] = np.where(i[None, :] <= i[:, None], 0, NEG)
    t[:, CN.all("mask_b")] = np.where(i[None, :] >= i[:, None], 0, NEG)
    rot = np.zeros((P, P), np.float32)
    for m in i:
        if m % 32 < 16:
            rot[m + 16, m] = -1
        else:
            rot[m - 16, m] = 1
    t[:, CN.all("rot")] = rot
    inv = np.float32(10000.0) ** (-np.arange(0, DH // 2, 2, dtype=np.float32) / np.float32(DH // 2))
    tok = np.arange(T)
    row, col = (tok // GRID_W).astype(np.float32), (tok % GRID_W).astype(np.float32)
    for m in i:
        ang = (row if m % DH < 32 else col) * inv[m % 16]
        t[m, CN.all("cos")], t[m, CN.all("sin")] = np.cos(ang), np.sin(ang)
    win = np.zeros((P, TT, 2 * T), np.float32)
    nbr = np.zeros((P, TT, T), np.float32)
    kc = np.arange(T) % GRID_W
    for qt in range(TT):
        q = qt * P + i
        win[:, qt, 0:T] = np.where(np.abs(q[:, None] - tok[None, :]) <= WINDOW, 0, NEG)
        w0 = np.clip(q % GRID_W - WIN_C // 2, 0, GRID_W - WIN_C)
        nbr[:, qt] = np.where((kc[None, :] >= w0[:, None]) & (kc[None, :] < w0[:, None] + WIN_C), 0, NEG)
    t[:, CN.all("win_mask")] = win.reshape(P, -1)
    t[:, CN.all("nbr_mask")] = nbr.reshape(P, -1)
    t[:, CN.all("slot")] = np.arange(CAP)[None, :]
    e = np.arange(EXPERTS)
    t[:, CN.all("before")] = (e[None, :] < e[:, None]).reshape(1, -1)
    t[:, CN.all("eps5")], t[:, CN.all("eps6")], t[:, CN.all("one")] = 1e-5, 1e-6, 1
    return t


def relative_rows(rpb):
    out = np.zeros((DEPTH, GRID_W, HEADS, 2 * ROWS - 1, GRID_W), np.float32)
    for c in range(GRID_W):
        lo, hi = max(0, c - 15), min(GRID_W, c + 16)
        out[:, c, :, :, lo:hi] = rpb[:, :, 4:4 + 2 * ROWS - 1, lo - c + 15:hi - c + 15]
    return out


def kernel(**inputs):
    import concourse.bacc as _bacc
    from concourse.bass_utils import run_bass_kernel_spmd as _run

    a = {k: np.asarray(v) for k, v in inputs.items()}

    def feature_major(v):
        return np.ascontiguousarray(v.T.reshape(-1, P, v.shape[0]).transpose(1, 0, 2))

    arrays = {
        "weights": weight_units(a),
        "params": param_tile(a),
        "consts": const_tile(),
        "x_t": feature_major(a["x"][0]),
        "ctx_t": feature_major(a["ctx_2"][0]),
        "p_t": np.ascontiguousarray(np.stack([feature_major(a["p"][l, 0]) for l in range(DEPTH)], axis=1)),
        "rel": relative_rows(a["rpb"]),
    }
    nc = _bacc.Bacc("TRN2", target_bir_lowering=False, num_devices=1)
    args = [nc.dram_tensor(n, v.shape, F32, kind="ExternalInput").ap() for n, v in arrays.items()]
    out = nc.dram_tensor("out", (P, KC, T), F32, kind="ExternalOutput").ap()
    build(nc, *args, out)
    r = _run(nc, [arrays], core_ids=[0])
    y = r.results[0]["out"]
    return np.ascontiguousarray(y.transpose(2, 1, 0).reshape(1, T, D))
```
